# Optimizing a Trainium2 kernel written in Bass

```python
import math
import jax, jax.numpy as jnp
from jax import lax
import numpy as np

D_MODEL = 1024
BATCH = 1
SEQ = 512
DEPTH = 1

HEAD_DIM = 64
D_MIX = D_MODEL
D_ATTN = D_MIX // 2
D_SGU = D_MIX - D_ATTN
N_ATTN_HEADS = D_ATTN // HEAD_DIM
N_SGU_GROUPS = D_SGU // HEAD_DIM
SGU_GROUP_DIM = D_SGU // N_SGU_GROUPS
D_IN_PROJ = 3 * D_ATTN + 2 * D_SGU
DILATED_BRANCHES = ((128, 1), (512, 4), (2048, 16))
SGU_CHUNK = 128
D_FF = 4 * D_MODEL
N_REL_BUCKETS = 32
REL_MAX_DISTANCE = 1024
RMS_EPS = 1e-6
LN_EPS = 1e-5
NEG_INF = -1e30


def rms_norm(x, g):
    xf = x.astype(jnp.float32)
    y = xf * lax.rsqrt(jnp.mean(xf * xf, axis=-1, keepdims=True) + RMS_EPS)
    return (y * g.astype(jnp.float32)).astype(x.dtype)

def layer_norm(x, g, b):
    xf = x.astype(jnp.float32)
    mu = jnp.mean(xf, axis=-1, keepdims=True)
    xc = xf - mu
    y = xc * lax.rsqrt(jnp.mean(xc * xc, axis=-1, keepdims=True) + LN_EPS)
    return (y * g.astype(jnp.float32) + b.astype(jnp.float32)).astype(x.dtype)

def t5_bucket(rel):
    half = N_REL_BUCKETS // 2
    max_exact = half // 2
    ret = jnp.where(rel > 0, half, 0)
    n = jnp.abs(rel)
    nf = jnp.maximum(n, 1).astype(jnp.float32)
    large = max_exact + (jnp.log(nf / max_exact) / math.log(REL_MAX_DISTANCE / max_exact)
                         * (half - max_exact)).astype(jnp.int32)
    large = jnp.minimum(large, half - 1)
    return ret + jnp.where(n < max_exact, n, large)

def dilated_window_branch(q, k, v, rel_bias, window, dil):
    B, S, H, Dh = q.shape
    half = window // (2 * dil)
    blk = half
    L = S // dil
    nb = -(-L // blk)
    Lp = nb * blk

    def to_blocks(t):
        t = t.reshape(B, L, dil, H, Dh).transpose(0, 2, 1, 3, 4)
        t = jnp.pad(t, ((0, 0), (0, 0), (0, Lp - L), (0, 0), (0, 0)))
        return t.reshape(B, dil, nb, blk, H, Dh)

    def neighbourhood(t):
        tp = jnp.pad(t, ((0, 0), (0, 0), (1, 1), (0, 0), (0, 0), (0, 0)))
        return jnp.concatenate([tp[:, :, :-2], tp[:, :, 1:-1], tp[:, :, 2:]], axis=3)

    qb = to_blocks(q)
    kw = neighbourhood(to_blocks(k))
    vw = neighbourhood(to_blocks(v))

    q_local = jnp.arange(blk)
    k_local = jnp.arange(3 * blk) - blk
    rel = k_local[None, :] - q_local[:, None]
    bias = rel_bias[t5_bucket(rel * dil)].astype(jnp.float32)
    k_idx = jnp.arange(nb)[:, None] * blk + k_local[None, :]
    valid = (jnp.abs(rel) <= half)[None] & ((k_idx >= 0) & (k_idx < L))[:, None, :]

    s = jnp.einsum('brnqhd,brnkhd->brnhqk', qb, kw).astype(jnp.float32)
    s = s + bias.transpose(2, 0, 1)
    s = jnp.where(valid[:, None], s, NEG_INF)
    m = jnp.max(s, axis=-1, keepdims=True)
    p = jnp.exp(s - m)
    den = jnp.sum(p, axis=-1, keepdims=True)
    o = jnp.einsum('brnhqk,brnkhd->brnqhd', (p / den).astype(v.dtype), vw)
    lse = (m + jnp.log(den))[..., 0].transpose(0, 1, 2, 4, 3)

    o = o.reshape(B, dil, Lp, H, Dh)[:, :, :L].transpose(0, 2, 1, 3, 4).reshape(B, S, H, Dh)
    lse = lse.reshape(B, dil, Lp, H)[:, :, :L].transpose(0, 2, 1, 3).reshape(B, S, H)
    return o, lse

def dilated_attention(q, k, v, rel_bias):
    outs, lses = [], []
    for window, dil in DILATED_BRANCHES:
        o, l = dilated_window_branch(q, k, v, rel_bias, window, dil)
        outs.append(o)
        lses.append(l)
    w = jax.nn.softmax(jnp.stack(lses, axis=0), axis=0)
    return jnp.einsum('ibsh,ibshd->bshd', w.astype(q.dtype), jnp.stack(outs, axis=0))

def spatial_gating(u, v, ln_g, ln_b, w_s, b_s):
    B, S, _ = u.shape
    nc = S // SGU_CHUNK
    v = layer_norm(v, ln_g, ln_b).reshape(B, nc, SGU_CHUNK, N_SGU_GROUPS, SGU_GROUP_DIM)
    mixed = jnp.einsum('gts,bnsgc->bntgc', w_s, v) + b_s.T[None, None, :, :, None]
    return u * mixed.reshape(B, S, D_SGU)

def hybrid_layer(x, g_pre_mix, w_in, sgu_ln_g, sgu_ln_b, sgu_w, sgu_b, w_out, g_post_mix,
                 g_pre_ffn, w_ff1, w_ff2, g_post_ffn, rel_bias):
    B, S, _ = x.shape
    h = rms_norm(x, g_pre_mix)
    z = h @ w_in
    q, k, v, zu, zv = jnp.split(
        z, [D_ATTN, 2 * D_ATTN, 3 * D_ATTN, 3 * D_ATTN + D_SGU], axis=-1)
    q = q.reshape(B, S, N_ATTN_HEADS, HEAD_DIM) * (HEAD_DIM ** -0.5)
    k = k.reshape(B, S, N_ATTN_HEADS, HEAD_DIM)
    v = v.reshape(B, S, N_ATTN_HEADS, HEAD_DIM)
    attn = dilated_attention(q, k, v, rel_bias).reshape(B, S, D_ATTN)
    sgu = spatial_gating(jax.nn.gelu(zu), jax.nn.gelu(zv), sgu_ln_g, sgu_ln_b, sgu_w, sgu_b)
    mix = jnp.concatenate([attn, sgu], axis=-1) @ w_out
    x = x + rms_norm(mix, g_post_mix)
    h = rms_norm(x, g_pre_ffn)
    f = jnp.square(jax.nn.relu(h @ w_ff1)) @ w_ff2
    return x + rms_norm(f, g_post_ffn)

def first_inputs(seed: int = 0) -> dict:
    key = jax.random.key(seed)
    ks = jax.random.split(key, 16)
    f32 = jnp.float32

    def nrm(k, shape, scale):
        return jax.random.normal(k, shape, f32) * scale

    def gain(k, shape):
        return 1.0 + 0.05 * jax.random.normal(k, shape, f32)

    return {
        "x": jax.random.normal(ks[0], (BATCH, SEQ, D_MODEL), f32),
        "g_pre_mix": gain(ks[1], (DEPTH, D_MODEL)),
        "w_in": nrm(ks[2], (DEPTH, D_MODEL, D_IN_PROJ), D_MODEL ** -0.5),
        "sgu_ln_g": gain(ks[3], (DEPTH, D_SGU)),
        "sgu_ln_b": nrm(ks[4], (DEPTH, D_SGU), 0.02),
        "sgu_w": nrm(ks[5], (DEPTH, N_SGU_GROUPS, SGU_CHUNK, SGU_CHUNK), SGU_CHUNK ** -0.5),
        "sgu_b": gain(ks[6], (DEPTH, N_SGU_GROUPS, SGU_CHUNK)),
        "w_out": nrm(ks[7], (DEPTH, D_MIX, D_MODEL), D_MIX ** -0.5),
        "g_post_mix": gain(ks[8], (DEPTH, D_MODEL)),
        "g_pre_ffn": gain(ks[9], (DEPTH, D_MODEL)),
        "w_ff1": nrm(ks[10], (DEPTH, D_MODEL, D_FF), D_MODEL ** -0.5),
        "w_ff2": nrm(ks[11], (DEPTH, D_FF, D_MODEL), D_FF ** -0.5),
        "g_post_ffn": gain(ks[12], (DEPTH, D_MODEL)),
        "rel_bias": nrm(ks[13], (N_REL_BUCKETS, N_ATTN_HEADS), 0.5),
    }

def first_block(x, g_pre_mix, w_in, sgu_ln_g, sgu_ln_b, sgu_w, sgu_b, w_out, g_post_mix,
              g_pre_ffn, w_ff1, w_ff2, g_post_ffn, rel_bias):
    for layer in range(DEPTH):
        x = hybrid_layer(x, g_pre_mix[layer], w_in[layer], sgu_ln_g[layer], sgu_ln_b[layer],
                         sgu_w[layer], sgu_b[layer], w_out[layer], g_post_mix[layer],
                         g_pre_ffn[layer], w_ff1[layer], w_ff2[layer], g_post_ffn[layer],
                         rel_bias)
    return x


DEPTH_2 = 2

CHUNK = 64
EPS = 1e-6
D_CONV = D_MODEL // 2
N_CONV_GROUPS = 4
CONV_WIDTH = 31
D_POOL = D_MODEL // 2
POOL_WINDOWS = (2, 4, 8, 16)
N_POOL_GROUPS = len(POOL_WINDOWS)
POOL_GROUP = D_POOL // N_POOL_GROUPS
HG_HEADS = 8
HG_DK = D_MODEL // HG_HEADS
HG_DV = HG_DK
D_HG = HG_HEADS * HG_DK
D_FF_2 = -(-8 * D_MODEL // (3 * 256)) * 256
N_EVEN = (DEPTH_2 + 1) // 2
N_ODD = DEPTH_2 // 2


def rmsnorm(x, g):
    xf = x.astype(jnp.float32)
    y = xf * lax.rsqrt(jnp.mean(xf * xf, axis=-1, keepdims=True) + EPS)
    return (y * g.astype(jnp.float32)).astype(x.dtype)

def layernorm(x, g, b):
    xf = x.astype(jnp.float32)
    mu = jnp.mean(xf, axis=-1, keepdims=True)
    var = jnp.mean(jnp.square(xf - mu), axis=-1, keepdims=True)
    y = (xf - mu) * lax.rsqrt(var + EPS)
    return (y * g.astype(jnp.float32) + b.astype(jnp.float32)).astype(x.dtype)

def swiglu_ffn(h, w1, w3, w2):
    return (jax.nn.silu(h @ w1) * (h @ w3)) @ w2

def conv_pool_mixer(h, w_in, dw_w, dw_b, ln_g, ln_b, pool_w, pool_scale, w_out):
    B, T, _ = h.shape
    z = h @ w_in
    a_val = z[..., :D_CONV]
    a_gate = z[..., D_CONV:2 * D_CONV]
    u = z[..., 2 * D_CONV:]

    a = a_val * jax.nn.sigmoid(a_gate)
    a = lax.conv_general_dilated(
        a, dw_w[:, None, :].astype(a.dtype), window_strides=(1,),
        padding=[(CONV_WIDTH - 1, 0)],
        dimension_numbers=('NWC', 'WIO', 'NWC'),
        feature_group_count=D_CONV) + dw_b
    a = jax.nn.silu(layernorm(a, ln_g, ln_b))

    ug = u.reshape(B, T, N_POOL_GROUPS, POOL_GROUP)
    cs = jnp.cumsum(ug.astype(jnp.float32), axis=1)
    cs = jnp.pad(cs, ((0, 0), (1, 0), (0, 0), (0, 0)))
    t = jnp.arange(T)
    means = []
    for g, w in enumerate(POOL_WINDOWS):
        lo = jnp.maximum(t + 1 - w, 0)
        s = cs[:, 1:, g] - cs[:, lo, g]
        cnt = jnp.minimum(t + 1, w).astype(jnp.float32)[:, None]
        means.append(s / cnt)
    pooled = jnp.stack(means, axis=2)
    d = (pooled - ug.astype(jnp.float32)).astype(u.dtype)
    p = jnp.einsum('btgc,gcd->btgd', d, pool_w).reshape(B, T, D_POOL) * pool_scale

    return jnp.concatenate([a, p], axis=-1) @ w_out

def hgrn2_mixer(h, w_in, lb, gn_g, w_out):
    B, T, _ = h.shape
    NC = T // CHUNK
    z = h @ w_in
    q, f_raw, i, g = jnp.split(z, 4, axis=-1)
    f = lb + (1.0 - lb) * jax.nn.sigmoid(f_raw.astype(jnp.float32))
    log_f = jnp.log(f)
    k = 1.0 - f

    def to_chunks(a, dh):
        a = a.astype(jnp.float32).reshape(B, NC, CHUNK, HG_HEADS, dh)
        return a.transpose(1, 0, 3, 2, 4)

    qc = to_chunks(q, HG_DK)
    kc = to_chunks(k, HG_DK)
    vc = to_chunks(i, HG_DV)
    bc = jnp.cumsum(to_chunks(log_f, HG_DK), axis=3)
    tril = jnp.tril(jnp.ones((CHUNK, CHUNK), dtype=bool))

    def step(S, inp):
        qt, kt, vt, bt = inp
        diff = bt[:, :, :, None, :] - bt[:, :, None, :, :]
        decay = jnp.exp(jnp.where(tril[:, :, None], diff, -jnp.inf))
        scores = jnp.einsum('bhtk,bhsk,bhtsk->bhts', qt, kt, decay)
        o = (jnp.einsum('bhts,bhsv->bhtv', scores, vt)
             + jnp.einsum('bhtk,bhkv->bhtv', qt * jnp.exp(bt), S))
        b_last = bt[:, :, -1:, :]
        S = (jnp.exp(b_last[:, :, 0, :])[..., None] * S
             + jnp.einsum('bhsk,bhsv->bhkv', kt * jnp.exp(b_last - bt), vt))
        return S, o

    S0 = jnp.zeros((B, HG_HEADS, HG_DK, HG_DV), jnp.float32)
    _, o = lax.scan(step, S0, (qc, kc, vc, bc))
    o = o.transpose(1, 0, 3, 2, 4).reshape(B, T, HG_HEADS, HG_DV)
    o = o * lax.rsqrt(jnp.mean(o * o, axis=-1, keepdims=True) + EPS)
    o = o * gn_g.astype(jnp.float32).reshape(HG_HEADS, HG_DV)
    o = o.reshape(B, T, D_HG).astype(h.dtype) * jax.nn.silu(g)
    return o @ w_out

def second_inputs(seed: int = 0) -> dict:
    key = jax.random.key(seed)
    ks = jax.random.split(key, 20)
    nrm = lambda k, shape, s: jax.random.normal(k, shape, jnp.float32) * s
    gain = lambda k, shape: 1.0 + 0.05 * jax.random.normal(k, shape, jnp.float32)
    d_in0 = 2 * D_CONV + D_POOL
    return {
        "x": jax.random.normal(ks[0], (BATCH, SEQ, D_MODEL), jnp.float32),
        "norm_mix_g": gain(ks[1], (DEPTH_2, D_MODEL)),
        "norm_ffn_g": gain(ks[2], (DEPTH_2, D_MODEL)),
        "final_g": gain(ks[3], (D_MODEL,)),
        "cp_w_in": nrm(ks[4], (N_EVEN, D_MODEL, d_in0), D_MODEL ** -0.5),
        "cp_dw_w": nrm(ks[5], (N_EVEN, CONV_WIDTH, D_CONV), CONV_WIDTH ** -0.5),
        "cp_dw_b": nrm(ks[6], (N_EVEN, D_CONV), 0.01),
        "cp_ln_g": gain(ks[7], (N_EVEN, D_CONV)),
        "cp_ln_b": nrm(ks[8], (N_EVEN, D_CONV), 0.01),
        "cp_pool_w": nrm(ks[9], (N_EVEN, N_POOL_GROUPS, POOL_GROUP, POOL_GROUP), POOL_GROUP ** -0.5),
        "cp_pool_scale": gain(ks[10], (N_EVEN, D_POOL)),
        "cp_w_out": nrm(ks[11], (N_EVEN, D_CONV + D_POOL, D_MODEL), (D_CONV + D_POOL) ** -0.5),
        "hg_w_in": nrm(ks[12], (N_ODD, D_MODEL, 4 * D_HG), D_MODEL ** -0.5),
        "hg_lb_logits": nrm(ks[13], (DEPTH_2, D_HG), 0.1),
        "hg_gn_g": gain(ks[14], (N_ODD, D_HG)),
        "hg_w_out": nrm(ks[15], (N_ODD, D_HG, D_MODEL), D_HG ** -0.5),
        "ffn_w1": nrm(ks[16], (DEPTH_2, D_MODEL, D_FF_2), D_MODEL ** -0.5),
        "ffn_w3": nrm(ks[17], (DEPTH_2, D_MODEL, D_FF_2), D_MODEL ** -0.5),
        "ffn_w2": nrm(ks[18], (DEPTH_2, D_FF_2, D_MODEL), D_FF_2 ** -0.5),
    }

def second_block(x, norm_mix_g, norm_ffn_g, final_g, cp_w_in, cp_dw_w, cp_dw_b,
              cp_ln_g, cp_ln_b, cp_pool_w, cp_pool_scale, cp_w_out, hg_w_in,
              hg_lb_logits, hg_gn_g, hg_w_out, ffn_w1, ffn_w3, ffn_w2):
    p = jax.nn.softmax(hg_lb_logits.astype(jnp.float32), axis=0)
    lower_bounds = jnp.cumsum(p, axis=0) - p[0:1]
    h = x
    for layer in range(DEPTH_2):
        hn = rmsnorm(h, norm_mix_g[layer])
        j = layer // 2
        if layer % 2 == 0:
            mix = conv_pool_mixer(hn, cp_w_in[j], cp_dw_w[j], cp_dw_b[j], cp_ln_g[j],
                                  cp_ln_b[j], cp_pool_w[j], cp_pool_scale[j], cp_w_out[j])
        else:
            mix = hgrn2_mixer(hn, hg_w_in[j], lower_bounds[layer], hg_gn_g[j], hg_w_out[j])
        h = h + mix
        h = h + swiglu_ffn(rmsnorm(h, norm_ffn_g[layer]), ffn_w1[layer], ffn_w3[layer], ffn_w2[layer])
    return rmsnorm(h, final_g)


def setup_inputs(seed=0):
    out = dict(first_inputs(seed))
    for name, value in second_inputs(seed + 1).items():
        if name != "x":
            out[name + "_2"] = value
    return out


def reference(
    x, g_pre_mix, w_in, sgu_ln_g, sgu_ln_b, sgu_w, sgu_b, w_out, g_post_mix, g_pre_ffn, w_ff1,
    w_ff2, g_post_ffn, rel_bias, norm_mix_g_2, norm_ffn_g_2, final_g_2, cp_w_in_2, cp_dw_w_2,
    cp_dw_b_2, cp_ln_g_2, cp_ln_b_2, cp_pool_w_2, cp_pool_scale_2, cp_w_out_2, hg_w_in_2,
    hg_lb_logits_2, hg_gn_g_2, hg_w_out_2, ffn_w1_2, ffn_w3_2, ffn_w2_2,
):
    x = first_block(
        x, g_pre_mix, w_in, sgu_ln_g, sgu_ln_b, sgu_w, sgu_b, w_out, g_post_mix, g_pre_ffn,
        w_ff1, w_ff2, g_post_ffn, rel_bias,
    )
    return second_block(
        x, norm_mix_g_2, norm_ffn_g_2, final_g_2, cp_w_in_2, cp_dw_w_2, cp_dw_b_2, cp_ln_g_2,
        cp_ln_b_2, cp_pool_w_2, cp_pool_scale_2, cp_w_out_2, hg_w_in_2, hg_lb_logits_2,
        hg_gn_g_2, hg_w_out_2, ffn_w1_2, ffn_w3_2, ffn_w2_2,
    )


_drawn_inputs = setup_inputs


def setup_inputs(seed=0):
    import zlib

    import numpy as np

    out = dict(_drawn_inputs(seed))
    spreads = {}
    factors = {'sgu_ln_b': 4.551,
     'cp_dw_b_2': 8.0,
     'cp_ln_g_2': 3.489,
     'cp_ln_b_2': 8.0,
     'cp_pool_scale_2': 2.801,
     'hg_gn_g_2': 3.664}
    for name, (base, spread) in spreads.items():
        noise = np.random.default_rng([zlib.crc32(name.encode()), seed]).standard_normal(out[name].shape)
        drawn = base * np.exp(spread * noise) if base else spread * noise
        out[name] = __import__('jax').numpy.asarray(drawn.astype(out[name].dtype))
    for name, factor in factors.items():
        out[name] = (out[name] * factor).astype(out[name].dtype)
    return out
```

```python
import math
from contextlib import ExitStack

import numpy as np
import concourse.bass as bass
from concourse import mybir

ALU = mybir.AluOpType
ACT = mybir.ActivationFunctionType
F32 = mybir.dt.float32
F32R = mybir.dt.float32r
I32 = mybir.dt.int32

P = 128
SEQ = 512
D = 1024
KT = D // P
TT = SEQ // P
HEAD_DIM = 64
D_ATTN = D // 2
PAIRS = D_ATTN // P
N_HEADS = D_ATTN // HEAD_DIM
SGU_TILES = (D - D_ATTN) // P
D_FF = 4 * D
D_FF_2 = -(-8 * D // (3 * 256)) * 256
TAPS = 31
PAD = TAPS - 1
POOL_WINDOWS = (2, 4, 8, 16)
POOL_PAD = 16
HG_HEADS = D // P
WIN = 128
LEVELS = [64, 32, 16, 8, 4, 2, 1]
N_BUCKETS = 32
REL_MAX = 1024
BRANCHES = ((128, 1), (512, 4), (2048, 16))
SKEW = SEQ + SEQ - P
LOG_TABLES = "natural_log_exp_and_others"

RING = 4
COLS = 512
AHEAD = 2

FFN_GROUPS = D_FF // COLS
GLU_GROUPS = D_FF_2 // 256

U_ZV = 0
U_QKV = U_ZV + 4
U_WOUT = U_QKV + 4 * PAIRS
U_FFN = U_WOUT + 8
U_CPIN = U_FFN + 8 * FFN_GROUPS
U_CPOUT = U_CPIN + 12
U_GLU = [U_CPOUT + 8, 0]
U_HGIN = U_GLU[0] + 6 * GLU_GROUPS
U_HGOUT = U_HGIN + 4 * HG_HEADS
U_GLU[1] = U_HGOUT + 8
UNITS = U_GLU[1] + 6 * GLU_GROUPS

VECTORS = (("g_pre_mix", 8), ("g_post_mix", 8), ("g_pre_ffn", 8), ("g_post_ffn", 8),
           ("norm_mix_g_2", 16), ("norm_ffn_g_2", 16), ("final_g_2", 8), ("sgu_ln_g", 4),
           ("sgu_ln_b", 4), ("cp_dw_b_2", 4), ("cp_ln_g_2", 4), ("cp_ln_b_2", 4),
           ("cp_pool_scale_2", 4), ("hg_gn_g_2", 8), ("hg_lb_logits_2", 16))
COL = {}
for _name, _n in VECTORS:
    COL[_name] = sum(n for _, n in VECTORS[:len(COL)])
N_VEC = sum(n for _, n in VECTORS)


class Banks:

    def __init__(self):
        self.count = [0] * 8
        self.first = {}
        self.per = {}

    def stage(self, name, uses, repeats=1):
        n = [0] * 8
        for tag, b in uses:
            n[b] += 1
            self.first[name, tag] = (b, self.count[b] + n[b])
        for tag, b in uses:
            self.per[name, tag] = n[b]
        for b in range(8):
            self.count[b] += n[b] * repeats

    def bank(self, name, tag):
        return self.first[name, tag][0]

    def nth(self, name, tag, turn=0):
        k = self.first[name, tag][1]
        return k if isinstance(turn, int) and turn == 0 else turn * self.per[name, tag] + k

    def before(self, name, tag, turn=0):
        return self.nth(name, tag, turn) - 1


def bank_plan():
    b = Banks()
    up = [(("m", m), m) for m in range(4)]
    b.stage("start", [("vec", 4), ("taps", 5), ("rel0", 6), ("rel1", 7), ("ws0", 4), ("ws1", 5)]
            + [(("x", k), k % 4) for k in range(KT)])
    b.stage("norm0", [("sum", 6)])
    b.stage("zv", up + [("mean", 4), ("var", 5)])
    b.stage("qkv0", up)
    b.stage("sgu", [(("vt", j), 4 + j) for j in range(4)] + [(("mix", j), 4 + j) for j in range(4)])
    b.stage("qkv", up, PAIRS - 1)
    b.stage("att", [("vtok", 6)] + [(("s", i), 4 + i % 2) for i in range(8)]
            + [(("t", i), 6) for i in range(8)] + [(("o", e), 7) for e in range(2)], PAIRS)
    out = [(("h", h, m), 4 * h + m) for h in range(2) for m in range(4)]
    b.stage("wout", out)
    b.stage("norm1", [("sum", 0)])
    b.stage("norm2", [("sum", 1)])
    down = [(("d", h, m), 4 + m) for h in range(2) for m in range(4)]
    b.stage("ffn", up + down, FFN_GROUPS)
    b.stage("norm3", [("sum", 0)])
    b.stage("norm4", [("sum", 1)])
    b.stage("cpin", [(("g", 0, m), m) for m in range(4)] + [(("g", 1, m), 4 + m) for m in range(4)]
            + [(("g", 2, m), m) for m in range(4)] + [(("pool", j), 6 + j % 2) for j in range(4)]
            + [("mean", 4), ("var", 5)])
    b.stage("cpout", out)
    b.stage("norm5", [("sum", 0)])
    b.stage("glu0", up + down, GLU_GROUPS)
    b.stage("norm6", [("sum", 0)])
    b.stage("hgin", up, HG_HEADS)
    b.stage("hg", [("lft", 4), ("ket", 4), ("o", 4), ("vt", 5), ("cum", 6), ("u", 6), ("sum", 6)]
            + [(("s", i), 5 if i % 2 == 0 else 7) for i in range(len(LEVELS) + 1)], HG_HEADS)
    b.stage("hgout", out)
    b.stage("norm7", [("sum", 0)])
    b.stage("glu1", up + down, GLU_GROUPS)
    b.stage("norm8", [("sum", 0)])
    b.stage("end", [(("y", k), 1 + k % 4) for k in range(KT)])
    return b


def build(nc, x, w, vec, sgu_w, sgu_b, rel_bias, dw_w, pool_w, ident_c, tri_c, onehot_c, lnmult_c,
          poolinv_c, mask_c, diag_c, scratch, out):
    banks = bank_plan()
    nth, before = banks.nth, banks.before

    with ExitStack() as ctx:
        def sb(name, shape, dt=F32, scope=ctx):
            return scope.enter_context(nc.sbuf_tensor(name, shape, dt))

        def sem(name):
            return ctx.enter_context(nc.semaphore(name))

        raw = sb("raw", [P, RING, 2, COLS])
        whi = sb("whi", [P, RING, 2, COLS], F32R)
        wlo = sb("wlo", [P, RING, 2, COLS], F32R)
        xT = sb("xT", [P, KT, SEQ])
        h_hi = sb("h_hi", [P, KT, SEQ], F32R)
        h_lo = sb("h_lo", [P, KT, SEQ], F32R)
        m_hi = sb("m_hi", [P, KT, SEQ], F32R)
        m_lo = sb("m_lo", [P, KT, SEQ], F32R)
        ident = sb("ident", [P, P])
        ones = sb("ones", [P, P])
        tri = sb("tri", [P, P])
        vecs = sb("vecs", [P, N_VEC])
        taps = sb("taps", [P, TAPS, 4])
        eps6 = sb("eps6", [P, 1])
        eps5 = sb("eps5", [P, 1])
        lbt = sb("lbt", [P, 8, HG_HEADS])
        hcol = sb("hcol", [P, HG_HEADS, 4])
        mask = sb("mask", [P, len(LEVELS), 64], I32)
        diag = sb("diag", [P, P], I32)
        poolinv = sb("poolinv", [P, 4, POOL_PAD])
        rs = sb("rs", [P, SEQ])
        hf = sb("hf", [P, 2, SEQ])
        sq = hf

        with ExitStack() as s:
            xin = sb("xin", [P, TT, D], scope=s)
            vrows = sb("vrows", [N_VEC, P], scope=s)
            trows = sb("trows", [TAPS * 4, P], scope=s)
            relb = sb("relb", [N_BUCKETS, N_HEADS], scope=s)
            onehot = sb("onehot", [N_BUCKETS, 1024], scope=s)
            lnmult = sb("lnmult", [N_HEADS, 1024], scope=s)
            relrow = sb("relrow", [N_HEADS, 1024], scope=s)
            wsin = sb("wsin", [P, 8, P], scope=s)
        with ExitStack() as s:
            btab = sb("btab", [P, N_HEADS, SKEW], scope=s)
            qs = sb("qs", [P, SEQ], scope=s)
            ks = sb("ks", [P, SEQ], scope=s)
            vT = sb("vT", [P, SEQ], scope=s)
            ug = sb("ug", [P, SEQ], scope=s)
            vtok = sb("vtok", [P, SEQ], scope=s)
            sbias = sb("sbias", [P, 2, SEQ], scope=s)
            prob = sb("prob", [P, 2, SEQ], scope=s)
            probT = sb("probT", [P, TT, SEQ], scope=s)
            gv = sb("gv", [P, 4, SEQ], scope=s)
            wsT = sb("wsT", [P, 8, P], scope=s)
            sgub = sb("sgub", [P, 4, P], scope=s)
            amax = sb("amax", [P, 8], scope=s)
            nmax = sb("nmax", [P, 8], scope=s)
            den = sb("den", [P, 8], scope=s)
            rden = sb("rden", [P, 8], scope=s)
        sgu_vt = probT
        with ExitStack() as s:
            acc = sb("acc", [P, KT, SEQ], scope=s)
            relu = sb("relu", [P, 2, SEQ], scope=s)
            hid = sb("hid", [P, 2, SEQ], scope=s)
        with ExitStack() as s:
            apad = sb("apad", [P, 4, PAD + SEQ], scope=s)
            conv = sb("conv", [P, 4, SEQ], scope=s)
            csq = sb("csq", [P, 4, SEQ], scope=s)
            csig = sb("csig", [P, 2, SEQ], scope=s)
            ctap = sb("ctap", [P, TAPS + 1], scope=s)
            upad = sb("upad", [P, 4, POOL_PAD + SEQ], scope=s)
            wsum = sb("wsum", [P, 2, POOL_PAD + SEQ], scope=s)
            pmean = sb("pmean", [P, SEQ], scope=s)
            pdiff = sb("pdiff", [P, 4, SEQ], scope=s)
            pout = sb("pout", [P, 4, SEQ], scope=s)
            poolw = sb("poolw", [P, 4, P], scope=s)
        with ExitStack() as s:
            silu = sb("silu", [P, 2, SEQ], scope=s)
            ghid = sb("ghid", [P, 2, SEQ], scope=s)
        with ExitStack() as s:
            sgf = sb("sgf", [P, SEQ], scope=s)
            sgg = sb("sgg", [P, SEQ], scope=s)
            gT = sb("gT", [P, SEQ], scope=s)
            gs = sb("gs", [P, SEQ], scope=s)
            qh = sb("qh", [P, SEQ], scope=s)
            kk = sb("kk", [P, SEQ], scope=s)
            iT = sb("iT", [P, SEQ], scope=s)
            lf = sb("lf", [P, SEQ], scope=s)
            lfT = sb("lfT", [P, SEQ], scope=s)
            vh = sb("vh", [P, SEQ], scope=s)
            cum = sb("cum", [P, SEQ], scope=s)
            e0 = sb("e0", [P, SEQ], scope=s)
            qb = sb("qb", [P, SEQ], scope=s)
            dend = sb("dend", [P, SEQ], scope=s)
            kend = sb("kend", [P, SEQ], scope=s)
            keT = sb("keT", [P, 3 * P], scope=s)
            state = sb("state", [P, 3 * P], scope=s)
            dlev = sb("dlev", [P, 2, SEQ], scope=s)
            elev = sb("elev", [P, 2, SEQ], scope=s)
            qlev = sb("qlev", [P, len(LEVELS), SEQ // 2], scope=s)
            klev = sb("klev", [P, len(LEVELS), SEQ], scope=s)
            score = sb("score", [P, SEQ], scope=s)
            hsq = sb("hsq", [P, SEQ], scope=s)
            hln = sb("hln", [P, SEQ], scope=s)
            hrs = hln
            hn = ho = hsq
            fcol = sb("fcol", [P, 4], scope=s)
            gcol = sb("gcol", [P, 1], scope=s)
        with ExitStack() as s:
            yT = sb("yT", [P, 2, SEQ], scope=s)
            otok = sb("otok", [P, TT, D], scope=s)

        ps = ctx.enter_context(nc.psum_tensor("ps", [P, 8, 512], F32))

        def bank(stage, tag):
            return ps[:, banks.bank(stage, tag), :]

        filled = [sem(f"filled{b}") for b in range(8)]
        drained = [sem(f"drained{b}") for b in range(8)]
        x_in = sem("x_in")
        consts_in = sem("consts_in")
        sgu_in = sem("sgu_in")
        poolw_in = sem("poolw_in")
        rel_out = sem("rel_out")
        btab_in = sem("btab_in")
        unit_in = [sem(f"unit_in{i}") for i in range(RING)]
        unit_hi = sem("unit_hi")
        unit_lo = sem("unit_lo")
        unit_begun = sem("unit_begun")
        set_up = sem("set_up")
        lb_step = sem("lb_step")
        lb_exp = sem("lb_exp")
        sq_ready = sem("sq_ready")
        sq_used = sem("sq_used")
        rs_ready = sem("rs_ready")
        hf_ready = sem("hf_ready")
        hi_ready = sem("hi_ready")
        lo_ready = sem("lo_ready")
        post_step = sem("post_step")
        x_ready = sem("x_ready")
        gelu_v = sem("gelu_v")
        sgu_step = sem("sgu_step")
        sgu_sq = sem("sgu_sq")
        sgu_y = sem("sgu_y")
        ug_ready = sem("ug_ready")
        sg_ready = sem("sg_ready")
        sg_hi = sem("sg_hi")
        sg_lo = sem("sg_lo")
        neg_ready = sem("neg_ready")
        prob_ready = sem("prob_ready")
        den_inv = sem("den_inv")
        probn_ready = sem("probn_ready")
        o_hi = sem("o_hi")
        acc_sq = sem("acc_sq")
        relu_ready = sem("relu_ready")
        hid_ready = sem("hid_ready")
        hid_hi = sem("hid_hi")
        hid_lo = sem("hid_lo")
        csig_ready = sem("csig_ready")
        ctap_ready = sem("ctap_ready")
        tap_done = sem("tap_done")
        win_step = sem("win_step")
        pdiff_ready = sem("pdiff_ready")
        pout_ready = sem("pout_ready")
        pout_hi = sem("pout_hi")
        pout_lo = sem("pout_lo")
        cln_step = sem("cln_step")
        cln_sq = sem("cln_sq")
        cln_y = sem("cln_y")
        cs_ready = sem("cs_ready")
        cs_hi = sem("cs_hi")
        cs_lo = sem("cs_lo")
        silu_ready = sem("silu_ready")
        ghid_hi = sem("ghid_hi")
        ghid_lo = sem("ghid_lo")
        fcol_ready = sem("fcol_ready")
        gcol_ready = sem("gcol_ready")
        sgf_ready = sem("sgf_ready")
        sgg_ready = sem("sgg_ready")
        lf_ready = sem("lf_ready")
        kk_ready = sem("kk_ready")
        gs_ready = sem("gs_ready")
        e0_ready = sem("e0_ready")
        dend_ready = sem("dend_ready")
        eend_ready = sem("eend_ready")
        kend_ready = sem("kend_ready")
        qb_ready = sem("qb_ready")
        dlev_ready = sem("dlev_ready")
        elev_ready = sem("elev_ready")
        qk_ready = sem("qk_ready")
        state_ready = sem("state_ready")
        placing = sem("placing")
        hsq_ready = sem("hsq_ready")
        hln_ready = sem("hln_ready")
        hrs_ready = sem("hrs_ready")
        hn_ready = sem("hn_ready")
        ho_ready = sem("ho_ready")
        ho_hi = sem("ho_hi")
        ho_lo = sem("ho_lo")
        y_ready = sem("y_ready")
        out_done = sem("out_done")

        def levels(t, m):
            return t.rearrange("p (n two m) -> p n two m", two=2, m=m)

        def tile_of(t, p):
            return t[:, p, :] if isinstance(p, int) else t[:, bass.ds(p, 1), :].squeeze(1)

        block = ctx.enter_context(nc.Block())

        @block.sync
        def _(sp):
            for t in range(TT):
                sp.dma_start(xin[:, t, :], x[t * P:(t + 1) * P, :]).then_inc(x_in, 16)

            def load(first, j, halves, turn=0, per=0):
                u = first + j
                if u >= RING:
                    sp.wait_ge(unit_lo, turn * per + (u - RING + 1))
                for a, src in enumerate(halves):
                    dst = raw[:, u % RING, a, :]
                    if len(src.shape) == 3:
                        dst = dst.rearrange("p (b c) -> p b c", b=src.shape[1])
                    sp.dma_start(dst, src).then_inc(unit_in[u % RING], 16)

            def rows(name):
                return w[name].rearrange("(k p) n -> p k n", p=P)

            def pieces(name, kts, c0):
                v = rows(name)
                return [v[:, k, bass.ds(c0, COLS)] for k in kts]

            wi = w["w_in"].rearrange("(k p) (b c) -> p k b c", p=P, c=D_ATTN)
            for j in range(4):
                load(U_ZV, j, [wi[:, 2 * j + a, 4, :] for a in range(2)])
            with sp.Fori(0, PAIRS) as p:
                for j in range(4):
                    load(U_QKV, j, [wi[:, 2 * j + a, 0:4, bass.ds(p * P, P)] for a in range(2)], p, 4)
            order = ((4, 5), (6, 7), (0, 1), (2, 3))
            for h in range(2):
                for j, kts in enumerate(order):
                    load(U_WOUT, 4 * h + j, pieces("w_out", kts, h * COLS))
            with sp.Fori(0, FFN_GROUPS) as g:
                for j in range(4):
                    load(U_FFN, j, pieces("w_ff1", (2 * j, 2 * j + 1), g * COLS), g, 8)
                v = rows("w_ff2")
                for j in range(4):
                    h, i = j // 2, j % 2
                    load(U_FFN, 4 + j, [v[:, bass.ds(g * 4 + (2 * i + a), 1), h * COLS:(h + 1) * COLS]
                                        for a in range(2)], g, 8)
            ci = w["cp_w_in_2"].rearrange("(k p) (b c) -> p k b c", p=P, c=D // 2)
            for g in range(2):
                for j in range(4):
                    load(U_CPIN, 4 * g + j, [ci[:, 2 * j + a, 0:2, g * 256:(g + 1) * 256] for a in range(2)])
            for j in range(4):
                load(U_CPIN, 8 + j, [ci[:, 2 * j + a, 2, :] for a in range(2)])
            for h in range(2):
                for j, kts in enumerate(order):
                    load(U_CPOUT, 4 * h + j, pieces("cp_w_out_2", kts, h * COLS))

            def glu(layer):
                w1, w3, w2 = (w[f"ffn_{n}_2"][layer].rearrange("(k p) n -> p k n", p=P) for n in ("w1", "w3", "w2"))

                def up(j0, g, turn, per):
                    for j in range(4):
                        u = U_GLU[layer] + j0 + j
                        if u >= RING:
                            sp.wait_ge(unit_lo, turn * per + (u - RING + 1))
                        slot = raw[:, u % RING, :, :]
                        for a, v in enumerate((w1, w3)):
                            sp.dma_start(slot[:, :, a * 256:(a + 1) * 256],
                                         v[:, 2 * j:2 * j + 2, bass.ds(g * 256, 256)]).then_inc(unit_in[u % RING], 16)

                def down(j0, g, turn, per):
                    for h in range(2):
                        load(U_GLU[layer], j0 + h, [w2[:, bass.ds(g * 2 + a, 1), h * COLS:(h + 1) * COLS]
                                                    for a in range(2)], turn, per)

                up(0, 0, 0, 0)
                with sp.Fori(0, GLU_GROUPS // 2) as i:
                    up(4, i * 2 + 1, i, 12)
                    down(8, i * 2, i, 12)
                    up(10, i * 2 + 2, i, 12)
                    down(14, i * 2 + 1, i, 12)
                down(6 * GLU_GROUPS - 2, GLU_GROUPS - 1, 0, 0)

            glu(0)
            hi = w["hg_w_in_2"].rearrange("(k p) (b c) -> p k b c", p=P, c=D)
            with sp.Fori(0, HG_HEADS) as n:
                for j in range(4):
                    load(U_HGIN, j, [hi[:, 2 * j + a, 0:4, bass.ds(n * P, P)] for a in range(2)], n, 4)
            for h in range(2):
                for j in range(4):
                    load(U_HGOUT, 4 * h + j, pieces("hg_w_out_2", (2 * j, 2 * j + 1), h * COLS))
            glu(1)

        @block.gpsimd
        def _(pool):
            def lo_parts(first, n):
                with pool.Fori(0, n // RING) as r:
                    for i in range(RING):
                        u = first + i
                        pool.wait_ge(unit_hi, r * RING + (u + 1))
                        pool.tensor_tensor(wlo[:, u % RING, :, :], raw[:, u % RING, :, :],
                                           whi[:, u % RING, :, :].bitcast(F32), ALU.subtract).then_inc(unit_lo, 1)

            lo_parts(0, U_CPOUT)
            n = 0
            pool.wait_ge(set_up, 6)
            for j in range(4):
                last = upad[:, j, :]
                pool.wait_ge(drained[j], nth("cpin", ("g", 2, j)))
                for i in range(j + 1):
                    d = 1 << i
                    lo = 2 * d - 1
                    if n:
                        pool.wait_ge(win_step, n)
                    pool.tensor_tensor(wsum[:, i % 2, lo:], last[:, lo:], last[:, lo - d:POOL_PAD + SEQ - d],
                                       ALU.add).then_inc(win_step, 1)
                    n += 1
                    last = wsum[:, i % 2, :]
                pool.wait_ge(win_step, n)
                pool.tensor_scalar(pmean[:, :], last[:, POOL_PAD:], 1.0 / POOL_WINDOWS[j], None,
                                   ALU.mult).then_inc(win_step, 1)
                n += 1
                pool.wait_ge(win_step, n)
                pool.tensor_tensor(pmean[:, 0:POOL_PAD], last[:, POOL_PAD:2 * POOL_PAD], poolinv[:, j, :],
                                   ALU.mult).then_inc(win_step, 1)
                n += 1
                pool.wait_ge(win_step, n)
                pool.tensor_tensor(pdiff[:, j, :], pmean[:, :], upad[:, j, POOL_PAD:], ALU.subtract)\
                    .then_inc(pdiff_ready, 1)
                pool.wait_ge(pdiff_ready, j + 1)
            for j in range(4):
                pool.wait_ge(pout_hi, j + 1)
                pool.tensor_tensor(m_lo[:, 4 + j, :], pout[:, j, :], m_hi[:, 4 + j, :].bitcast(F32), ALU.subtract)\
                    .then_inc(pout_lo, 1)
            lo_parts(U_CPOUT, UNITS - U_CPOUT)

        @block.scalar
        def _(act):
            n_const = 0
            for dst, src in ((vrows[:, :], vec), (ident[:, :], ident_c),
                             (trows[:, :], dw_w.rearrange("t (j p) -> (t j) p", p=P)),
                             (relb[:, :], rel_bias), (onehot[:, :], onehot_c), (lnmult[:, :], lnmult_c),
                             (tri[:, :], tri_c), (mask[:, :, :], mask_c), (diag[:, :], diag_c),
                             (poolinv[:, :, :], poolinv_c), (wsin[:, :, :], sgu_w.rearrange("g t s -> t g s"))):
                act.dma_start(dst, src).then_inc(consts_in, 16)
                n_const += 16
            act.preload_act_table_set(LOG_TABLES)

            def split(first, j, turn=0, per=0):
                u = first + j + AHEAD
                act.wait_ge(unit_in[u % RING], turn * (8 * per) + 32 * (u // RING + 1))
                if u >= RING:
                    act.wait_ge(unit_begun, turn * per + (u - RING + 2))
                act.activation(whi[:, u % RING, :, :], raw[:, u % RING, :, :], ACT.Copy).then_inc(unit_hi, 1)

            def squares(i, src, ready):
                for k in range(KT):
                    ready(k)
                    if k >= 2:
                        act.wait_ge(sq_used, 7 * i + k - 1)
                    act.activation(sq[:, k % 2, :], src[:, k, :], ACT.Square).then_inc(sq_ready, 1)

            def inv_rms(i):
                act.wait_ge(filled[banks.bank(f"norm{i}", "sum")], nth(f"norm{i}", "sum"))
                act.activation(rs[:, :], bank(f"norm{i}", "sum"), ACT.Ln, bias=eps6[:, :], scale=1.0 / D)\
                    .then_inc(drained[banks.bank(f"norm{i}", "sum")], 1)
                act.wait_ge(drained[banks.bank(f"norm{i}", "sum")], nth(f"norm{i}", "sum"))
                act.activation(rs[:, :], rs[:, :], ACT.Exp, scale=-0.5).then_inc(rs_ready, 1)

            def h_parts(i):
                for k in range(KT):
                    act.wait_ge(hf_ready, KT * i + k + 1)
                    act.activation(h_hi[:, k, :], hf[:, k % 2, :], ACT.Copy).then_inc(hi_ready, 1)

            def x_is(n):
                return lambda k: act.wait_ge(x_ready, n + k + 1)

            def out_done_is(stage):
                return lambda k: act.wait_ge(drained[k], nth(stage, ("h", k // 4, k % 4)))

            for k in range(1, KT, 2):
                act.wait_ge(filled[k % 4], nth("start", ("x", k)))
                act.activation(xT[:, k, :], bank("start", ("x", k)), ACT.Copy).then_inc(drained[k % 4], 1)
            squares(0, xT, lambda k: act.wait_ge(drained[k % 4], nth("start", ("x", k))))
            act.wait_ge(unit_in[0], 32)
            act.activation(whi[:, 0, :, :], raw[:, 0, :, :], ACT.Copy).then_inc(unit_hi, 1)
            act.wait_ge(unit_in[1], 32)
            act.activation(whi[:, 1, :, :], raw[:, 1, :, :], ACT.Copy).then_inc(unit_hi, 1)
            act.wait_ge(set_up, 3)
            inv_rms(0)
            h_parts(0)
            act.wait_ge(lb_step, 3)
            act.activation(lbt[:, 2, :], lbt[:, 1, :], ACT.Exp).then_inc(lb_exp, 1)
            act.activation(lbt[:, 4, :], lbt[:, 3, :], ACT.Exp).then_inc(lb_exp, 1)
            for i in range(2):
                act.wait_ge(drained[6 + i], nth("start", f"rel{i}"))
            act.dma_start(scratch[:, :, 0:1024], relrow[:, :].unsqueeze(1).broadcast_to([N_HEADS, P, 1024]))\
                .then_inc(rel_out, 16)
            act.wait_ge(rel_out, 16)
            act.dma_start(btab[:, :, :], bass.AP(scratch.tensor, P - 1, [[1024, P], [1025 * P, N_HEADS], [1, SKEW]]))\
                .then_inc(btab_in, 16)
            for e in range(2):
                act.dma_start(sgub[HEAD_DIM * e:HEAD_DIM * (e + 1), :, :],
                              bass.AP(sgu_b.tensor, e * P, [[0, HEAD_DIM], [2 * P, 4], [1, P]])).then_inc(sgu_in, 16)

            for j in range(4):
                split(U_ZV, j)
            for m in range(4):
                act.wait_ge(filled[m], nth("zv", ("m", m)))
                act.activation(gv[:, m, :], bank("zv", ("m", m)), ACT.Gelu_apprx_tanh).then_inc(drained[m], 1)
            act.preload_act_table_set(LOG_TABLES)
            split(U_QKV, 0)
            for m in range(4):
                act.wait_ge(sgu_step, m + 1)
                act.activation(sgu_vt[:, m, :], gv[:, m, :], ACT.Square).then_inc(sgu_sq, 1)
            split(U_QKV, 1)
            act.wait_ge(filled[5], nth("zv", "var"))
            act.activation(rs[:, :], bank("zv", "var"), ACT.Ln, bias=eps5[:, :], scale=1.0 / (4 * P))\
                .then_inc(drained[5], 1)
            act.wait_ge(drained[5], nth("zv", "var"))
            act.activation(rs[:, :], rs[:, :], ACT.Exp, scale=-0.5).then_inc(rs_ready, 1)
            split(U_QKV, 2)
            split(U_QKV, 3)

            def drain_qkv(stage, turn, p):
                for m, dst in enumerate((qs, ks, vT)):
                    act.wait_ge(filled[m], nth(stage, ("m", m), turn))
                    act.activation(dst[:, :], bank(stage, ("m", m)), ACT.Copy,
                                   scale=HEAD_DIM ** -0.5 if m == 0 else 1.0).then_inc(drained[m], 1)
                act.wait_ge(filled[3], nth(stage, ("m", 3), turn))
                if not isinstance(p, int):
                    act.wait_ge(sg_lo, p)
                act.activation(ug[:, :], bank(stage, ("m", 3)), ACT.Gelu_apprx_tanh).then_inc(drained[3], 1)
                act.preload_act_table_set(LOG_TABLES)

            def sgu_part(p):
                act.wait_ge(sg_ready, p + 1)
                act.activation(tile_of(m_hi, 4 + p),
                               ug[:, :], ACT.Copy).then_inc(sg_hi, 1)

            for j in range(4):
                act.wait_ge(filled[4 + j], nth("sgu", ("vt", j)))
                act.activation(sgu_vt[:, j, :], bank("sgu", ("vt", j)), ACT.Copy).then_inc(drained[4 + j], 1)
            drain_qkv("qkv0", 0, 0)
            sgu_part(0)

            def attend(p, units):
                act.wait_ge(filled[6], nth("att", "vtok", p))
                act.activation(vtok[:, :], bank("att", "vtok"), ACT.Copy).then_inc(drained[6], 1)
                for i in range(8):
                    act.wait_ge(neg_ready, p * 8 + (i + 1))
                    if i >= 2:
                        act.wait_ge(filled[6], nth("att", ("t", i - 2), p))
                    act.activation(prob[:, i % 2, :], sbias[:, i % 2, :], ACT.Exp, bias=nmax[:, i:i + 1],
                                   accum_out=den[:, i:i + 1]).then_inc(prob_ready, 1)
                    if i % 2:
                        units(i // 2)
                    if i in (5, 7):
                        e = (i - 5) // 2
                        rows = slice(HEAD_DIM * e, HEAD_DIM * (e + 1))
                        act.wait_ge(filled[7], nth("att", ("o", e), p))
                        act.activation(tile_of(m_hi, p)[rows],
                                       bank("att", ("o", e))[rows, :], ACT.Copy).then_inc(o_hi, 1)

            with act.Fori(0, PAIRS - 1) as p:
                attend(p, lambda i: split(U_QKV + 4, i, p, 4))
                drain_qkv("qkv", p, p + 1)
                sgu_part(p + 1)
            attend(PAIRS - 1, lambda i: split(U_WOUT, i) if i < 3 else None)
            for j in range(3, 8):
                split(U_WOUT, j)
            squares(1, acc, lambda k: act.wait_ge(drained[k], nth("wout", ("h", k // 4, k % 4))))
            inv_rms(1)
            squares(2, xT, x_is(0))
            inv_rms(2)
            h_parts(1)

            with act.Fori(0, FFN_GROUPS) as g:
                for j in range(4):
                    split(U_FFN, j, g, 8)
                for m in range(4):
                    act.wait_ge(filled[m], nth("ffn", ("m", m), g))
                    if m >= 2:
                        act.wait_ge(hid_ready, g * 4 + (m - 1))
                    act.activation(relu[:, m % 2, :], bank("ffn", ("m", m)), ACT.Relu).then_inc(drained[m], 1)
                    act.wait_ge(drained[m], nth("ffn", ("m", m), g))
                    act.activation(m_hi[:, m, :], relu[:, m % 2, :], ACT.Square).then_inc(hid_hi, 1)
                for j in range(4, 8):
                    split(U_FFN, j, g, 8)
            squares(3, acc, lambda k: act.wait_ge(
                drained[4 + k % 4], nth("ffn", ("d", k // 4, k % 4), FFN_GROUPS - 1)))
            inv_rms(3)
            squares(4, xT, x_is(KT))
            inv_rms(4)
            h_parts(2)

            act.dma_start(poolw[:, :, :], pool_w.rearrange("g c d -> c g d")).then_inc(poolw_in, 16)
            for g in range(2):
                for j in range(4):
                    split(U_CPIN, 4 * g + j)
                for i in range(2):
                    b = banks.bank("cpin", ("g", g, 2 + i))
                    act.wait_ge(filled[b], nth("cpin", ("g", g, 2 + i)))
                    if g:
                        act.wait_ge(drained[i], nth("cpin", ("g", 0, i)))
                    act.activation(csig[:, i, :], bank("cpin", ("g", g, 2 + i)), ACT.Sigmoid).then_inc(drained[b], 1)
            for j in range(4):
                split(U_CPIN, 8 + j)
            for m in range(4):
                act.wait_ge(filled[m], nth("cpin", ("g", 2, m)))
                act.activation(upad[:, m, POOL_PAD:], bank("cpin", ("g", 2, m)), ACT.Copy).then_inc(drained[m], 1)
            for j in range(4):
                b = banks.bank("cpin", ("pool", j))
                act.wait_ge(filled[b], nth("cpin", ("pool", j)))
                c = COL["cp_pool_scale_2"] + j
                act.activation(pout[:, j, :], bank("cpin", ("pool", j)), ACT.Copy, scale=vecs[:, c:c + 1])\
                    .then_inc(drained[b], 1)
                act.wait_ge(drained[b], nth("cpin", ("pool", j)))
                act.activation(m_hi[:, 4 + j, :], pout[:, j, :], ACT.Copy).then_inc(pout_hi, 1)
            split(U_CPOUT, 0)
            split(U_CPOUT, 1)
            act.preload_act_table_set(LOG_TABLES)
            for j in range(4):
                act.wait_ge(cln_step, j + 1)
                act.activation(csq[:, j, :], conv[:, j, :], ACT.Square).then_inc(cln_sq, 1)
            act.wait_ge(filled[5], nth("cpin", "var"))
            act.activation(rs[:, :], bank("cpin", "var"), ACT.Ln, bias=eps6[:, :], scale=1.0 / (4 * P))\
                .then_inc(drained[5], 1)
            act.wait_ge(drained[5], nth("cpin", "var"))
            act.activation(rs[:, :], rs[:, :], ACT.Exp, scale=-0.5).then_inc(rs_ready, 1)
            for j in range(4):
                cg, cb = COL["cp_ln_g_2"] + j, COL["cp_ln_b_2"] + j
                act.wait_ge(cln_y, j + 1)
                act.activation(csq[:, j, :], conv[:, j, :], ACT.Silu, bias=vecs[:, cb:cb + 1],
                               scale=vecs[:, cg:cg + 1]).then_inc(cs_ready, 1)
                act.wait_ge(cs_ready, j + 1)
                act.activation(m_hi[:, j, :], csq[:, j, :], ACT.Copy).then_inc(cs_hi, 1)
            act.preload_act_table_set(LOG_TABLES)
            for j in range(2, 8):
                split(U_CPOUT, j)
            squares(5, xT, out_done_is("cpout"))
            inv_rms(5)
            h_parts(3)

            def glu(layer):
                first, stage = U_GLU[layer], f"glu{layer}"

                def up(j0, g, par, turn, per):
                    for j in range(4):
                        split(first, j0 + j, turn, per)
                    for i in range(2):
                        act.wait_ge(filled[i], nth(stage, ("m", i), g))
                        act.wait_ge(drained[2 + i], before(stage, ("m", 2 + i), g))
                        act.activation(silu[:, i, :], bank(stage, ("m", i)), ACT.Silu).then_inc(drained[i], 1)
                    for i in range(2):
                        act.wait_ge(drained[2 + i], nth(stage, ("m", 2 + i), g))
                        act.activation(m_hi[:, 2 * par + i, :], ghid[:, i, :], ACT.Copy).then_inc(ghid_hi, 1)

                def down(j0, turn, per):
                    for h in range(2):
                        split(first, j0 + h, turn, per)

                up(0, 0, 0, 0, 0)
                with act.Fori(0, GLU_GROUPS // 2) as i:
                    up(4, i * 2 + 1, 1, i, 12)
                    down(8, i, 12)
                    up(10, i * 2 + 2, 0, i, 12)
                    down(14, i, 12)
                if layer == 0:
                    down(6 * GLU_GROUPS - 2, 0, 0)
                act.preload_act_table_set(LOG_TABLES)

            glu(0)

            def glu_x(layer):
                return lambda k: act.wait_ge(drained[4 + k % 4], nth(f"glu{layer}", ("d", k // 4, k % 4), GLU_GROUPS - 1))

            squares(6, xT, glu_x(0))
            inv_rms(6)
            h_parts(4)

            def drain_head(n):
                act.wait_ge(filled[1], nth("hgin", ("m", 1), n))
                act.activation(sgf[:, :], bank("hgin", ("m", 1)), ACT.Sigmoid).then_inc(drained[1], 1)
                act.wait_ge(filled[0], nth("hgin", ("m", 0), n))
                act.activation(qh[:, :], bank("hgin", ("m", 0)), ACT.Copy).then_inc(drained[0], 1)
                act.wait_ge(filled[2], nth("hgin", ("m", 2), n))
                act.activation(iT[:, :], bank("hgin", ("m", 2)), ACT.Copy).then_inc(drained[2], 1)
                act.wait_ge(filled[3], nth("hgin", ("m", 3), n))
                act.activation(sgg[:, :], bank("hgin", ("m", 3)), ACT.Sigmoid).then_inc(sgg_ready, 1)
                act.activation(gT[:, :], bank("hgin", ("m", 3)), ACT.Copy).then_inc(drained[3], 1)
                act.preload_act_table_set(LOG_TABLES)
                act.wait_ge(drained[1], nth("hgin", ("m", 1), n))
                act.wait_ge(fcol_ready, n + 1)
                act.activation(lf[:, :], sgf[:, :], ACT.Ln, bias=fcol[:, 1:2], scale=fcol[:, 0:1]).then_inc(lf_ready, 1)

            def core(n, units, tail):
                act.wait_ge(filled[4], nth("hg", "lft", n))
                act.activation(lfT[:, :], bank("hg", "lft"), ACT.Copy).then_inc(drained[4], 1)
                units(0)
                act.wait_ge(filled[5], nth("hg", "vt", n))
                act.activation(vh[:, :], bank("hg", "vt"), ACT.Copy).then_inc(drained[5], 1)
                act.wait_ge(filled[6], nth("hg", "cum", n))
                act.activation(cum[:, :], bank("hg", "cum"), ACT.Copy).then_inc(drained[6], 1)
                act.wait_ge(drained[6], nth("hg", "cum", n))
                act.activation(e0[:, :], cum[:, :], ACT.Exp).then_inc(e0_ready, 1)
                act.wait_ge(dend_ready, n + 1)
                act.activation(dend[:, :], dend[:, :], ACT.Exp).then_inc(eend_ready, 1)
                L = len(LEVELS)
                for i in range(L):
                    act.wait_ge(dlev_ready, n * (2 * L) + (2 * i + 2))
                    if i >= 2:
                        act.wait_ge(qk_ready, n * (2 * L) + 2 * (i - 1))
                    act.activation(elev[:, i % 2, :], dlev[:, i % 2, :], ACT.Exp).then_inc(elev_ready, 1)
                    if i == 1:
                        units(1)
                act.wait_ge(filled[4], nth("hg", "ket", n))
                act.activation(keT[:, :], bank("hg", "ket")[:, 0:3 * P], ACT.Copy).then_inc(drained[4], 1)
                units(2)
                units(3)
                tail()
                act.wait_ge(filled[4], nth("hg", "o", n))
                act.activation(hsq[:, :], bank("hg", "o"), ACT.Square).then_inc(hsq_ready, 1)
                act.wait_ge(filled[6], nth("hg", "sum", n))
                act.activation(hln[:, :], bank("hg", "sum"), ACT.Ln, bias=eps6[:, :], scale=1.0 / P)\
                    .then_inc(drained[6], 1)
                act.wait_ge(drained[6], nth("hg", "sum", n))
                act.activation(hrs[:, :], hln[:, :], ACT.Exp, scale=-0.5).then_inc(hrs_ready, 1)
                act.wait_ge(ho_ready, n + 1)
                act.activation(tile_of(m_hi, n),
                               ho[:, :], ACT.Copy).then_inc(ho_hi, 1)

            for j in range(4):
                split(U_HGIN, j)
            drain_head(0)

            def next_head(n):
                act.wait_ge(qk_ready, n * (2 * len(LEVELS)) + 2 * len(LEVELS))
                act.wait_ge(filled[7], nth("hg", ("s", len(LEVELS)), n))
                act.wait_ge(gs_ready, n + 1)
                drain_head(n + 1)

            with act.Fori(0, HG_HEADS - 1) as n:
                core(n, lambda j: split(U_HGIN + 4, j, n, 4), lambda: next_head(n))
            core(HG_HEADS - 1, lambda j: split(U_HGOUT, j), lambda: None)
            for j in range(4, 8):
                split(U_HGOUT, j)
            squares(7, xT, out_done_is("hgout"))
            inv_rms(7)
            h_parts(5)
            glu(1)
            squares(8, xT, glu_x(1))
            inv_rms(8)
            for k in range(1, KT, 2):
                b = banks.bank("end", ("y", k))
                act.wait_ge(filled[b], nth("end", ("y", k)))
                act.activation(otok[:, :, k * P:(k + 1) * P], bank("end", ("y", k)).rearrange("p (t f) -> p t f", f=P),
                               ACT.Copy).then_inc(drained[b], 1)
            for k in range(KT):
                b = banks.bank("end", ("y", k))
                act.wait_ge(drained[b], nth("end", ("y", k)))
            for t in range(TT):
                act.dma_start(out[t * P:(t + 1) * P, :], otok[:, t, :]).then_inc(out_done, 16)
            act.wait_ge(out_done, 16 * TT)

        @block.tensor
        def _(pe):
            def unit(first, j, xh, xl, kts, stage, tags, starts, stops, turn=0, per=0, order=(0, 1, 2, 3), use=None,
                     wait_tile=None):
                use = turn if use is None else use
                u = first + j
                s = u % RING
                pe.wait_ge(unit_lo, turn * per + (u + 1))
                begun = False
                for a in range(2):
                    if wait_tile:
                        wait_tile(a)
                    for m in order:
                        b = banks.bank(stage, tags[m])
                        if starts and a == 0:
                            pe.wait_ge(drained[b], before(stage, tags[m], use))
                        for i, (wt, xt) in enumerate(((wlo, xh), (whi, xl), (whi, xh))):
                            last = stops and a == 1 and i == 2
                            mm = pe.matmul(ps[:, b, :], wt[:, s, a, m * P:(m + 1) * P], xt[:, kts[a], :],
                                           start=starts and a == 0 and i == 0, stop=last)
                            if not begun:
                                mm.then_inc(unit_begun, 1)
                                begun = True
                            if last:
                                mm.then_inc(filled[b], 1)

            def group(first, j0, stage, tags, turn=0, per=0, order=(0, 1, 2, 3), use=None, n=None, between=None):
                for j in range(4):
                    def tile(a, j=j):
                        pe.wait_ge(lo_ready, KT * n + 2 * j + a + 1)
                    unit(first, j0 + j, h_hi, h_lo, (2 * j, 2 * j + 1), stage, tags, j == 0, j == 3, turn, per, order,
                         use, tile if n is not None else None)
                    if between:
                        between(j)

            def norm_sum(i):
                b = banks.bank(f"norm{i}", "sum")
                pe.wait_ge(drained[b], before(f"norm{i}", "sum"))
                for k in range(KT):
                    pe.wait_ge(sq_ready, KT * i + k + 1)
                    mm = pe.matmul(ps[:, b, :], ones[:, :], sq[:, k % 2, :], start=k == 0, stop=k == KT - 1)
                    mm.then_inc(sq_used if k < KT - 1 else filled[b], 1)

            up_tags = [("m", m) for m in range(4)]

            pe.wait_ge(consts_in, 16 * 11)
            pe.transpose(bank("start", "vec")[:, 0:N_VEC], vrows[:, :], ident[0:N_VEC, 0:N_VEC]).then_inc(filled[4], 1)
            pe.transpose(bank("start", "taps")[:, 0:4 * TAPS], trows[:, :], ident[0:4 * TAPS, 0:4 * TAPS])\
                .then_inc(filled[5], 1)
            pe.wait_ge(x_in, 16 * TT)
            for k in range(KT):
                b = k % 4
                pe.wait_ge(drained[b], before("start", ("x", k)))
                for t in range(TT):
                    mm = pe.transpose(ps[:, b, t * P:(t + 1) * P], xin[:, t, k * P:(k + 1) * P], ident[:, :])
                mm.then_inc(filled[b], 1)
            for i in range(2):
                pe.matmul(bank("start", f"rel{i}")[0:N_HEADS, :], relb[:, :], onehot[:, i * 512:(i + 1) * 512],
                          start=True, stop=True).then_inc(filled[6 + i], 1)
            for i in range(2):
                pe.wait_ge(drained[4 + i], before("start", f"ws{i}"))
                for g in range(4):
                    mm = pe.transpose(ps[:, 4 + i, g * P:(g + 1) * P], wsin[:, 4 * i + g, :], ident[:, :])
                mm.then_inc(filled[4 + i], 1)
            pe.wait_ge(set_up, 3)
            norm_sum(0)

            group(U_ZV, 0, "zv", up_tags, n=0)

            def sgu_sums(j):
                if j == 0:
                    pe.wait_ge(drained[4], before("zv", "mean"))
                    for m in range(4):
                        pe.wait_ge(drained[m], nth("zv", ("m", m)))
                        mm = pe.matmul(bank("zv", "mean"), ones[:, :], gv[:, m, :], start=m == 0, stop=m == 3)
                    mm.then_inc(filled[4], 1)
                if j == 1:
                    pe.wait_ge(drained[5], before("zv", "var"))
                    for m in range(4):
                        pe.wait_ge(sgu_sq, m + 1)
                        mm = pe.matmul(bank("zv", "var"), ones[:, :], sgu_vt[:, m, :], start=m == 0, stop=m == 3)
                    mm.then_inc(filled[5], 1)

            group(U_QKV, 0, "qkv0", up_tags, between=sgu_sums)
            for j in range(4):
                pe.wait_ge(drained[4 + j], before("sgu", ("vt", j)))
                pe.wait_ge(sgu_y, j + 1)
                for t in range(TT):
                    mm = pe.transpose(ps[:, 4 + j, t * P:(t + 1) * P], gv[:, j, t * P:(t + 1) * P], ident[:, :])
                mm.then_inc(filled[4 + j], 1)
            for j in range(4):
                pe.wait_ge(drained[4 + j], before("sgu", ("mix", j)))
                for t in range(TT):
                    for e in range(2):
                        mm = pe.matmul(ps[HEAD_DIM * e:HEAD_DIM * (e + 1), 4 + j, t * P:(t + 1) * P],
                                       sgu_vt[:, j, t * P + HEAD_DIM * e:t * P + HEAD_DIM * (e + 1)],
                                       wsT[:, 2 * j + e, :], start=True, stop=True)
                mm.then_inc(filled[4 + j], 1)

            def attend(p, units):
                def scores(i):
                    e, t = i // 4, i % 4
                    rows = slice(HEAD_DIM * e, HEAD_DIM * (e + 1))
                    b = banks.bank("att", ("s", i))
                    pe.wait_ge(drained[b], before("att", ("s", i), p))
                    pe.matmul(ps[:, b, :], qs[rows, t * P:(t + 1) * P], ks[rows, :], start=True, stop=True)\
                        .then_inc(filled[b], 1)

                def turn(i):
                    pe.wait_ge(probn_ready, p * 8 + (i + 1))
                    pe.wait_ge(drained[6], before("att", ("t", i), p))
                    for k in range(TT):
                        mm = pe.transpose(ps[:, 6, k * P:(k + 1) * P], prob[:, i % 2, k * P:(k + 1) * P], ident[:, :])
                    mm.then_inc(filled[6], 1)

                def values(e):
                    rows = slice(HEAD_DIM * e, HEAD_DIM * (e + 1))
                    pe.wait_ge(drained[7], before("att", ("o", e), p))
                    pe.wait_ge(drained[6], nth("att", ("t", 4 * e + 3), p))
                    for k in range(TT):
                        mm = pe.matmul(ps[rows, 7, :], vtok[:, k * P + HEAD_DIM * e:k * P + HEAD_DIM * (e + 1)], probT[:, k, :], start=k == 0, stop=k == TT - 1)
                    mm.then_inc(filled[7], 1)

                pe.wait_ge(drained[2], vT_count(p))
                pe.wait_ge(drained[6], before("att", "vtok", p))
                for t in range(TT):
                    mm = pe.transpose(ps[:, 6, t * P:(t + 1) * P], vT[:, t * P:(t + 1) * P], ident[:, :])
                mm.then_inc(filled[6], 1)
                scores(0)
                scores(1)
                units(0)
                turn(0)
                scores(2)
                turn(1)
                scores(3)
                units(1)
                turn(2)
                scores(4)
                turn(3)
                scores(5)
                units(2)
                values(0)
                turn(4)
                scores(6)
                turn(5)
                scores(7)
                units(3)
                turn(6)
                turn(7)
                values(1)

            def vT_count(p):
                return nth("qkv0", ("m", 2)) + p

            with pe.Fori(0, PAIRS - 1) as p:
                attend(p, lambda j: unit(U_QKV + 4, j, h_hi, h_lo, (2 * j, 2 * j + 1), "qkv", up_tags, j == 0, j == 3, p, 4))

            order = ((4, 5), (6, 7), (0, 1), (2, 3))

            def out_unit(first, stage, j):
                h = j // 4
                unit(first, j, m_hi, m_lo, order[j % 4], stage, [("h", h, m) for m in range(4)], j % 4 == 0, j % 4 == 3)

            def wout_early(j):
                if j == 0:
                    pe.wait_ge(sg_lo, PAIRS)
                if j < 3:
                    out_unit(U_WOUT, "wout", j)

            attend(PAIRS - 1, wout_early)
            pe.wait_ge(drained[7], nth("att", ("o", 1), PAIRS - 1))
            for j in range(3, 8):
                out_unit(U_WOUT, "wout", j)
            norm_sum(1)
            norm_sum(2)

            with pe.Fori(0, FFN_GROUPS) as g:
                group(U_FFN, 0, "ffn", up_tags, g, 8, n=1)
                for j in range(4):
                    h, i = j // 2, j % 2

                    def tile(a):
                        pe.wait_ge(hid_lo, g * 4 + (2 * i + a + 1))
                    unit(U_FFN, 4 + j, m_hi, m_lo, (2 * i, 2 * i + 1), "ffn", [("d", h, m) for m in range(4)],
                         i == 0, i == 1, g, 8, wait_tile=tile)
            norm_sum(3)
            norm_sum(4)

            for g in range(3):
                group(U_CPIN, 4 * g, "cpin", [("g", g, m) for m in range(4)], n=2 if g == 0 else None)
            pe.wait_ge(poolw_in, 16)
            for j in range(4):
                b = banks.bank("cpin", ("pool", j))
                pe.wait_ge(drained[b], before("cpin", ("pool", j)))
                pe.wait_ge(pdiff_ready, j + 1)
                pe.matmul(ps[:, b, :], poolw[:, j, :], pdiff[:, j, :], start=True, stop=True).then_inc(filled[b], 1)
            pe.wait_ge(pout_lo, 4)
            out_unit(U_CPOUT, "cpout", 0)
            out_unit(U_CPOUT, "cpout", 1)
            pe.wait_ge(drained[4], before("cpin", "mean"))
            for j in range(4):
                pe.wait_ge(tap_done, TAPS * (j + 1))
                mm = pe.matmul(bank("cpin", "mean"), ones[:, :], conv[:, j, :], start=j == 0, stop=j == 3)
            mm.then_inc(filled[4], 1)
            pe.wait_ge(drained[5], before("cpin", "var"))
            for j in range(4):
                pe.wait_ge(cln_sq, j + 1)
                mm = pe.matmul(bank("cpin", "var"), ones[:, :], csq[:, j, :], start=j == 0, stop=j == 3)
            mm.then_inc(filled[5], 1)
            pe.wait_ge(cs_lo, 4)
            for j in range(2, 8):
                out_unit(U_CPOUT, "cpout", j)
            norm_sum(5)

            def glu(layer, n):
                first, stage = U_GLU[layer], f"glu{layer}"
                done = 2 * GLU_GROUPS * layer

                def up(j0, g, turn, per):
                    group(first, j0, stage, up_tags, turn, per, (0, 2, 1, 3), g)

                def down(j0, g, par, turn, per):
                    for h in range(2):
                        def tile(a):
                            pe.wait_ge(ghid_lo, g * 2 + (done + a + 1))
                        unit(first, j0 + h, m_hi, m_lo, (2 * par, 2 * par + 1), stage,
                             [("d", h, m) for m in range(4)], True, True, turn, per, use=g, wait_tile=tile)

                group(first, 0, stage, up_tags, 0, 0, (0, 2, 1, 3), 0, n)
                with pe.Fori(0, GLU_GROUPS // 2) as i:
                    up(4, i * 2 + 1, i, 12)
                    down(8, i * 2, 0, i, 12)
                    up(10, i * 2 + 2, i, 12)
                    down(14, i * 2 + 1, 1, i, 12)
                down(6 * GLU_GROUPS - 2, GLU_GROUPS - 1, 0, 0, 0)

            glu(0, 3)
            norm_sum(6)

            head_order = (1, 0, 2, 3)
            group(U_HGIN, 0, "hgin", up_tags, order=head_order, n=4)

            def core(n, units):
                L = len(LEVELS)
                pe.wait_ge(lf_ready, n + 1)
                pe.wait_ge(drained[4], before("hg", "lft", n))
                for t in range(TT):
                    mm = pe.transpose(ps[:, 4, t * P:(t + 1) * P], lf[:, t * P:(t + 1) * P], ident[:, :])
                mm.then_inc(filled[4], 1)
                units(0)
                pe.wait_ge(drained[2], nth("hgin", ("m", 2), n))
                pe.wait_ge(drained[5], before("hg", "vt", n))
                for t in range(TT):
                    mm = pe.transpose(ps[:, 5, t * P:(t + 1) * P], iT[:, t * P:(t + 1) * P], ident[:, :])
                mm.then_inc(filled[5], 1)
                pe.wait_ge(drained[4], nth("hg", "lft", n))
                pe.wait_ge(drained[6], before("hg", "cum", n))
                for t in range(TT):
                    mm = pe.matmul(ps[:, 6, t * P:(t + 1) * P], lfT[:, t * P:(t + 1) * P], tri[:, :], start=True, stop=True)
                mm.then_inc(filled[6], 1)
                units(1)
                pe.wait_ge(kend_ready, n + 1)
                pe.wait_ge(drained[4], before("hg", "ket", n))
                for t in range(3):
                    mm = pe.transpose(ps[:, 4, t * P:(t + 1) * P], kend[:, t * P:(t + 1) * P], ident[:, :])
                mm.then_inc(filled[4], 1)
                units(2)
                pe.wait_ge(drained[4], nth("hg", "ket", n))
                pe.wait_ge(drained[5], nth("hg", "vt", n))
                pe.wait_ge(drained[6], before("hg", "u", n))
                for t in range(3):
                    mm = pe.matmul(ps[:, 6, t * P:(t + 1) * P], keT[:, t * P:(t + 1) * P], vh[:, t * P:(t + 1) * P], start=True, stop=True)
                mm.then_inc(filled[6], 1)
                for i in range(L):
                    b = banks.bank("hg", ("s", i))
                    pe.wait_ge(drained[b], before("hg", ("s", i), n))
                    pe.wait_ge(qk_ready, n * (2 * L) + 2 * (i + 1))
                    for t in range(TT):
                        mm = pe.matmul(ps[:, b, t * 64:(t + 1) * 64], klev[:, i, t * P:(t + 1) * P],
                                       qlev[:, i, t * 64:(t + 1) * 64], start=True, stop=True)
                    mm.then_inc(filled[b], 1)
                b = banks.bank("hg", ("s", L))
                pe.wait_ge(drained[b], before("hg", ("s", L), n))
                for t in range(TT):
                    mm = pe.matmul(ps[:, b, t * P:(t + 1) * P], kk[:, t * P:(t + 1) * P], qh[:, t * P:(t + 1) * P],
                                   start=True, stop=True)
                mm.then_inc(filled[b], 1)
                units(3)
                pe.wait_ge(drained[4], before("hg", "o", n))
                pe.wait_ge(drained[b], nth("hg", ("s", L), n))
                pe.wait_ge(drained[5], nth("hg", ("s", L - 1), n))
                pe.wait_ge(state_ready, n * 3 + 3)
                pe.wait_ge(qb_ready, n + 1)
                for t in range(TT):
                    cols = slice(t * P, (t + 1) * P)
                    mm = pe.matmul(ps[:, 4, cols], vh[:, t * P:(t + 1) * P], score[:, cols], start=True, stop=t == 0)
                    if t:
                        mm = pe.matmul(ps[:, 4, cols], state[:, (t - 1) * P:t * P], qb[:, cols], start=False, stop=True)
                mm.then_inc(filled[4], 1)
                pe.wait_ge(hsq_ready, n + 1)
                pe.wait_ge(drained[6], before("hg", "sum", n))
                pe.matmul(ps[:, 6, :], ones[:, :], hsq[:, :], start=True, stop=True).then_inc(filled[6], 1)

            with pe.Fori(0, HG_HEADS - 1) as n:
                core(n, lambda j: unit(U_HGIN + 4, j, h_hi, h_lo, (2 * j, 2 * j + 1), "hgin", up_tags, j == 0, j == 3, n, 4,
                                       head_order, use=n + 1))

            def hgout(j):
                def tile(a):
                    pe.wait_ge(ho_lo, 2 * (j % 4) + a + 1)
                unit(U_HGOUT, j, m_hi, m_lo, (2 * (j % 4), 2 * (j % 4) + 1), "hgout",
                     [("h", j // 4, m) for m in range(4)], j % 4 == 0, j % 4 == 3, wait_tile=tile)

            core(HG_HEADS - 1, lambda j: hgout(j) if j < 3 else None)
            for j in range(3, 8):
                hgout(j)
            norm_sum(7)
            glu(1, 5)
            norm_sum(8)
            for k in range(KT):
                b = banks.bank("end", ("y", k))
                pe.wait_ge(y_ready, k + 1)
                pe.wait_ge(drained[b], before("end", ("y", k)))
                for t in range(TT):
                    mm = pe.transpose(ps[:, b, t * P:(t + 1) * P], yT[:, k % 2, t * P:(t + 1) * P], ident[:, :])
                mm.then_inc(filled[b], 1)

        @block.vector
        def _(dve):
            dve.memset(ones[:, :], 1.0).then_inc(set_up, 1)
            dve.memset(eps6[:, :], 1e-6).then_inc(set_up, 1)
            dve.memset(eps5[:, :], 1e-5).then_inc(set_up, 1)

            def col(name, k):
                return vecs[:, COL[name] + k:COL[name] + k + 1]

            def normed(i, rs_n, name, off=0):
                dve.wait_ge(rs_ready, rs_n)
                for k in range(KT + 1):
                    if k < KT:
                        if k >= 2:
                            dve.wait_ge(lo_ready, KT * i + k - 1)
                        dve.scalar_tensor_tensor(out=hf[:, k % 2, :], in0=xT[:, k, :], scalar=col(name, off + k),
                                                 in1=rs[:, :], op0=ALU.mult, op1=ALU.mult).then_inc(hf_ready, 1)
                    if k:
                        dve.wait_ge(hi_ready, KT * i + k)
                        dve.tensor_tensor(h_lo[:, k - 1, :], hf[:, (k - 1) % 2, :], h_hi[:, k - 1, :].bitcast(F32),
                                          ALU.subtract).then_inc(lo_ready, 1)

            def post_normed(i, rs_n, name, ready):
                dve.wait_ge(rs_ready, rs_n)
                for k in range(KT):
                    ready(k)
                    dve.scalar_tensor_tensor(out=acc[:, k, :], in0=acc[:, k, :], scalar=col(name, k), in1=rs[:, :],
                                             op0=ALU.mult, op1=ALU.mult).then_inc(post_step, 1)
                    dve.wait_ge(post_step, KT * i + k + 1)
                    dve.tensor_tensor(xT[:, k, :], xT[:, k, :], acc[:, k, :], ALU.add).then_inc(x_ready, 1)

            dve.wait_ge(filled[4], nth("start", "vec"))
            dve.tensor_copy(vecs[:, :], bank("start", "vec")[:, 0:N_VEC]).then_inc(drained[4], 1)
            dve.wait_ge(filled[5], nth("start", "taps"))
            dve.tensor_copy(taps[:, :, :], bank("start", "taps")[:, 0:4 * TAPS].rearrange("p (t j) -> p t j", j=4))\
                .then_inc(drained[5], 1)
            for k in range(0, KT, 2):
                dve.wait_ge(filled[k % 4], nth("start", ("x", k)))
                dve.tensor_copy(xT[:, k, :], bank("start", ("x", k))).then_inc(drained[k % 4], 1)
            dve.wait_ge(consts_in, 16 * 11)
            for i in range(2):
                dve.wait_ge(filled[6 + i], nth("start", f"rel{i}"))
                dve.tensor_tensor(relrow[:, i * 512:(i + 1) * 512], bank("start", f"rel{i}")[0:N_HEADS, :],
                                  lnmult[:, i * 512:(i + 1) * 512], ALU.add).then_inc(drained[6 + i], 1)
            for i in range(2):
                dve.wait_ge(filled[4 + i], nth("start", f"ws{i}"))
                dve.tensor_copy(wsT[:, 4 * i:4 * i + 4, :], bank("start", f"ws{i}").rearrange("p (g t) -> p g t", t=P))\
                    .then_inc(drained[4 + i], 1)
            dve.wait_ge(drained[4], nth("start", "vec"))
            normed(0, 1, "g_pre_mix")

            logits = [vecs[:, COL["hg_lb_logits_2"] + i * HG_HEADS:COL["hg_lb_logits_2"] + (i + 1) * HG_HEADS]
                      for i in range(2)]
            top, less, ex, tot, inv, p0, p1, lb = (lbt[:, i, :] for i in range(8))
            less1, ex1 = tot, inv
            dve.tensor_tensor(top, logits[0], logits[1], ALU.max).then_inc(lb_step, 1)
            dve.wait_ge(lb_step, 1)
            dve.tensor_tensor(less, logits[0], top, ALU.subtract).then_inc(lb_step, 1)
            dve.tensor_tensor(less1, logits[1], top, ALU.subtract).then_inc(lb_step, 1)
            dve.wait_ge(lb_exp, 2)
            dve.tensor_tensor(tot, ex, ex1, ALU.add).then_inc(lb_step, 1)
            dve.wait_ge(lb_step, 4)
            dve.reciprocal(top, tot).then_inc(lb_step, 1)
            dve.wait_ge(lb_step, 5)
            dve.tensor_tensor(p0, ex, top, ALU.mult).then_inc(lb_step, 1)
            dve.tensor_tensor(p1, ex1, top, ALU.mult).then_inc(lb_step, 1)
            dve.wait_ge(lb_step, 7)
            dve.tensor_tensor(lb, p0, p1, ALU.add).then_inc(lb_step, 1)
            dve.wait_ge(lb_step, 8)
            dve.tensor_tensor(hcol[:, :, 1], lb, p0, ALU.subtract).then_inc(lb_step, 1)
            dve.wait_ge(lb_step, 9)
            dve.tensor_scalar(hcol[:, :, 0], hcol[:, :, 1], -1.0, 1.0, ALU.mult, ALU.add).then_inc(lb_step, 1)
            dve.tensor_scalar(hcol[:, :, 2], hcol[:, :, 1], -1.0, None, ALU.add).then_inc(lb_step, 1)
            dve.tensor_copy(hcol[:, :, 3], vecs[:, COL["hg_gn_g_2"]:COL["hg_gn_g_2"] + HG_HEADS]).then_inc(lb_step, 1)
            dve.wait_ge(lb_step, 12)

            dve.wait_ge(filled[4], nth("zv", "mean"))
            for m in range(4):
                dve.scalar_tensor_tensor(out=gv[:, m, :], in0=bank("zv", "mean"), scalar=-1.0 / (4 * P), in1=gv[:, m, :],
                                         op0=ALU.mult, op1=ALU.add).then_inc(sgu_step, 1)
            dve.wait_ge(sgu_step, 4)
            dve.sem_inc(drained[4], 1)
            dve.wait_ge(rs_ready, 2)
            for m in range(4):
                dve.tensor_tensor(gv[:, m, :], gv[:, m, :], rs[:, :], ALU.mult).then_inc(sgu_step, 1)
                dve.wait_ge(sgu_step, 5 + m)
                dve.tensor_scalar(gv[:, m, :], gv[:, m, :], col("sgu_ln_g", m), col("sgu_ln_b", m), ALU.mult, ALU.add)\
                    .then_inc(sgu_y, 1)
            dve.wait_ge(sgu_in, 32)
            for j in range(4):
                dve.wait_ge(filled[4 + j], nth("sgu", ("mix", j)))
                dve.tensor_tensor(gv[:, j, :].rearrange("p (t s) -> p t s", s=P),
                                  bank("sgu", ("mix", j)).rearrange("p (t s) -> p t s", s=P),
                                  sgub[:, j, :].unsqueeze(1).broadcast_to([P, TT, P]), ALU.add).then_inc(drained[4 + j], 1)

            def sgu_out(p, u_count):
                dve.wait_ge(drained[3], u_count)
                dve.tensor_tensor(ug[:, :], ug[:, :], tile_of(gv, p), ALU.mult).then_inc(sg_ready, 1)
                dve.wait_ge(sg_hi, p + 1)
                dve.tensor_tensor(tile_of(m_lo, 4 + p), ug[:, :], tile_of(m_hi, 4 + p).bitcast(F32), ALU.subtract)\
                    .then_inc(sg_lo, 1)

            dve.wait_ge(drained[7], nth("sgu", ("mix", 3)))
            sgu_out(0, nth("qkv0", ("m", 3)))
            dve.wait_ge(btab_in, 16)

            def attend(p):
                def biased(i):
                    e, t = i // 4, i % 4
                    b = banks.bank("att", ("s", i))
                    dve.wait_ge(filled[b], nth("att", ("s", i), p))
                    tab = btab[:, 2 * p + e, (3 - t) * P:(3 - t) * P + SEQ]
                    if i >= 2:
                        dve.wait_ge(prob_ready, p * 8 + (i - 1))
                    dve.tensor_tensor_reduce(sbias[:, i % 2, :], ps[:, b, :], tab, 1.0, -3e38, ALU.add, ALU.max,
                                             amax[:, i:i + 1]).then_inc(drained[b], 1)
                    dve.wait_ge(drained[b], nth("att", ("s", i), p))
                    dve.tensor_scalar(nmax[:, i:i + 1], amax[:, i:i + 1], -1.0, None, ALU.mult).then_inc(neg_ready, 1)

                def normal(i):
                    dve.wait_ge(prob_ready, p * 8 + (i + 1))
                    dve.reciprocal(rden[:, i:i + 1], den[:, i:i + 1]).then_inc(den_inv, 1)
                    dve.wait_ge(den_inv, p * 8 + (i + 1))
                    dve.tensor_scalar(prob[:, i % 2, :], prob[:, i % 2, :], rden[:, i:i + 1], None, ALU.mult)\
                        .then_inc(probn_ready, 1)

                def turned(i):
                    dve.wait_ge(filled[6], nth("att", ("t", i), p))
                    if i == 4:
                        dve.wait_ge(filled[7], nth("att", ("o", 0), p))
                    t = i % 4
                    dve.tensor_copy(probT[:, :, t * P:(t + 1) * P], ps[:, 6, :].rearrange("p (k q) -> p k q", q=P))\
                        .then_inc(drained[6], 1)

                def low(e):
                    rows = slice(HEAD_DIM * e, HEAD_DIM * (e + 1))
                    dve.wait_ge(o_hi, p * 2 + (e + 1))
                    dve.tensor_tensor(tile_of(m_lo, p)[rows], ps[rows, 7, :], tile_of(m_hi, p)[rows].bitcast(F32),
                                      ALU.subtract).then_inc(drained[7], 1)

                biased(0)
                biased(1)
                normal(0)
                normal(1)
                turned(0)
                biased(2)
                turned(1)
                biased(3)
                normal(2)
                normal(3)
                turned(2)
                biased(4)
                turned(3)
                biased(5)
                normal(4)
                normal(5)
                low(0)
                turned(4)
                biased(6)
                turned(5)
                biased(7)
                normal(6)
                normal(7)
                turned(6)
                turned(7)
                low(1)

            for p in range(PAIRS - 1):
                attend(p)
                sgu_out(p + 1, nth("qkv", ("m", 3), p))
            attend(PAIRS - 1)

            for k in range(KT):
                b = banks.bank("wout", ("h", k // 4, k % 4))
                dve.wait_ge(filled[b], nth("wout", ("h", k // 4, k % 4)))
                dve.tensor_copy(acc[:, k, :], ps[:, b, :]).then_inc(drained[b], 1)
            post_normed(0, 3, "g_post_mix", lambda k: None)
            normed(1, 4, "g_pre_ffn")
            dve.memset(acc[:, :, :], 0.0).then_inc(set_up, 1)
            dve.wait_ge(set_up, 4)
            with dve.Fori(0, FFN_GROUPS) as g:
                for m in range(4):
                    dve.wait_ge(drained[m], nth("ffn", ("m", m), g))
                    dve.tensor_tensor(hid[:, m % 2, :], relu[:, m % 2, :], relu[:, m % 2, :], ALU.mult)\
                        .then_inc(hid_ready, 1)
                    dve.wait_ge(hid_ready, g * 4 + (m + 1))
                    dve.wait_ge(hid_hi, g * 4 + (m + 1))
                    dve.tensor_tensor(m_lo[:, m, :], hid[:, m % 2, :], m_hi[:, m, :].bitcast(F32), ALU.subtract)\
                        .then_inc(hid_lo, 1)
                for h in range(2):
                    for m in range(4):
                        dve.wait_ge(filled[4 + m], nth("ffn", ("d", h, m), g))
                        dve.tensor_tensor(acc[:, 4 * h + m, :], acc[:, 4 * h + m, :], ps[:, 4 + m, :], ALU.add)\
                            .then_inc(drained[4 + m], 1)
            post_normed(1, 5, "g_post_ffn", lambda k: dve.wait_ge(
                drained[4 + k % 4], nth("ffn", ("d", k // 4, k % 4), FFN_GROUPS - 1)))
            dve.memset(apad[:, :, 0:PAD], 0.0).then_inc(set_up, 1)
            dve.memset(upad[:, :, 0:POOL_PAD], 0.0).then_inc(set_up, 1)
            normed(2, 6, "norm_mix_g_2")

            dve.wait_ge(set_up, 6)

            def gated(j):
                g, i = j // 2, j % 2
                b = banks.bank("cpin", ("g", g, i))
                bg = banks.bank("cpin", ("g", g, 2 + i))
                dve.wait_ge(filled[b], nth("cpin", ("g", g, i)))
                dve.wait_ge(drained[bg], nth("cpin", ("g", g, 2 + i)))
                dve.tensor_tensor(apad[:, j, PAD:], csig[:, i, :], ps[:, b, :], ALU.mult).then_inc(drained[b], 1)
                dve.wait_ge(drained[b], nth("cpin", ("g", g, i)))

            def convolve(first):
                with dve.Fori(0, 2) as r:
                    j = r + first
                    dve.tensor_copy(ctap[:, 0:TAPS], taps[:, :, bass.ds(j, 1)].squeeze(2)).then_inc(ctap_ready, 1)
                    dve.tensor_copy(ctap[:, TAPS:TAPS + 1], vecs[:, bass.ds(j + COL["cp_dw_b_2"], 1)]).then_inc(ctap_ready, 1)
                    dve.wait_ge(ctap_ready, j * 2 + 2)
                    c = tile_of(conv, j)
                    for i in range(TAPS):
                        a = tile_of(apad, j)[:, i:i + SEQ]
                        if i == 0:
                            dve.tensor_scalar(c, a, ctap[:, 0:1], ctap[:, TAPS:TAPS + 1], ALU.mult, ALU.add)\
                                .then_inc(tap_done, 1)
                        else:
                            dve.wait_ge(tap_done, j * TAPS + i)
                            dve.scalar_tensor_tensor(out=c, in0=a, scalar=ctap[:, i:i + 1], in1=c, op0=ALU.mult,
                                                     op1=ALU.add).then_inc(tap_done, 1)
                    dve.wait_ge(tap_done, j * TAPS + TAPS)

            gated(0)
            gated(1)
            convolve(0)
            gated(2)
            gated(3)
            convolve(2)
            dve.wait_ge(filled[4], nth("cpin", "mean"))
            for j in range(4):
                dve.scalar_tensor_tensor(out=conv[:, j, :], in0=bank("cpin", "mean"), scalar=-1.0 / (4 * P),
                                         in1=conv[:, j, :], op0=ALU.mult, op1=ALU.add).then_inc(cln_step, 1)
            dve.wait_ge(cln_step, 4)
            dve.sem_inc(drained[4], 1)
            dve.wait_ge(rs_ready, 7)
            for j in range(4):
                dve.tensor_tensor(conv[:, j, :], conv[:, j, :], rs[:, :], ALU.mult).then_inc(cln_y, 1)
            for j in range(4):
                dve.wait_ge(cs_hi, j + 1)
                dve.tensor_tensor(m_lo[:, j, :], csq[:, j, :], m_hi[:, j, :].bitcast(F32), ALU.subtract).then_inc(cs_lo, 1)

            def add_out(stage):
                for k in range(KT):
                    b = banks.bank(stage, ("h", k // 4, k % 4))
                    dve.wait_ge(filled[b], nth(stage, ("h", k // 4, k % 4)))
                    dve.tensor_tensor(xT[:, k, :], xT[:, k, :], ps[:, b, :], ALU.add).then_inc(drained[b], 1)

            add_out("cpout")
            normed(3, 8, "norm_ffn_g_2")

            def glu(layer):
                stage = f"glu{layer}"
                done = 2 * GLU_GROUPS * layer

                def up(g, par):
                    for i in range(2):
                        dve.wait_ge(drained[i], nth(stage, ("m", i), g))
                        dve.wait_ge(filled[2 + i], nth(stage, ("m", 2 + i), g))
                        if not isinstance(g, int):
                            dve.wait_ge(ghid_lo, g * 2 + (done + i - 1))
                        dve.tensor_tensor(ghid[:, i, :], silu[:, i, :], ps[:, 2 + i, :], ALU.mult)\
                            .then_inc(drained[2 + i], 1)
                    for i in range(2):
                        dve.wait_ge(ghid_hi, g * 2 + (done + i + 1))
                        dve.tensor_tensor(m_lo[:, 2 * par + i, :], ghid[:, i, :], m_hi[:, 2 * par + i, :].bitcast(F32),
                                          ALU.subtract).then_inc(ghid_lo, 1)

                def down(g):
                    for h in range(2):
                        for m in range(4):
                            dve.wait_ge(filled[4 + m], nth(stage, ("d", h, m), g))
                            dve.tensor_tensor(xT[:, 4 * h + m, :], xT[:, 4 * h + m, :], ps[:, 4 + m, :], ALU.add)\
                                .then_inc(drained[4 + m], 1)

                up(0, 0)
                with dve.Fori(0, GLU_GROUPS // 2) as i:
                    up(i * 2 + 1, 1)
                    down(i * 2)
                    up(i * 2 + 2, 0)
                    down(i * 2 + 1)
                down(GLU_GROUPS - 1)

            glu(0)
            dve.memset(score[:, :], 0.0).then_inc(set_up, 1)
            dve.memset(klev[:, :, :], 0.0).then_inc(set_up, 1)
            dve.wait_ge(set_up, 8)
            normed(4, 9, "norm_mix_g_2", KT)

            def f_cols(n):
                dve.tensor_copy(fcol[:, :], tile_of(hcol, n))\
                    .then_inc(fcol_ready, 1)

            f_cols(0)

            def core(n, last=False):
                L = len(LEVELS)
                dve.wait_ge(drained[1], nth("hgin", ("m", 1), n))
                dve.wait_ge(fcol_ready, n + 1)
                dve.tensor_scalar(kk[:, :], sgf[:, :], fcol[:, 2:3], fcol[:, 0:1], ALU.mult, ALU.add).then_inc(kk_ready, 1)
                dve.tensor_copy(gcol[:, :], fcol[:, 3:4]).then_inc(gcol_ready, 1)
                dve.wait_ge(drained[3], nth("hgin", ("m", 3), n))
                dve.wait_ge(sgg_ready, n + 1)
                dve.tensor_tensor(gs[:, :], gT[:, :], sgg[:, :], ALU.mult).then_inc(gs_ready, 1)
                if not last:
                    dve.wait_ge(lf_ready, n + 1)
                    dve.wait_ge(kk_ready, n + 1)
                    dve.wait_ge(gcol_ready, n + 1)
                    f_cols(n + 1)
                dve.wait_ge(drained[6], nth("hg", "cum", n))
                win = cum[:, :].rearrange("p (w t) -> p w t", t=WIN)
                dve.tensor_tensor(dend[:, :].rearrange("p (w t) -> p w t", t=WIN),
                                  win[:, :, WIN - 1:WIN].broadcast_to([P, TT, WIN]), win, ALU.subtract)\
                    .then_inc(dend_ready, 1)

                def diffs(i):
                    m = LEVELS[i]
                    c = levels(cum[:, :], m)
                    d = levels(dlev[:, i % 2, :], m)
                    mid = c[:, :, 0, m - 1:m].broadcast_to([P, SEQ // (2 * m), m])
                    if i >= 2:
                        dve.wait_ge(elev_ready, n * L + (i - 1))
                    dve.tensor_tensor(d[:, :, 1, :], c[:, :, 1, :], mid, ALU.subtract).then_inc(dlev_ready, 1)
                    dve.tensor_tensor(d[:, :, 0, :], mid, c[:, :, 0, :], ALU.subtract).then_inc(dlev_ready, 1)

                def decayed(i):
                    m = LEVELS[i]
                    e = levels(elev[:, i % 2, :], m)
                    dve.wait_ge(elev_ready, n * L + (i + 1))
                    dve.tensor_tensor(qlev[:, i, :].rearrange("p (n m) -> p n m", m=m), levels(qh[:, :], m)[:, :, 1, :],
                                      e[:, :, 1, :], ALU.mult).then_inc(qk_ready, 1)
                    dve.tensor_tensor(levels(klev[:, i, :], m)[:, :, 0, :], levels(kk[:, :], m)[:, :, 0, :],
                                      e[:, :, 0, :], ALU.mult).then_inc(qk_ready, 1)

                diffs(0)
                dve.wait_ge(drained[0], nth("hgin", ("m", 0), n))
                dve.wait_ge(kk_ready, n + 1)
                dve.wait_ge(e0_ready, n + 1)
                dve.tensor_tensor(qb[:, :], qh[:, :], e0[:, :], ALU.mult).then_inc(qb_ready, 1)
                dve.wait_ge(eend_ready, n + 1)
                dve.tensor_tensor(kend[:, :], kk[:, :], dend[:, :], ALU.mult).then_inc(kend_ready, 1)
                diffs(1)
                for i in range(L):
                    decayed(i)
                    if i + 2 < L:
                        diffs(i + 2)
                dve.wait_ge(filled[6], nth("hg", "u", n))
                for w_ in range(3):
                    u = ps[:, 6, w_ * P:(w_ + 1) * P]
                    if w_ == 0:
                        dve.tensor_copy(state[:, 0:P], u).then_inc(state_ready, 1)
                    else:
                        dve.wait_ge(state_ready, n * 3 + w_)
                        e = e0[:, w_ * WIN + WIN - 1:w_ * WIN + WIN]
                        dve.scalar_tensor_tensor(out=state[:, w_ * P:(w_ + 1) * P], in0=state[:, (w_ - 1) * P:w_ * P], scalar=e, in1=u,
                                                 op0=ALU.mult, op1=ALU.add).then_inc(state_ready, 1)
                dve.wait_ge(state_ready, n * 3 + 3)
                dve.sem_inc(drained[6], 1)
                for i in range(L):
                    m = LEVELS[i]
                    b = banks.bank("hg", ("s", i))
                    if i:
                        dve.wait_ge(drained[banks.bank("hg", ("s", i - 1))], nth("hg", ("s", i - 1), n))
                    dve.wait_ge(filled[b], nth("hg", ("s", i), n))
                    dve.sem_inc(placing, 1)
                    dst = score[:, :].rearrange("p (w n two m) -> p w n two m", w=TT, two=2, m=m)[:, :, :, 1, :]
                    src = ps[:, b, 0:256].rearrange("p (w n m) -> p w n m", w=TT, m=m)
                    msk = mask[:, i, :].rearrange("p (n m) -> p n m", m=m).unsqueeze(1).broadcast_to([P, TT, 64 // m, m])
                    dve.copy_predicated(dst, msk, src).then_inc(drained[b], 1)
                b = banks.bank("hg", ("s", L))
                dve.wait_ge(drained[banks.bank("hg", ("s", L - 1))], nth("hg", ("s", L - 1), n))
                dve.wait_ge(filled[b], nth("hg", ("s", L), n))
                dve.sem_inc(placing, 1)
                dve.copy_predicated(score[:, :].rearrange("p (w t) -> p w t", t=P),
                                    diag[:, :].unsqueeze(1).broadcast_to([P, TT, P]),
                                    ps[:, b, :].rearrange("p (w t) -> p w t", t=P)).then_inc(drained[b], 1)
                dve.wait_ge(hrs_ready, n + 1)
                dve.wait_ge(gcol_ready, n + 1)
                dve.wait_ge(gs_ready, n + 1)
                dve.scalar_tensor_tensor(out=hn[:, :], in0=bank("hg", "o"), scalar=gcol[:, :], in1=hrs[:, :],
                                         op0=ALU.mult, op1=ALU.mult).then_inc(drained[4], 1)
                dve.wait_ge(drained[4], nth("hg", "o", n))
                dve.tensor_tensor(ho[:, :], hn[:, :], gs[:, :], ALU.mult).then_inc(ho_ready, 1)
                dve.wait_ge(ho_hi, n + 1)
                dve.tensor_tensor(tile_of(m_lo, n), ho[:, :], tile_of(m_hi, n).bitcast(F32), ALU.subtract).then_inc(ho_lo, 1)

            with dve.Fori(0, HG_HEADS - 1) as n:
                core(n)
            core(HG_HEADS - 1, True)
            add_out("hgout")
            normed(5, 10, "norm_ffn_g_2", KT)
            glu(1)
            dve.wait_ge(rs_ready, 11)
            for k in range(KT + 2):
                if k < KT:
                    if k >= 2:
                        dve.wait_ge(filled[banks.bank("end", ("y", k - 2))], nth("end", ("y", k - 2)))
                    dve.scalar_tensor_tensor(out=yT[:, k % 2, :], in0=xT[:, k, :], scalar=col("final_g_2", k),
                                             in1=rs[:, :], op0=ALU.mult, op1=ALU.mult).then_inc(y_ready, 1)
                if k % 2 and k >= 1 and k - 1 < KT:
                    b = banks.bank("end", ("y", k - 1))
                    dve.wait_ge(filled[b], nth("end", ("y", k - 1)))
                    dve.tensor_copy(otok[:, :, (k - 1) * P:k * P], ps[:, b, :].rearrange("p (t f) -> p t f", f=P))\
                        .then_inc(drained[b], 1)


def constants():
    dist = np.arange(1024) - (SEQ - 1)
    n = np.abs(dist)
    half = N_BUCKETS // 2
    exact = half // 2
    large = exact + (np.log(np.maximum(n, 1).astype(np.float32) / np.float32(exact))
                     / np.float32(math.log(REL_MAX / exact)) * np.float32(half - exact)).astype(np.int32)
    bucket = np.where(dist > 0, half, 0) + np.where(n < exact, n, np.minimum(large, half - 1))
    onehot = (bucket[None, :] == np.arange(N_BUCKETS)[:, None]).astype(np.float32)
    seen = sum(((n % dil == 0) & (n <= window // 2)).astype(np.int32) for window, dil in BRANCHES)
    lnmult = np.where(seen > 0, np.log(np.maximum(seen, 1)), -1e30).astype(np.float32)
    t = np.arange(P)
    mask = np.zeros((P, len(LEVELS), 64), np.int32)
    for i, m in enumerate(LEVELS):
        later = (np.arange(64) // m) * (2 * m) + m + np.arange(64) % m
        mask[:, i, :] = (t[:, None] // (2 * m) == later[None, :] // (2 * m)) & (t[:, None] % (2 * m) < m)
    inv = np.stack([1.0 / np.minimum(np.arange(POOL_PAD) + 1, w) for w in POOL_WINDOWS]).astype(np.float32)
    return {
        "ident": np.eye(P, dtype=np.float32),
        "tri": (t[:, None] <= t[None, :]).astype(np.float32),
        "onehot": onehot,
        "lnmult": np.ascontiguousarray(np.broadcast_to(lnmult, (N_HEADS, 1024))),
        "poolinv": np.ascontiguousarray(np.broadcast_to(inv, (P,) + inv.shape)),
        "mask": mask,
        "diag": np.eye(P, dtype=np.int32),
    }


WEIGHTS = ("w_in", "w_out", "w_ff1", "w_ff2", "cp_w_in_2", "cp_w_out_2", "hg_w_in_2", "hg_w_out_2",
           "ffn_w1_2", "ffn_w3_2", "ffn_w2_2")


def kernel(**inputs):
    import concourse.bacc as bacc
    from concourse.bass_utils import run_bass_kernel_spmd

    nc = bacc.Bacc("TRN2", target_bir_lowering=False, num_devices=1)
    arrays = {}

    def take(name, a):
        arrays[name] = np.ascontiguousarray(a)
        return nc.dram_tensor(name, arrays[name].shape, mybir.dt.from_np(arrays[name].dtype), kind="ExternalInput").ap()

    get = {k: np.asarray(v) for k, v in inputs.items()}
    x = take("in_x", get["x"][0])
    w = {}
    for name in WEIGHTS:
        a = get[name]
        w[name] = take("in_" + name, a if name.startswith("ffn_") else a[0])
    vec = take("in_vectors", np.concatenate([get[name].reshape(-1, P) for name, _ in VECTORS]))
    rest = [take("in_" + name, get[name][0]) for name in ("sgu_w", "sgu_b")]
    rest.append(take("in_rel_bias", get["rel_bias"]))
    rest += [take("in_" + name, get[name][0]) for name in ("cp_dw_w_2", "cp_pool_w_2")]
    c = constants()
    rest += [take("const_" + name, c[name]) for name in ("ident", "tri", "onehot", "lnmult", "poolinv", "mask", "diag")]
    scratch = nc.dram_tensor("bias_rows", (N_HEADS, P, 1025), F32, kind="Internal").ap()
    out = nc.dram_tensor("out_0", (SEQ, D), F32, kind="ExternalOutput").ap()
    build(nc, x, w, vec, *rest, scratch, out)
    r = run_bass_kernel_spmd(nc, [arrays], core_ids=[0])
    return r.results[0]["out_0"].reshape(1, SEQ, D)
```

```python
import math
from contextlib import ExitStack

import numpy as np
import concourse.bass as bass
from concourse import mybir

ALU = mybir.AluOpType
ACT = mybir.ActivationFunctionType
F32 = mybir.dt.float32
F32R = mybir.dt.float32r
I32 = mybir.dt.int32

P = 128
SEQ = 512
D = 1024
KT = D // P
TT = SEQ // P
HEAD_DIM = 64
D_ATTN = D // 2
PAIRS = D_ATTN // P
N_HEADS = D_ATTN // HEAD_DIM
SGU_TILES = (D - D_ATTN) // P
D_FF = 4 * D
D_FF_2 = -(-8 * D // (3 * 256)) * 256
TAPS = 31
PAD = TAPS - 1
POOL_WINDOWS = (2, 4, 8, 16)
POOL_PAD = 16
HG_HEADS = D // P
WIN = 128
LEVELS = [64, 32, 16, 8, 4, 2, 1]
N_BUCKETS = 32
REL_MAX = 1024
BRANCHES = ((128, 1), (512, 4), (2048, 16))
SKEW = SEQ + SEQ - P
LOG_TABLES = "natural_log_exp_and_others"

RING = 4
COLS = 512
AHEAD = 2

FFN_GROUPS = D_FF // COLS
GLU_GROUPS = D_FF_2 // 256

U_ZV = 0
U_QKV = U_ZV + 4
U_WOUT = U_QKV + 4 * PAIRS
U_FFN = U_WOUT + 8
U_CPIN = U_FFN + 8 * FFN_GROUPS
U_CPOUT = U_CPIN + 12
U_GLU = [U_CPOUT + 8, 0]
U_HGIN = U_GLU[0] + 6 * GLU_GROUPS
U_HGOUT = U_HGIN + 4 * HG_HEADS
U_GLU[1] = U_HGOUT + 8
UNITS = U_GLU[1] + 6 * GLU_GROUPS

VECTORS = (("g_pre_mix", 8), ("g_post_mix", 8), ("g_pre_ffn", 8), ("g_post_ffn", 8),
           ("norm_mix_g_2", 16), ("norm_ffn_g_2", 16), ("final_g_2", 8), ("sgu_ln_g", 4),
           ("sgu_ln_b", 4), ("cp_dw_b_2", 4), ("cp_ln_g_2", 4), ("cp_ln_b_2", 4),
           ("cp_pool_scale_2", 4), ("hg_gn_g_2", 8), ("hg_lb_logits_2", 16))
COL = {}
for _name, _n in VECTORS:
    COL[_name] = sum(n for _, n in VECTORS[:len(COL)])
N_VEC = sum(n for _, n in VECTORS)


class Banks:

    def __init__(self):
        self.count = [0] * 8
        self.first = {}
        self.per = {}

    def stage(self, name, uses, repeats=1):
        n = [0] * 8
        for tag, b in uses:
            n[b] += 1
            self.first[name, tag] = (b, self.count[b] + n[b])
        for tag, b in uses:
            self.per[name, tag] = n[b]
        for b in range(8):
            self.count[b] += n[b] * repeats

    def bank(self, name, tag):
        return self.first[name, tag][0]

    def nth(self, name, tag, turn=0):
        k = self.first[name, tag][1]
        return k if isinstance(turn, int) and turn == 0 else turn * self.per[name, tag] + k

    def before(self, name, tag, turn=0):
        return self.nth(name, tag, turn) - 1


def bank_plan():
    b = Banks()
    up = [(("m", m), m) for m in range(4)]
    b.stage("start", [("vec", 4)] + [(("h", k), k) for k in range(KT)])
    b.stage("zv", up)
    b.stage("small", [("taps", 5), ("rel0", 6), ("rel1", 7), ("ws0", 4), ("ws1", 5)])
    b.stage("x", [(("x", k), 4 + k % 4) for k in range(KT)])
    b.stage("zvnorm", [("mean", 4), ("var", 5)])
    b.stage("qkv0", up)
    b.stage("sgu", [(("vt", j), 4 + j) for j in range(4)] + [(("mix", j), 4 + j) for j in range(4)])
    b.stage("qkv", up, PAIRS - 1)
    b.stage("att", [("vtok", 6)] + [(("s", i), 4 + i % 2) for i in range(8)]
            + [(("t", i), 6) for i in range(8)] + [(("o", e), 7) for e in range(2)] + [("oT", 7)], PAIRS)
    out = [(("h", h, m), 4 * h + m) for h in range(2) for m in range(4)]
    b.stage("wout", out)
    b.stage("norm1", [("sum", 0)])
    b.stage("norm2", [("sum", 3)])
    down = [(("d", h, m), 4 + m) for h in range(2) for m in range(4)]
    b.stage("ffn0", [(("m", m), 4 + m) for m in range(4)])
    b.stage("ffnup", up, FFN_GROUPS - 1)
    b.stage("ffndown", down, FFN_GROUPS)
    b.stage("norm3", [("sum", 0)])
    b.stage("norm4", [("sum", 4)])
    b.stage("cpin", [(("g", 0, m), m) for m in range(4)] + [(("g", 2, m), 4 + m) for m in range(4)]
            + [(("g", 1, m), m) for m in range(4)] + [("conv", 4), ("mean", 5)]
            + [(("pool", j), 6 + j % 2) for j in range(4)] + [("var", 4)])
    b.stage("cpout", out)
    b.stage("norm5", [("sum", 4)])
    b.stage("glu0", up + down, GLU_GROUPS)
    b.stage("norm6", [("sum", 4)])
    b.stage("hgin", up, HG_HEADS)
    b.stage("hg", [("vt", 5), ("ket", 4), ("u", 6)]
            + [(("s", i), (5, 4, 7)[i % 3]) for i in range(len(LEVELS) + 1)] + [("o", 6), ("sum", 4)], HG_HEADS)
    b.stage("hgout", out)
    b.stage("norm7", [("sum", 4)])
    b.stage("glu1", up + down, GLU_GROUPS)
    b.stage("end", [("sum", 7)] + [(("y", t, h), 4 * h + t) for h in range(2) for t in range(TT)])
    return b


def build(nc, x, w, vec, sgu_w, sgu_b, rel_bias, dw_w, pool_w, ident_c, onehot_c, lnmult_c,
          poolinv_c, mask_c, diag_c, scratch, out):
    banks = bank_plan()
    nth, before = banks.nth, banks.before

    with ExitStack() as ctx:
        def sb(name, shape, dt=F32, scope=ctx):
            return scope.enter_context(nc.sbuf_tensor(name, shape, dt))

        def sem(name):
            return ctx.enter_context(nc.semaphore(name))

        raw = sb("raw", [P, RING, 2, COLS])
        whi = sb("whi", [P, RING, 2, COLS], F32R)
        wlo = sb("wlo", [P, RING, 2, COLS], F32R)
        xT = sb("xT", [P, KT, SEQ])
        h_hi = sb("h_hi", [P, KT, SEQ], F32R)
        h_lo = sb("h_lo", [P, KT, SEQ], F32R)
        m_hi = sb("m_hi", [P, KT, SEQ], F32R)
        m_lo = sb("m_lo", [P, KT, SEQ], F32R)
        ident = sb("ident", [P, P])
        ones = sb("ones", [P, P])
        vecs = sb("vecs", [P, N_VEC])
        taps = sb("taps", [P, TAPS, 4])
        eps6 = sb("eps6", [P, 1])
        eps5 = sb("eps5", [P, 1])
        lbt = sb("lbt", [P, 8, HG_HEADS])
        hcol = sb("hcol", [P, HG_HEADS, 4])
        mask = sb("mask", [P, len(LEVELS), 64], I32)
        diag = sb("diag", [P, P], I32)
        poolinv = sb("poolinv", [P, 4, POOL_PAD])
        rs = sb("rs", [P, SEQ])
        sq = sb("sq", [P, 2, SEQ])
        ss = sb("ss", [P, SEQ])

        with ExitStack() as s:
            xin = sb("xin", [P, TT, D], scope=s)
            vrows = sb("vrows", [N_VEC, P], scope=s)
            trows = sb("trows", [TAPS * 4, P], scope=s)
            relb = sb("relb", [N_BUCKETS, N_HEADS], scope=s)
            onehot = sb("onehot", [N_BUCKETS, 1024], scope=s)
            lnmult = sb("lnmult", [N_HEADS, 1024], scope=s)
            relrow = sb("relrow", [N_HEADS, 1024], scope=s)
            wsin = sb("wsin", [P, 8, P], scope=s)
            xsq = sb("xsq", [P, D], scope=s)
            xss = sb("xss", [P, TT], scope=s)
            xrs = sb("xrs", [P, TT], scope=s)
            xdiag = sb("xdiag", [P, TT, P], scope=s)
        with ExitStack() as s:
            btab = sb("btab", [P, N_HEADS, SKEW], scope=s)
            k_lo = sb("k_lo", [P, SEQ], F32R, scope=s)
            vT = sb("vT", [P, SEQ], scope=s)
            ug = sb("ug", [P, SEQ], scope=s)
            with ExitStack() as before_pairs:
                sgu_vt = sb("sgu_vt", [P, TT, SEQ], scope=before_pairs)
                wsT = sb("wsT", [P, 8, P], scope=before_pairs)
            sbias = sb("sbias", [P, 2, SEQ], scope=s)
            prob = sbias
            probT = sb("probT", [P, 2, SEQ], scope=s)
            vtok = sb("vtok", [P, SEQ], scope=s)
            onorm = sb("onorm", [P, TT, P], scope=s)
            q_parts = sb("q_parts", [P, 2, SEQ], F32R, scope=s)
            k_his = sb("k_his", [P, 2, SEQ], F32R, scope=s)
            gsum = ug
            gv = sb("gv", [P, 4, SEQ], scope=s)
            sgub = sb("sgub", [P, 4, P], scope=s)
            amax = sb("amax", [P, 8], scope=s)
            nmax = sb("nmax", [P, 8], scope=s)
            den = sb("den", [P, 8], scope=s)
            rden = sb("rden", [P, 8], scope=s)
        with ExitStack() as s:
            acc = sb("acc", [P, KT, SEQ], scope=s)
            relu = sb("relu", [P, 2, SEQ], scope=s)
            hid = sb("hid", [P, 2, SEQ], scope=s)
        with ExitStack() as s:
            apad = sb("apad", [P, 4, PAD + SEQ], scope=s)
            conv = sb("conv", [P, 4, SEQ], scope=s)
            csig = sb("csig", [P, 2, SEQ], scope=s)
            odd = sb("odd", [P, SEQ], scope=s)
            csum = sb("csum", [P, SEQ], scope=s)
            upad = sb("upad", [P, 4, POOL_PAD + SEQ], scope=s)
            late = sb("late", [P, 8, SEQ], scope=s)
            wsum = sb("wsum", [P, 2, POOL_PAD + SEQ], scope=s)
            pmean = sb("pmean", [P, SEQ], scope=s)
            pdiff = sb("pdiff", [P, 4, SEQ], scope=s)
            poolw = sb("poolw", [P, 4, P], scope=s)
            crs = sb("crs", [P, SEQ], scope=s)
        tapdiag = late[:, :, :].rearrange("p a (b c) -> p (a b) c", c=P)
        csq, pout = late[:, 0:4, :], late[:, 4:8, :]
        with ExitStack() as s:
            gate = sb("gate", [P, 2, SEQ], scope=s)
            silu = sb("silu", [P, 2, SEQ], scope=s)
            ghid = sb("ghid", [P, 2, SEQ], scope=s)
        with ExitStack() as s:
            sgf = sb("sgf", [P, SEQ], scope=s)
            sgg = sb("sgg", [P, SEQ], scope=s)
            gT = sb("gT", [P, SEQ], scope=s)
            gs = sb("gs", [P, SEQ], scope=s)
            qh = sb("qh", [P, SEQ], scope=s)
            kk = sb("kk", [P, SEQ], scope=s)
            iT = sb("iT", [P, SEQ], scope=s)
            lf = sb("lf", [P, SEQ], scope=s)
            vh = sb("vh", [P, SEQ], scope=s)
            cum = sb("cum", [P, SEQ], scope=s)
            e0 = sb("e0", [P, SEQ], scope=s)
            qb = sb("qb", [P, SEQ], scope=s)
            dend = sb("dend", [P, SEQ], scope=s)
            kend = dend
            keT = sb("keT", [P, 3 * P], scope=s)
            state = sb("state", [P, 3 * P], scope=s)
            dlev = sb("dlev", [P, 2, SEQ], scope=s)
            elev = sb("elev", [P, 2, SEQ], scope=s)
            qlev = sb("qlev", [P, len(LEVELS), SEQ // 2], scope=s)
            klev = sb("klev", [P, len(LEVELS), SEQ], scope=s)
            score = sb("score", [P, SEQ], scope=s)
            hsq = sb("hsq", [P, SEQ], scope=s)
            hln = sb("hln", [P, SEQ], scope=s)
            hrs = hln
            hn = ho = hsq
            fcol = sb("fcol", [P, 4], scope=s)
            gcol = sb("gcol", [P, 1], scope=s)
        with ExitStack() as s:
            yT = sb("yT", [P, KT, SEQ], scope=s)
            otok = sb("otok", [P, TT, D], scope=s)
            yrs = sb("yrs", [P, TT], scope=s)

        ps = ctx.enter_context(nc.psum_tensor("ps", [P, 8, 512], F32))

        def bank(stage, tag):
            return ps[:, banks.bank(stage, tag), :]

        filled = [sem(f"filled{b}") for b in range(8)]
        drained = [sem(f"drained{b}") for b in range(8)]
        x_in = [sem(f"x_in{t}") for t in range(TT)]
        gains_in = sem("gains_in")
        small_in = sem("small_in")
        consts_in = sem("consts_in")
        xss_ready = sem("xss_ready")
        xrs_ready = sem("xrs_ready")
        xdiag_ready = sem("xdiag_ready")
        sgu_in = sem("sgu_in")
        poolw_in = sem("poolw_in")
        rel_out = sem("rel_out")
        btab_in = sem("btab_in")
        unit_in = [sem(f"unit_in{i}") for i in range(RING)]
        unit_hi = sem("unit_hi")
        unit_lo = sem("unit_lo")
        unit_begun = sem("unit_begun")
        set_up = sem("set_up")
        lb_step = sem("lb_step")
        lb_exp = sem("lb_exp")
        sq_ready = sem("sq_ready")
        sq_used = sem("sq_used")
        rs_ready = sem("rs_ready")
        hi_ready = sem("hi_ready")
        lo_ready = sem("lo_ready")
        post_step = sem("post_step")
        x_ready = sem("x_ready")
        gelu_v = sem("gelu_v")
        sgu_step = sem("sgu_step")
        sgu_sq = sem("sgu_sq")
        gsum_step = sem("gsum_step")
        csum_step = sem("csum_step")
        sgu_y = sem("sgu_y")
        ug_ready = sem("ug_ready")
        sg_ready = sem("sg_ready")
        sg_hi = sem("sg_hi")
        sg_lo = sem("sg_lo")
        neg_ready = sem("neg_ready")
        qk_hi = sem("qk_hi")
        qk_lo = sem("qk_lo")
        prob_ready = sem("prob_ready")
        den_inv = sem("den_inv")
        onorm_ready = sem("onorm_ready")
        o_hi = sem("o_hi")
        hid_ready = sem("hid_ready")
        hid_hi = sem("hid_hi")
        hid_lo = sem("hid_lo")
        csig_ready = sem("csig_ready")
        apad_ready = sem("apad_ready")
        tapdiag_ready = sem("tapdiag_ready")
        conv_ready = sem("conv_ready")
        crs_ready = sem("crs_ready")
        tap_done = [sem(f"tap_done{j}") for j in range(3)]
        odd_done = sem("odd_done")
        win_step = sem("win_step")
        pdiff_ready = sem("pdiff_ready")
        pout_ready = sem("pout_ready")
        pout_hi = sem("pout_hi")
        pout_lo = sem("pout_lo")
        cln_step = sem("cln_step")
        cln_sq = sem("cln_sq")
        cln_y = sem("cln_y")
        cs_ready = sem("cs_ready")
        cs_hi = sem("cs_hi")
        cs_lo = sem("cs_lo")
        gate_a = sem("gate_a")
        gate_b = sem("gate_b")
        silu_ready = sem("silu_ready")
        ghid_ready = sem("ghid_ready")
        ghid_hi = sem("ghid_hi")
        ghid_lo = sem("ghid_lo")
        fcol_ready = sem("fcol_ready")
        gcol_ready = sem("gcol_ready")
        f_ready = sem("f_ready")
        g_ready = sem("g_ready")
        sgf_ready = sem("sgf_ready")
        sgg_ready = sem("sgg_ready")
        lf_ready = sem("lf_ready")
        cum_ready = sem("cum_ready")
        kk_ready = sem("kk_ready")
        gs_ready = sem("gs_ready")
        e0_ready = sem("e0_ready")
        dend_ready = sem("dend_ready")
        eend_ready = sem("eend_ready")
        kend_ready = sem("kend_ready")
        qb_ready = sem("qb_ready")
        dlev_ready = sem("dlev_ready")
        elev_ready = sem("elev_ready")
        qk_ready = sem("qk_ready")
        state_ready = sem("state_ready")
        placing = sem("placing")
        hsq_ready = sem("hsq_ready")
        hln_ready = sem("hln_ready")
        hrs_ready = sem("hrs_ready")
        ho_ready = sem("ho_ready")
        ho_hi = sem("ho_hi")
        ho_lo = sem("ho_lo")
        y_ready = sem("y_ready")
        yrs_ready = sem("yrs_ready")
        out_done = sem("out_done")

        def levels(t, m):
            return t.rearrange("p (n two m) -> p n two m", two=2, m=m)

        def own_rows(e):
            return slice(HEAD_DIM * e, HEAD_DIM * (e + 1))

        def tile_of(t, p):
            return t[:, p, :] if isinstance(p, int) else t[:, bass.ds(p, 1), :].squeeze(1)

        block = ctx.enter_context(nc.Block())

        @block.sync
        def _(sp):
            for t in range(TT):
                sp.dma_start(xin[:, t, :], x[t * P:(t + 1) * P, :]).then_inc(x_in[t], 16)
                if t == 0:
                    sp.dma_start(ident[:, :], ident_c).then_inc(gains_in, 16)
                    sp.dma_start(vrows[:, :], vec).then_inc(gains_in, 16)

            def load(first, j, halves, turn=0, per=0):
                u = first + j
                if u >= RING:
                    sp.wait_ge(unit_lo, turn * per + (u - RING + 1))
                for a, src in enumerate(halves):
                    dst = raw[:, u % RING, a, :]
                    if len(src.shape) == 3:
                        dst = dst.rearrange("p (b c) -> p b c", b=src.shape[1])
                    sp.dma_start(dst, src).then_inc(unit_in[u % RING], 16)

            def rows(name):
                return w[name].rearrange("(k p) n -> p k n", p=P)

            def pieces(name, kts, c0):
                v = rows(name)
                return [v[:, k, bass.ds(c0, COLS)] for k in kts]

            wi = w["w_in"].rearrange("(k p) (b c) -> p k b c", p=P, c=D_ATTN)
            for j in range(4):
                load(U_ZV, j, [wi[:, 2 * j + a, 4, :] for a in range(2)])
            for dst, src in ((trows[:, :], dw_w.rearrange("t (j p) -> (t j) p", p=P)), (relb[:, :], rel_bias),
                             (onehot[:, :], onehot_c), (lnmult[:, :], lnmult_c),
                             (wsin[:, :, :], sgu_w.rearrange("g t s -> t g s"))):
                sp.dma_start(dst, src).then_inc(small_in, 16)

            def qkv(p, turn=0, per=0):
                for j in range(4):
                    load(U_QKV, j, [wi[:, 2 * j + a, 0:4, bass.ds(p * P, P)] for a in range(2)], turn, per)

            qkv(0)
            for i in range(2):
                sp.wait_ge(drained[6 + i], nth("small", f"rel{i}"))
            sp.dma_start(scratch[:, :, 0:1024], relrow[:, :].unsqueeze(1).broadcast_to([N_HEADS, P, 1024]))\
                .then_inc(rel_out, 16)
            for e in range(2):
                sp.dma_start(sgub[HEAD_DIM * e:HEAD_DIM * (e + 1), :, :],
                             bass.AP(sgu_b.tensor, e * P, [[0, HEAD_DIM], [2 * P, 4], [1, P]])).then_inc(sgu_in, 16)
            for dst, src in ((mask[:, :, :], mask_c), (diag[:, :], diag_c), (poolinv[:, :, :], poolinv_c)):
                sp.dma_start(dst, src).then_inc(consts_in, 16)
            for k in range(4, KT):
                b = banks.bank("x", ("x", k))
                sp.wait_ge(drained[b], nth("x", ("x", k)))
            sp.wait_ge(rel_out, 16)
            sp.dma_start(btab[:, :, :], bass.AP(scratch.tensor, P - 1, [[1024, P], [1025 * P, N_HEADS], [1, SKEW]]))\
                .then_inc(btab_in, 16)
            with sp.Fori(0, PAIRS - 1) as r:
                qkv(r + 1, r + 1, 4)
            order = ((4, 5), (6, 7), (0, 1), (2, 3))
            for h in range(2):
                for j, kts in enumerate(order):
                    load(U_WOUT, 4 * h + j, pieces("w_out", kts, h * COLS))
            ff2 = rows("w_ff2")

            def ffn_up(j0, g, turn=0, per=0):
                for j in range(4):
                    load(U_FFN, j0 + j, pieces("w_ff1", (2 * j, 2 * j + 1), g * COLS), turn, per)

            def ffn_down(j0, g, turn=0, per=0):
                for j in range(4):
                    h, i = j // 2, j % 2
                    load(U_FFN, j0 + j, [ff2[:, bass.ds(g * 4 + (2 * i + a), 1), h * COLS:(h + 1) * COLS]
                                         for a in range(2)], turn, per)

            ffn_up(0, 0)
            with sp.Fori(0, FFN_GROUPS // 2 - 1) as i:
                ffn_up(4, i * 2 + 1, i, 16)
                ffn_down(8, i * 2, i, 16)
                ffn_up(12, i * 2 + 2, i, 16)
                ffn_down(16, i * 2 + 1, i, 16)
            ffn_up(8 * FFN_GROUPS - 12, FFN_GROUPS - 1)
            ffn_down(8 * FFN_GROUPS - 8, FFN_GROUPS - 2)
            ffn_down(8 * FFN_GROUPS - 4, FFN_GROUPS - 1)
            ci = w["cp_w_in_2"].rearrange("(k p) (b c) -> p k b c", p=P, c=D // 2)
            def cp_pair(j0, g):
                for j in range(4):
                    load(U_CPIN, j0 + j, [ci[:, 2 * j + a, 0:2, g * 256:(g + 1) * 256] for a in range(2)])

            cp_pair(0, 0)
            for j in range(4):
                load(U_CPIN, 4 + j, [ci[:, 2 * j + a, 2, :] for a in range(2)])
            cp_pair(8, 1)
            for h in range(2):
                for j, kts in enumerate(order):
                    load(U_CPOUT, 4 * h + j, pieces("cp_w_out_2", kts, h * COLS))

            def glu(layer):
                w1, w3, w2 = (w[f"ffn_{n}_2"][layer].rearrange("(k p) n -> p k n", p=P) for n in ("w1", "w3", "w2"))

                def up(j0, g, turn, per):
                    for j in range(4):
                        u = U_GLU[layer] + j0 + j
                        if u >= RING:
                            sp.wait_ge(unit_lo, turn * per + (u - RING + 1))
                        slot = raw[:, u % RING, :, :]
                        for a, v in enumerate((w1, w3)):
                            sp.dma_start(slot[:, :, a * 256:(a + 1) * 256],
                                         v[:, 2 * j:2 * j + 2, bass.ds(g * 256, 256)]).then_inc(unit_in[u % RING], 16)

                def down(j0, g, turn, per):
                    for h in range(2):
                        load(U_GLU[layer], j0 + h, [w2[:, bass.ds(g * 2 + a, 1), h * COLS:(h + 1) * COLS]
                                                    for a in range(2)], turn, per)

                up(0, 0, 0, 0)
                with sp.Fori(0, GLU_GROUPS // 2) as i:
                    up(4, i * 2 + 1, i, 12)
                    down(8, i * 2, i, 12)
                    up(10, i * 2 + 2, i, 12)
                    down(14, i * 2 + 1, i, 12)
                down(6 * GLU_GROUPS - 2, GLU_GROUPS - 1, 0, 0)

            glu(0)
            hi = w["hg_w_in_2"].rearrange("(k p) (b c) -> p k b c", p=P, c=D)
            with sp.Fori(0, HG_HEADS) as n:
                for j in range(4):
                    load(U_HGIN, j, [hi[:, 2 * j + a, 0:4, bass.ds(n * P, P)] for a in range(2)], n, 4)
            for h in range(2):
                for j in range(4):
                    load(U_HGOUT, 4 * h + j, pieces("hg_w_out_2", (2 * j, 2 * j + 1), h * COLS))
            glu(1)
            for t in range(TT):
                for h in range(2):
                    b = banks.bank("end", ("y", t, h))
                    sp.wait_ge(drained[b], nth("end", ("y", t, h)))
                    cols = slice(h * D // 2, (h + 1) * D // 2)
                    sp.dma_start(out[t * P:(t + 1) * P, cols], otok[:, t, cols]).then_inc(out_done, 16)
            sp.wait_ge(out_done, 16 * 2 * TT)

        @block.gpsimd
        def _(pool):
            def lo_parts(first, n):
                with pool.Fori(0, n // RING) as r:
                    for i in range(RING):
                        u = first + i
                        pool.wait_ge(unit_hi, r * RING + (u + 1))
                        pool.tensor_tensor(wlo[:, u % RING, :, :], raw[:, u % RING, :, :],
                                           whi[:, u % RING, :, :].bitcast(F32), ALU.subtract).then_inc(unit_lo, 1)

            lo_parts(0, U_CPIN)
            pool.tensor_tensor(tapdiag[:, 0:TAPS, :], ident[:, :].unsqueeze(1).broadcast_to([P, TAPS, P]),
                               taps[:, :, 3:4].broadcast_to([P, TAPS, P]), ALU.mult).then_inc(tapdiag_ready, 1)
            lo_parts(U_CPIN, 8)

            def lo_part(u):
                pool.wait_ge(unit_hi, u + 1)
                pool.tensor_tensor(wlo[:, u % RING, :, :], raw[:, u % RING, :, :],
                                   whi[:, u % RING, :, :].bitcast(F32), ALU.subtract).then_inc(unit_lo, 1)

            lo_part(U_CPIN + 8)
            lo_part(U_CPIN + 9)
            n = 0
            pool.wait_ge(set_up, 5)
            pool.wait_ge(consts_in, 16 * 3)
            for j in range(4):
                last = upad[:, j, :]
                b = banks.bank("cpin", ("g", 2, j))
                pool.wait_ge(drained[b], nth("cpin", ("g", 2, j)))
                for i in range(j + 1):
                    d = 1 << i
                    lo = 2 * d - 1
                    if n:
                        pool.wait_ge(win_step, n)
                    pool.tensor_tensor(wsum[:, i % 2, lo:], last[:, lo:], last[:, lo - d:POOL_PAD + SEQ - d],
                                       ALU.add).then_inc(win_step, 1)
                    n += 1
                    last = wsum[:, i % 2, :]
                pool.wait_ge(win_step, n)
                pool.tensor_scalar(pmean[:, :], last[:, POOL_PAD:], 1.0 / POOL_WINDOWS[j], None,
                                   ALU.mult).then_inc(win_step, 1)
                n += 1
                pool.wait_ge(win_step, n)
                pool.tensor_tensor(pmean[:, 0:POOL_PAD], last[:, POOL_PAD:2 * POOL_PAD], poolinv[:, j, :],
                                   ALU.mult).then_inc(win_step, 1)
                n += 1
                pool.wait_ge(win_step, n)
                pool.tensor_tensor(pdiff[:, j, :], pmean[:, :], upad[:, j, POOL_PAD:], ALU.subtract)\
                    .then_inc(pdiff_ready, 1)
                pool.wait_ge(pdiff_ready, j + 1)
                if j < 3:
                    lo_part(U_CPIN + 10 + j)
            for j in range(1, 3):
                lo_part(U_CPOUT + j)
            for j in range(4):
                pool.wait_ge(pout_hi, j + 1)
                pool.tensor_tensor(m_lo[:, 4 + j, :], pout[:, j, :], m_hi[:, 4 + j, :].bitcast(F32), ALU.subtract)\
                    .then_inc(pout_lo, 1)
            for j in range(3, 8):
                lo_part(U_CPOUT + j)
            lo_parts(U_GLU[0], UNITS - U_GLU[0])

        @block.scalar
        def _(act):
            act.preload_act_table_set(LOG_TABLES)

            def split(first, j, turn=0, per=0):
                u = first + j + AHEAD
                act.wait_ge(unit_in[u % RING], turn * (8 * per) + 32 * (u // RING + 1))
                if u >= RING:
                    act.wait_ge(unit_begun, turn * per + (u - RING + 2))
                act.activation(whi[:, u % RING, :, :], raw[:, u % RING, :, :], ACT.Copy).then_inc(unit_hi, 1)

            def square(i, k, tile):
                if k >= 2:
                    act.wait_ge(sq_used, KT * (i - 1) + k - 1)
                act.activation(sq[:, k % 2, :], tile, ACT.Square).then_inc(sq_ready, 1)

            def inv_rms(i):
                b = banks.bank(f"norm{i}", "sum")
                act.wait_ge(filled[b], nth(f"norm{i}", "sum"))
                act.activation(rs[:, :], bank(f"norm{i}", "sum"), ACT.Ln, bias=eps6[:, :], scale=1.0 / D)\
                    .then_inc(drained[b], 1)
                act.wait_ge(drained[b], nth(f"norm{i}", "sum"))
                act.activation(rs[:, :], rs[:, :], ACT.Exp, scale=-0.5).then_inc(rs_ready, 1)

            def h_parts(n, i, ready, name, off=0, units={}):
                for k in range(KT):
                    if k in units:
                        split(*units[k])
                    ready(k)
                    c = COL[name] + off + k
                    act.activation(h_hi[:, k, :], xT[:, k, :], ACT.Copy, scale=vecs[:, c:c + 1]).then_inc(hi_ready, 1)
                    square(i, k, xT[:, k, :])

            def x_is(n):
                return lambda k: act.wait_ge(x_ready, n + k + 1)

            def out_done_is(stage):
                return lambda k: act.wait_ge(drained[k], nth(stage, ("h", k // 4, k % 4)))

            act.wait_ge(set_up, 3)
            for t in range(TT):
                act.wait_ge(x_in[t], 16)
                if t:
                    act.wait_ge(xss_ready, t)
                act.activation(xsq[:, :], xin[:, t, :], ACT.Square, accum_out=xss[:, t:t + 1]).then_inc(xss_ready, 1)
                act.wait_ge(xss_ready, t + 1)
                act.activation(xrs[:, t:t + 1], xss[:, t:t + 1], ACT.Ln, bias=eps6[:, :], scale=1.0 / D)\
                    .then_inc(xrs_ready, 1)
                act.wait_ge(xrs_ready, 2 * t + 1)
                act.activation(xrs[:, t:t + 1], xrs[:, t:t + 1], ACT.Exp, scale=-0.5).then_inc(xrs_ready, 1)
            for u in range(AHEAD):
                act.wait_ge(unit_in[u], 32)
                act.activation(whi[:, u, :, :], raw[:, u, :, :], ACT.Copy).then_inc(unit_hi, 1)
            act.wait_ge(drained[4], nth("start", "vec"))
            for k in range(KT):
                act.wait_ge(filled[k], nth("start", ("h", k)))
                c = COL["g_pre_mix"] + k
                act.activation(h_hi[:, k, :], bank("start", ("h", k)), ACT.Copy, scale=vecs[:, c:c + 1])\
                    .then_inc(hi_ready, 1)
            for j in range(4):
                split(U_ZV, j)
            for m in range(4):
                act.wait_ge(filled[m], nth("zv", ("m", m)))
                act.activation(gv[:, m, :], bank("zv", ("m", m)), ACT.Gelu_apprx_tanh).then_inc(drained[m], 1)
            act.preload_act_table_set(LOG_TABLES)
            split(U_QKV, 0)
            act.wait_ge(lb_step, 3)
            act.activation(lbt[:, 2, :], lbt[:, 1, :], ACT.Exp).then_inc(lb_exp, 1)
            act.activation(lbt[:, 4, :], lbt[:, 3, :], ACT.Exp).then_inc(lb_exp, 1)
            for k in range(1, KT, 2):
                b = banks.bank("x", ("x", k))
                act.wait_ge(filled[b], nth("x", ("x", k)))
                act.activation(xT[:, k, :], bank("x", ("x", k)), ACT.Copy).then_inc(drained[b], 1)
            for m in range(4):
                act.wait_ge(sgu_step, m + 1)
                act.activation(sgu_vt[:, m, :], gv[:, m, :], ACT.Square).then_inc(sgu_sq, 1)
            split(U_QKV, 1)
            act.wait_ge(filled[5], nth("zvnorm", "var"))
            act.activation(rs[:, :], bank("zvnorm", "var"), ACT.Ln, bias=eps5[:, :], scale=1.0 / (4 * P))\
                .then_inc(drained[5], 1)
            act.wait_ge(drained[5], nth("zvnorm", "var"))
            act.activation(rs[:, :], rs[:, :], ACT.Exp, scale=-0.5).then_inc(rs_ready, 1)
            split(U_QKV, 2)
            split(U_QKV, 3)

            def drain_qkv(stage, turn, p):
                for e in range(2):
                    own, other = own_rows(e), own_rows(1 - e)
                    for m, dst in ((1, k_his), (0, q_parts)):
                        act.wait_ge(filled[m], nth(stage, ("m", m), turn))
                        act.activation(dst[own, e, :], bank(stage, ("m", m))[own], ACT.Copy,
                                       scale=HEAD_DIM ** -0.5 if m == 0 else 1.0).then_inc(qk_hi, 1)
                    act.wait_ge(qk_hi, p * 6 + (3 * e + 1))
                    act.activation(k_his[other, e, :], k_his[own, e, :].bitcast(F32), ACT.Copy).then_inc(qk_hi, 1)
                act.wait_ge(filled[2], nth(stage, ("m", 2), turn))
                act.activation(vT[:, :], bank(stage, ("m", 2)), ACT.Copy).then_inc(drained[2], 1)

            for j in range(4):
                act.wait_ge(filled[4 + j], nth("sgu", ("vt", j)))
                act.activation(sgu_vt[:, j, :], bank("sgu", ("vt", j)), ACT.Copy).then_inc(drained[4 + j], 1)
            drain_qkv("qkv0", 0, 0)

            def pair_out(p):
                act.wait_ge(filled[7], nth("att", "oT", p))
                act.activation(tile_of(m_hi, p), bank("att", "oT"), ACT.Copy).then_inc(o_hi, 1)

            def attend(p, u_count, units, before_it, following=None):
                act.wait_ge(filled[6], nth("att", "vtok", p))
                act.activation(vtok[:, :], bank("att", "vtok"), ACT.Copy).then_inc(drained[6], 1)
                act.wait_ge(filled[3], u_count)
                if before_it is not None:
                    act.wait_ge(sg_lo, before_it + 1)
                act.activation(ug[:, :], ps[:, 3, :], ACT.Gelu_apprx_tanh).then_inc(drained[3], 1)
                act.preload_act_table_set(LOG_TABLES)
                for i in range(8):
                    act.wait_ge(neg_ready, p * 8 + (i + 1))
                    act.activation(prob[:, i % 2, :], sbias[:, i % 2, :], ACT.Exp, bias=nmax[:, i:i + 1],
                                   accum_out=den[:, i:i + 1]).then_inc(prob_ready, 1)
                    if i % 2:
                        units(i // 2)
                    if i == 1:
                        act.wait_ge(sg_ready, p + 1)
                        act.activation(tile_of(m_hi, 4 + p), ug[:, :], ACT.Copy).then_inc(sg_hi, 1)
                        if before_it is not None:
                            pair_out(before_it)
                if following is not None:
                    drain_qkv("qkv", following, following + 1)

            u_first = nth("qkv0", ("m", 3))
            attend(0, u_first, lambda i: split(U_QKV + 4, i), None, 0)
            with act.Fori(0, PAIRS - 2) as r:
                attend(r + 1, r + (u_first + 1), lambda i: split(U_QKV + 8, i, r, 4), r, r + 1)
            attend(PAIRS - 1, u_first + PAIRS - 1, lambda i: split(U_WOUT, i) if i < 3 else None, PAIRS - 2)
            pair_out(PAIRS - 1)
            def acc_squares(tiles):
                for k in tiles:
                    b = 4 + k % 4
                    act.wait_ge(drained[b], nth("ffndown", ("d", k // 4, k % 4), FFN_GROUPS - 1))
                    square(3, k, acc[:, k, :])

            def wout_squares(tiles):
                for k in tiles:
                    b = banks.bank("wout", ("h", k // 4, k % 4))
                    act.wait_ge(drained[b], nth("wout", ("h", k // 4, k % 4)))
                    square(1, k, acc[:, k, :])

            first_half, second_half = range(KT // 2), range(KT // 2, KT)

            for j in range(3, 6):
                split(U_WOUT, j)
            wout_squares(first_half)
            split(U_WOUT, 6)
            split(U_WOUT, 7)
            wout_squares(second_half)
            inv_rms(1)
            h_parts(1, 2, x_is(0), "g_pre_ffn", 0, {3: (U_FFN, 0), 5: (U_FFN, 1)})

            def ffn_up(j0, g, turn_of_bank, par, turn=0, per=0, begin=0, middle=None):
                for j in range(begin, 4):
                    split(U_FFN, j0 + j, turn, per)
                if middle:
                    middle()
                stage = "ffn0" if isinstance(g, int) and g == 0 else "ffnup"
                for m in range(4):
                    act.wait_ge(drained[banks.bank(stage, ("m", m))], nth(stage, ("m", m), turn_of_bank))
                    act.activation(m_hi[:, 4 * par + m, :], relu[:, m % 2, :], ACT.Square).then_inc(hid_hi, 1)

            def ffn_down(j0, turn=0, per=0):
                for j in range(4):
                    split(U_FFN, j0 + j, turn, per)

            ffn_up(0, 0, 0, 0, begin=2, middle=lambda: inv_rms(2))
            with act.Fori(0, FFN_GROUPS // 2 - 1) as i:
                ffn_up(4, i * 2 + 1, i * 2, 1, i, 16)
                ffn_down(8, i, 16)
                ffn_up(12, i * 2 + 2, i * 2 + 1, 0, i, 16)
                ffn_down(16, i, 16)
            ffn_up(8 * FFN_GROUPS - 12, FFN_GROUPS - 1, FFN_GROUPS - 2, 1)
            ffn_down(8 * FFN_GROUPS - 8)

            split(U_FFN, 8 * FFN_GROUPS - 4)
            split(U_FFN, 8 * FFN_GROUPS - 3)
            acc_squares(first_half)
            split(U_FFN, 8 * FFN_GROUPS - 2)
            split(U_FFN, 8 * FFN_GROUPS - 1)
            acc_squares(second_half)
            inv_rms(3)
            h_parts(2, 4, x_is(KT), "norm_mix_g_2", 0, {3: (U_CPIN, 0), 5: (U_CPIN, 1)})

            act.dma_start(poolw[:, :, :], pool_w.rearrange("g c d -> c g d")).then_inc(poolw_in, 16)
            for j in range(2, 4):
                split(U_CPIN, j)
            inv_rms(4)
            for g in range(2):
                if g:
                    for j in range(4, 12):
                        split(U_CPIN, j)
                    split(U_CPOUT, 0)
                for i in range(2):
                    b = banks.bank("cpin", ("g", g, 2 + i))
                    act.wait_ge(drained[b], nth("cpin", ("g", g, 2 + i)))
                    act.activation(csig[:, i, :], csig[:, i, :], ACT.Sigmoid).then_inc(csig_ready, 1)
            def pool_out(j):
                b = banks.bank("cpin", ("pool", j))
                act.wait_ge(filled[b], nth("cpin", ("pool", j)))
                c = COL["cp_pool_scale_2"] + j
                act.activation(pout[:, j, :], bank("cpin", ("pool", j)), ACT.Copy, scale=vecs[:, c:c + 1])\
                    .then_inc(drained[b], 1)
                act.wait_ge(drained[b], nth("cpin", ("pool", j)))
                act.activation(m_hi[:, 4 + j, :], pout[:, j, :], ACT.Copy).then_inc(pout_hi, 1)

            act.wait_ge(filled[4], nth("cpin", "conv"))
            c = COL["cp_dw_b_2"] + 3
            act.activation(conv[:, 3, :], bank("cpin", "conv"), ACT.Identity, bias=vecs[:, c:c + 1])\
                .then_inc(drained[4], 1)
            for j in range(4):
                pool_out(j)
            act.preload_act_table_set(LOG_TABLES)
            for j in range(4):
                act.wait_ge(cln_step, j + 1)
                act.activation(csq[:, j, :], conv[:, j, :], ACT.Square).then_inc(cln_sq, 1)
            split(U_CPOUT, 1)
            act.wait_ge(filled[4], nth("cpin", "var"))
            act.activation(crs[:, :], bank("cpin", "var"), ACT.Ln, bias=eps6[:, :], scale=1.0 / (4 * P))\
                .then_inc(drained[4], 1)
            act.wait_ge(drained[4], nth("cpin", "var"))
            act.activation(crs[:, :], crs[:, :], ACT.Exp, scale=-0.5).then_inc(crs_ready, 1)
            for j in range(4):
                cg, cb = COL["cp_ln_g_2"] + j, COL["cp_ln_b_2"] + j
                act.wait_ge(cln_y, j + 1)
                act.activation(csq[:, j, :], conv[:, j, :], ACT.Silu, bias=vecs[:, cb:cb + 1],
                               scale=vecs[:, cg:cg + 1]).then_inc(cs_ready, 1)
                act.wait_ge(cs_ready, j + 1)
                act.activation(m_hi[:, j, :], csq[:, j, :], ACT.Copy).then_inc(cs_hi, 1)
            act.preload_act_table_set(LOG_TABLES)
            for j in range(2, 6):
                split(U_CPOUT, j)

            h_parts(3, 5, out_done_is("cpout"), "norm_ffn_g_2", 0, {4: (U_CPOUT, 6), 5: (U_CPOUT, 7)})

            def glu(layer):
                first, stage = U_GLU[layer], f"glu{layer}"

                done = 2 * GLU_GROUPS * layer

                def up(j0, g, par, turn, per, middle=None):
                    for j in range(4):
                        split(first, j0 + j, turn, per)
                    if middle:
                        middle()
                    for i in range(2):
                        act.wait_ge(drained[i], nth(stage, ("m", i), g))
                        act.activation(silu[:, i, :], gate[:, i, :], ACT.Silu).then_inc(silu_ready, 1)
                    for i in range(2):
                        act.wait_ge(ghid_ready, g * 2 + (done + i + 1))
                        act.activation(m_hi[:, 2 * par + i, :], ghid[:, i, :], ACT.Copy).then_inc(ghid_hi, 1)

                def down(j0, turn, per):
                    for h in range(2):
                        split(first, j0 + h, turn, per)

                up(0, 0, 0, 0, 0, lambda: inv_rms(5 + 2 * layer))
                with act.Fori(0, GLU_GROUPS // 2) as i:
                    up(4, i * 2 + 1, 1, i, 12)
                    down(8, i, 12)
                    up(10, i * 2 + 2, 0, i, 12)
                    down(14, i, 12)
                if layer == 0:
                    down(6 * GLU_GROUPS - 2, 0, 0)
                act.preload_act_table_set(LOG_TABLES)

            glu(0)

            def glu_x(layer):
                return lambda k: act.wait_ge(drained[4 + k % 4], nth(f"glu{layer}", ("d", k // 4, k % 4), GLU_GROUPS - 1))

            h_parts(4, 6, glu_x(0), "norm_mix_g_2", KT)

            def head_gates(n):
                act.wait_ge(drained[1], nth("hgin", ("m", 1), n))
                act.activation(sgf[:, :], sgf[:, :], ACT.Sigmoid).then_inc(sgf_ready, 1)
                act.wait_ge(drained[3], nth("hgin", ("m", 3), n))
                act.activation(sgg[:, :], gT[:, :], ACT.Sigmoid).then_inc(sgg_ready, 1)
                act.preload_act_table_set(LOG_TABLES)
                act.wait_ge(sgf_ready, n + 1)
                act.wait_ge(fcol_ready, n + 1)
                act.activation(lf[:, :], sgf[:, :], ACT.Ln, bias=fcol[:, 1:2], scale=fcol[:, 0:1]).then_inc(lf_ready, 1)

            def head_norm(n):
                act.wait_ge(filled[4], nth("hg", "sum", n))
                act.activation(hln[:, :], bank("hg", "sum"), ACT.Ln, bias=eps6[:, :], scale=1.0 / P)\
                    .then_inc(drained[4], 1)
                act.wait_ge(drained[4], nth("hg", "sum", n))
                act.activation(hrs[:, :], hln[:, :], ACT.Exp, scale=-0.5).then_inc(hrs_ready, 1)

            def head_out(n):
                act.wait_ge(ho_ready, n + 1)
                act.activation(tile_of(m_hi, n), ho[:, :], ACT.Copy).then_inc(ho_hi, 1)

            def core(n, units, before_it, last=False):
                L = len(LEVELS)
                act.wait_ge(cum_ready, 4 * n + 4)
                act.activation(e0[:, :], cum[:, :], ACT.Exp).then_inc(e0_ready, 1)
                act.wait_ge(dend_ready, n + 1)
                act.activation(dend[:, :], dend[:, :], ACT.Exp).then_inc(eend_ready, 1)
                units(0)
                for i in range(L):
                    act.wait_ge(dlev_ready, n * (2 * L) + (2 * i + 2))
                    if i >= 2:
                        act.wait_ge(qk_ready, n * (2 * L) + 2 * (i - 1))
                    act.activation(elev[:, i % 2, :], dlev[:, i % 2, :], ACT.Exp).then_inc(elev_ready, 1)
                    if i == 0 and before_it is not None:
                        head_norm(before_it)
                    if i == 1:
                        act.wait_ge(filled[5], nth("hg", "vt", n))
                        act.activation(vh[:, :], bank("hg", "vt"), ACT.Copy).then_inc(drained[5], 1)
                    if i == 2:
                        if before_it is not None:
                            head_out(before_it)
                        units(1)
                    if i == 5:
                        act.wait_ge(filled[4], nth("hg", "ket", n))
                        act.activation(keT[:, :], bank("hg", "ket")[:, 0:3 * P], ACT.Copy).then_inc(drained[4], 1)
                        units(2)
                units(3)
                if not last:
                    head_gates(n + 1)
                act.wait_ge(filled[6], nth("hg", "o", n))
                act.activation(hsq[:, :], bank("hg", "o"), ACT.Square).then_inc(hsq_ready, 1)

            for j in range(4):
                split(U_HGIN, j)
            inv_rms(6)
            head_gates(0)
            core(0, lambda j: split(U_HGIN + 4, j), None)
            with act.Fori(0, HG_HEADS - 2) as r:
                core(r + 1, lambda j: split(U_HGIN + 8, j, r, 4), r)
            core(HG_HEADS - 1, lambda j: split(U_HGOUT, j) if j < 3 else None, HG_HEADS - 2, True)
            head_norm(HG_HEADS - 1)
            head_out(HG_HEADS - 1)
            for j in range(3, 6):
                split(U_HGOUT, j)
            h_parts(5, 7, out_done_is("hgout"), "norm_ffn_g_2", KT, {4: (U_HGOUT, 6), 5: (U_HGOUT, 7)})
            glu(1)
            for k in range(KT):
                glu_x(1)(k)
                square(8, k, xT[:, k, :])
            act.wait_ge(filled[7], nth("end", "sum"))
            act.activation(yrs[:, :], bank("end", "sum")[:, 0:TT], ACT.Ln, bias=eps6[:, :], scale=1.0 / D)\
                .then_inc(drained[7], 1)
            act.wait_ge(drained[7], nth("end", "sum"))
            act.activation(yrs[:, :], yrs[:, :], ACT.Exp, scale=-0.5).then_inc(yrs_ready, 1)
            act.wait_ge(yrs_ready, 1)
            for t in range(TT):
                act.wait_ge(filled[t], nth("end", ("y", t, 0)))
                act.activation(otok[:, t, 0:D // 2], bank("end", ("y", t, 0)), ACT.Copy, scale=yrs[:, t:t + 1])\
                    .then_inc(drained[t], 1)

        @block.tensor
        def _(pe):
            def unit(first, j, xh, xl, kts, stage, tags, starts, stops, turn=0, per=0, order=(0, 1, 2, 3), use=None,
                     wait_tile=None, by_tile=None):
                use = turn if use is None else use
                by_tile = stops if by_tile is None else by_tile
                u = first + j
                s = u % RING
                pe.wait_ge(unit_lo, turn * per + (u + 1))
                begun = False
                for a, m in [(a, m) for m in order for a in range(2)] if by_tile else [(a, m) for a in range(2) for m in order]:
                    if wait_tile and m == order[0]:
                        wait_tile(a)
                    b = banks.bank(stage, tags[m])
                    if starts and a == 0:
                        pe.wait_ge(drained[b], before(stage, tags[m], use))
                    for i, (wt, xt) in enumerate(((wlo, xh), (whi, xl), (whi, xh))):
                        last = stops and a == 1 and i == 2
                        mm = pe.matmul(ps[:, b, :], wt[:, s, a, m * P:(m + 1) * P], xt[:, kts[a], :],
                                       start=starts and a == 0 and i == 0, stop=last)
                        if not begun:
                            mm.then_inc(unit_begun, 1)
                            begun = True
                        if last:
                            mm.then_inc(filled[b], 1)

            def group(first, j0, stage, tags, turn=0, per=0, order=(0, 1, 2, 3), use=None, n=None, between=None):
                for j in range(4):
                    def tile(a, j=j):
                        k = 2 * j + a
                        if n == 0:
                            pe.wait_ge(drained[k], nth("start", ("h", k)))
                        else:
                            pe.wait_ge(lo_ready, KT * (n - 1) + k + 1)
                    unit(first, j0 + j, h_hi, h_lo, (2 * j, 2 * j + 1), stage, tags, j == 0, j == 3, turn, per, order,
                         use, tile if n is not None else None, j == 3 and n is None)
                    if between:
                        between(j)

            def keep_clock(b, n):
                for _ in range(n):
                    pe.matmul(ps[:, b, 0:P], ident[:, :], ident[:, :], start=True, stop=True)

            def norm_sum(i):
                b = banks.bank(f"norm{i}", "sum")
                pe.wait_ge(drained[b], before(f"norm{i}", "sum"))
                pe.wait_ge(sq_used, KT * i)
                pe.matmul(ps[:, b, :], ones[:, :], ss[:, :], start=True, stop=True).then_inc(filled[b], 1)

            up_tags = [("m", m) for m in range(4)]

            pe.wait_ge(gains_in, 16 * 2)
            pe.transpose(bank("start", "vec")[:, 0:N_VEC], vrows[:, :], ident[0:N_VEC, 0:N_VEC]).then_inc(filled[4], 1)
            for t in range(TT):
                pe.wait_ge(xdiag_ready, t + 1)
                for k in range(KT):
                    if t == 0:
                        pe.wait_ge(drained[k], before("start", ("h", k)))
                    mm = pe.matmul(ps[:, k, t * P:(t + 1) * P], xin[:, t, k * P:(k + 1) * P], xdiag[:, t, :],
                                   start=True, stop=True)
                    if t == TT - 1:
                        mm.then_inc(filled[k], 1)

            group(U_ZV, 0, "zv", up_tags, n=0)
            pe.wait_ge(small_in, 16 * 5)
            pe.wait_ge(drained[5], before("small", "taps"))
            pe.transpose(bank("small", "taps")[:, 0:4 * TAPS], trows[:, :], ident[0:4 * TAPS, 0:4 * TAPS])\
                .then_inc(filled[5], 1)
            for i in range(2):
                pe.wait_ge(drained[6 + i], before("small", f"rel{i}"))
                pe.matmul(bank("small", f"rel{i}")[0:N_HEADS, :], relb[:, :], onehot[:, i * 512:(i + 1) * 512],
                          start=True, stop=True).then_inc(filled[6 + i], 1)
            for i in range(2):
                pe.wait_ge(drained[4 + i], before("small", f"ws{i}"))
                for g in range(4):
                    mm = pe.transpose(ps[:, 4 + i, g * P:(g + 1) * P], wsin[:, 4 * i + g, :], ident[:, :])
                mm.then_inc(filled[4 + i], 1)
            for k in range(KT):
                b = banks.bank("x", ("x", k))
                pe.wait_ge(drained[b], before("x", ("x", k)))
                for t in range(TT):
                    mm = pe.transpose(ps[:, b, t * P:(t + 1) * P], xin[:, t, k * P:(k + 1) * P], ident[:, :])
                mm.then_inc(filled[b], 1)

            def sgu_sums(j):
                if j == 0:
                    pe.wait_ge(drained[4], before("zvnorm", "mean"))
                    pe.wait_ge(gsum_step, 3)
                    pe.matmul(bank("zvnorm", "mean"), ones[:, :], gsum[:, :], start=True, stop=True).then_inc(filled[4], 1)
                if j == 1:
                    pe.wait_ge(drained[5], before("zvnorm", "var"))
                    pe.wait_ge(gsum_step, 6)
                    pe.matmul(bank("zvnorm", "var"), ones[:, :], gsum[:, :], start=True, stop=True).then_inc(filled[5], 1)

            group(U_QKV, 0, "qkv0", up_tags, between=sgu_sums)
            for j in range(4):
                pe.wait_ge(drained[4 + j], before("sgu", ("vt", j)))
                pe.wait_ge(sgu_y, j + 1)
                for t in range(TT):
                    mm = pe.transpose(ps[:, 4 + j, t * P:(t + 1) * P], gv[:, j, t * P:(t + 1) * P], ident[:, :])
                mm.then_inc(filled[4 + j], 1)
            for j in range(4):
                pe.wait_ge(drained[4 + j], before("sgu", ("mix", j)))
                for t in range(TT):
                    for e in range(2):
                        mm = pe.matmul(ps[HEAD_DIM * e:HEAD_DIM * (e + 1), 4 + j, t * P:(t + 1) * P],
                                       sgu_vt[:, j, t * P + HEAD_DIM * e:t * P + HEAD_DIM * (e + 1)],
                                       wsT[:, 2 * j + e, :], start=True, stop=True)
                mm.then_inc(filled[4 + j], 1)

            def scores(i, p):
                e, t = i // 4, i % 4
                own, cols = own_rows(e), slice(t * P, (t + 1) * P)
                b = banks.bank("att", ("s", i))
                if t == 0:
                    pe.wait_ge(qk_hi, p * 6 + (3 * e + 3))
                    pe.wait_ge(qk_lo, p * 4 + (2 * e + 2))
                pe.wait_ge(drained[b], before("att", ("s", i), p))
                pe.matmul(ps[:, b, :], q_parts[own, e, cols], k_lo[own, :], start=True, stop=False)
                pe.matmul(ps[:, b, :], q_parts[:, e, cols], k_his[:, e, :], start=False, stop=True).then_inc(filled[b], 1)

            def values_turned(p):
                pe.wait_ge(drained[2], nth("qkv0", ("m", 2)) + p)
                pe.wait_ge(drained[6], before("att", "vtok", p))
                for t in range(TT):
                    mm = pe.transpose(ps[:, 6, t * P:(t + 1) * P], vT[:, t * P:(t + 1) * P], ident[:, :])
                mm.then_inc(filled[6], 1)

            def pair_out(p):
                pe.wait_ge(onorm_ready, p * 2 + 2)
                pe.wait_ge(drained[7], before("att", "oT", p))
                for t in range(TT):
                    mm = pe.transpose(ps[:, 7, t * P:(t + 1) * P], onorm[:, t, :], ident[:, :])
                mm.then_inc(filled[7], 1)

            def attend(p, units, before_it, following=None):
                def turn(i):
                    pe.wait_ge(prob_ready, p * 8 + (i + 1))
                    pe.wait_ge(drained[6], before("att", ("t", i), p))
                    for k in range(TT):
                        mm = pe.transpose(ps[:, 6, k * P:(k + 1) * P], prob[:, i % 2, k * P:(k + 1) * P], ident[:, :])
                    mm.then_inc(filled[6], 1)

                def values(i):
                    e, t = i // 4, i % 4
                    cols = slice(t * P + HEAD_DIM * e, t * P + HEAD_DIM * (e + 1))
                    pe.wait_ge(drained[6], nth("att", ("t", i), p))
                    if t == 0:
                        pe.wait_ge(drained[7], before("att", ("o", e), p))
                    for k in range(TT):
                        mm = pe.matmul(ps[:, 7, cols], probT[:, i % 2, k * P:(k + 1) * P],
                                       vtok[:, k * P + HEAD_DIM * e:k * P + HEAD_DIM * (e + 1)],
                                       start=k == 0, stop=k == TT - 1)
                    if t == TT - 1:
                        mm.then_inc(filled[7], 1)

                units(0)
                if before_it is not None:
                    pair_out(before_it)
                turn(0)
                scores(2, p)
                turn(1)
                scores(3, p)
                units(1)
                values(0)
                values(1)
                turn(2)
                scores(4, p)
                turn(3)
                scores(5, p)
                units(2)
                values(2)
                values(3)
                turn(4)
                scores(6, p)
                turn(5)
                scores(7, p)
                units(3)
                values(4)
                values(5)
                turn(6)
                if following is not None:
                    scores(0, following)
                turn(7)
                if following is not None:
                    scores(1, following)
                values(6)
                values(7)
                if following is not None:
                    values_turned(following)

            def head_units(j0, j, turn=0, per=0):
                unit(U_QKV + j0, j, h_hi, h_lo, (2 * j, 2 * j + 1), "qkv", up_tags, j == 0, j == 3, turn, per,
                     use=turn + (j0 // 4 - 1))

            order = ((4, 5), (6, 7), (0, 1), (2, 3))

            def out_unit(first, stage, j):
                h = j // 4
                unit(first, j, m_hi, m_lo, order[j % 4], stage, [("h", h, m) for m in range(4)], j % 4 == 0, j % 4 == 3)

            def wout_early(j):
                if j < 2:
                    pe.wait_ge(sg_lo, 2 * j + 2)
                if j < 2:
                    out_unit(U_WOUT, "wout", j)

            scores(0, 0)
            scores(1, 0)
            values_turned(0)
            attend(0, lambda j: head_units(4, j), None, 1)
            with pe.Fori(0, PAIRS - 2) as r:
                attend(r + 1, lambda j: head_units(8, j, r, 4), r, r + 2)
            attend(PAIRS - 1, wout_early, PAIRS - 2)
            pe.wait_ge(drained[7], nth("att", "oT", 1))
            out_unit(U_WOUT, "wout", 2)
            pair_out(PAIRS - 1)
            pe.wait_ge(drained[7], nth("att", "oT", PAIRS - 1))
            for j in range(3, 8):
                out_unit(U_WOUT, "wout", j)
            norm_sum(1)
            pe.wait_ge(drained[1], nth("wout", ("h", 0, 1)))
            keep_clock(1, 20)

            def ffn_up(j0, turn_of_bank, turn=0, per=0):
                group(U_FFN, j0, "ffnup", up_tags, turn, per, use=turn_of_bank)

            def ffn_down(j0, g, par, turn=0, per=0):
                for j in range(4):
                    h, i = j // 2, j % 2

                    def tile(a):
                        pe.wait_ge(hid_lo, g * 4 + (2 * i + a + 1))
                    kt = 4 * par + 2 * i
                    unit(U_FFN, j0 + j, m_hi, m_lo, (kt, kt + 1), "ffndown", [("d", h, m) for m in range(4)],
                         i == 0, i == 1, turn, per, use=g, wait_tile=tile)

            def norm_after(i, last):
                return lambda j: norm_sum(i) if j == last else None

            group(U_FFN, 0, "ffn0", up_tags, n=1, between=norm_after(2, 3))
            with pe.Fori(0, FFN_GROUPS // 2 - 1) as i:
                ffn_up(4, i * 2, i, 16)
                ffn_down(8, i * 2, 0, i, 16)
                ffn_up(12, i * 2 + 1, i, 16)
                ffn_down(16, i * 2 + 1, 1, i, 16)
            ffn_up(8 * FFN_GROUPS - 12, FFN_GROUPS - 2)
            ffn_down(8 * FFN_GROUPS - 8, FFN_GROUPS - 2, 0)
            ffn_down(8 * FFN_GROUPS - 4, FFN_GROUPS - 1, 1)
            norm_sum(3)
            pe.wait_ge(drained[1], nth("ffnup", ("m", 1), FFN_GROUPS - 2))
            keep_clock(1, 20)

            gates_first = (2, 3, 0, 1)
            group(U_CPIN, 0, "cpin", [("g", 0, m) for m in range(4)], order=gates_first, n=2, between=norm_after(4, 3))
            group(U_CPIN, 4, "cpin", [("g", 2, m) for m in range(4)])
            group(U_CPIN, 8, "cpin", [("g", 1, m) for m in range(4)], order=gates_first)

            def pool_product(j):
                b = banks.bank("cpin", ("pool", j))
                pe.wait_ge(drained[b], before("cpin", ("pool", j)))
                pe.wait_ge(pdiff_ready, j + 1)
                pe.matmul(ps[:, b, :], poolw[:, j, :], pdiff[:, j, :], start=True, stop=True).then_inc(filled[b], 1)

            pe.wait_ge(poolw_in, 16)
            pool_product(0)
            pool_product(1)
            pe.wait_ge(drained[4], before("cpin", "conv"))
            pe.wait_ge(tapdiag_ready, 1)
            pe.wait_ge(apad_ready, 4)
            for i in range(TAPS):
                mm = pe.matmul(bank("cpin", "conv"), tapdiag[:, i, :], apad[:, 3, i:i + SEQ],
                               start=i == 0, stop=i == TAPS - 1)
            mm.then_inc(filled[4], 1)
            pe.wait_ge(drained[5], before("cpin", "mean"))
            pe.wait_ge(csum_step, 3)
            pe.matmul(bank("cpin", "mean"), ones[:, :], csum[:, :], start=True, stop=True).then_inc(filled[5], 1)
            pool_product(2)
            pool_product(3)
            pe.wait_ge(pout_lo, 2)
            out_unit(U_CPOUT, "cpout", 0)
            pe.wait_ge(drained[4], before("cpin", "var"))
            pe.wait_ge(csum_step, 6)
            pe.matmul(bank("cpin", "var"), ones[:, :], csum[:, :], start=True, stop=True).then_inc(filled[4], 1)
            pe.wait_ge(pout_lo, 4)
            out_unit(U_CPOUT, "cpout", 1)
            for j in range(2, 8):
                if j < 4:
                    pe.wait_ge(cs_lo, 2 * j - 2)
                out_unit(U_CPOUT, "cpout", j)

            def glu(layer, n):
                first, stage = U_GLU[layer], f"glu{layer}"
                done = 2 * GLU_GROUPS * layer

                def up(j0, g, turn, per):
                    group(first, j0, stage, up_tags, turn, per, (0, 2, 1, 3), g)

                def down(j0, g, par, turn, per):
                    for h in range(2):
                        def tile(a):
                            pe.wait_ge(ghid_lo, g * 2 + (done + a + 1))
                        unit(first, j0 + h, m_hi, m_lo, (2 * par, 2 * par + 1), stage,
                             [("d", h, m) for m in range(4)], True, True, turn, per, use=g, wait_tile=tile)

                group(first, 0, stage, up_tags, 0, 0, (0, 2, 1, 3), 0, n, norm_after(5 + 2 * layer, 2))
                with pe.Fori(0, GLU_GROUPS // 2) as i:
                    up(4, i * 2 + 1, i, 12)
                    down(8, i * 2, 0, i, 12)
                    up(10, i * 2 + 2, i, 12)
                    down(14, i * 2 + 1, 1, i, 12)
                down(6 * GLU_GROUPS - 2, GLU_GROUPS - 1, 0, 0, 0)

            glu(0, 3)

            head_order = (1, 3, 0, 2)
            group(U_HGIN, 0, "hgin", up_tags, order=head_order, n=4, between=norm_after(6, 2))

            def head_sum(n):
                pe.wait_ge(hsq_ready, n + 1)
                pe.wait_ge(drained[4], before("hg", "sum", n))
                pe.matmul(ps[:, 4, :], ones[:, :], hsq[:, :], start=True, stop=True).then_inc(filled[4], 1)

            def core(n, units, before_it):
                L = len(LEVELS)
                units(0)
                if before_it is not None:
                    head_sum(before_it)
                pe.wait_ge(drained[2], nth("hgin", ("m", 2), n))
                pe.wait_ge(drained[5], before("hg", "vt", n))
                for t in range(TT):
                    mm = pe.transpose(ps[:, 5, t * P:(t + 1) * P], iT[:, t * P:(t + 1) * P], ident[:, :])
                mm.then_inc(filled[5], 1)
                units(1)
                pe.wait_ge(kend_ready, n + 1)
                pe.wait_ge(drained[4], before("hg", "ket", n))
                for t in range(3):
                    mm = pe.transpose(ps[:, 4, t * P:(t + 1) * P], kend[:, t * P:(t + 1) * P], ident[:, :])
                mm.then_inc(filled[4], 1)
                units(2)
                pe.wait_ge(drained[4], nth("hg", "ket", n))
                pe.wait_ge(drained[5], nth("hg", "vt", n))
                pe.wait_ge(drained[6], before("hg", "u", n))
                for t in range(3):
                    mm = pe.matmul(ps[:, 6, t * P:(t + 1) * P], keT[:, t * P:(t + 1) * P], vh[:, t * P:(t + 1) * P], start=True, stop=True)
                mm.then_inc(filled[6], 1)
                for i in range(L):
                    b = banks.bank("hg", ("s", i))
                    pe.wait_ge(drained[b], before("hg", ("s", i), n))
                    pe.wait_ge(qk_ready, n * (2 * L) + 2 * (i + 1))
                    for t in range(TT):
                        mm = pe.matmul(ps[:, b, t * 64:(t + 1) * 64], klev[:, i, t * P:(t + 1) * P],
                                       qlev[:, i, t * 64:(t + 1) * 64], start=True, stop=True)
                    mm.then_inc(filled[b], 1)
                b = banks.bank("hg", ("s", L))
                pe.wait_ge(drained[b], before("hg", ("s", L), n))
                for t in range(TT):
                    mm = pe.matmul(ps[:, b, t * P:(t + 1) * P], kk[:, t * P:(t + 1) * P], qh[:, t * P:(t + 1) * P],
                                   start=True, stop=True)
                mm.then_inc(filled[b], 1)
                units(3)
                pe.wait_ge(drained[6], before("hg", "o", n))
                for i in range(L - 2, L + 1):
                    b = banks.bank("hg", ("s", i))
                    pe.wait_ge(drained[b], nth("hg", ("s", i), n))
                pe.wait_ge(state_ready, n * 3 + 3)
                pe.wait_ge(qb_ready, n + 1)
                for t in range(TT):
                    cols = slice(t * P, (t + 1) * P)
                    mm = pe.matmul(ps[:, 6, cols], vh[:, t * P:(t + 1) * P], score[:, cols], start=True, stop=t == 0)
                    if t:
                        mm = pe.matmul(ps[:, 6, cols], state[:, (t - 1) * P:t * P], qb[:, cols], start=False, stop=True)
                mm.then_inc(filled[6], 1)

            def head_unit(j0, j, turn=0, per=0, use=None):
                unit(U_HGIN + j0, j, h_hi, h_lo, (2 * j, 2 * j + 1), "hgin", up_tags, j == 0, j == 3, turn, per, head_order,
                     use=use)

            core(0, lambda j: head_unit(4, j, use=1), None)
            with pe.Fori(0, HG_HEADS - 2) as r:
                core(r + 1, lambda j: head_unit(8, j, r, 4, use=r + 2), r)

            def hgout(j):
                def tile(a):
                    pe.wait_ge(ho_lo, 2 * (j % 4) + a + 1)
                unit(U_HGOUT, j, m_hi, m_lo, (2 * (j % 4), 2 * (j % 4) + 1), "hgout",
                     [("h", j // 4, m) for m in range(4)], j % 4 == 0, j % 4 == 3, wait_tile=tile)

            def last_units(j):
                if j < 2:
                    hgout(j)
                if j == 2:
                    b = banks.bank("hg", ("s", 2))
                    pe.wait_ge(drained[b], before("hg", ("s", 2), HG_HEADS - 1))
                    keep_clock(b, 16)

            core(HG_HEADS - 1, last_units, HG_HEADS - 2)
            head_sum(HG_HEADS - 1)
            hgout(2)
            for j in range(3, 8):
                hgout(j)
            glu(1, 5)

            def out_half(h, t):
                b = banks.bank("end", ("y", t, h))
                pe.wait_ge(drained[b], before("end", ("y", t, h)))
                for k in range(4):
                    pe.wait_ge(y_ready, 4 * h + k + 1)
                    mm = pe.transpose(ps[:, b, k * P:(k + 1) * P], yT[:, 4 * h + k, t * P:(t + 1) * P], ident[:, :])
                mm.then_inc(filled[b], 1)

            for t in range(TT):
                out_half(0, t)
            for t in range(TT - 1):
                out_half(1, t)
            pe.wait_ge(drained[7], before("end", "sum"))
            pe.wait_ge(sq_used, KT * 8)
            for t in range(TT):
                mm = pe.matmul(ps[:, 7, t:t + 1], ss[:, t * P:(t + 1) * P], ones[:, 0:1], start=True, stop=True)
            mm.then_inc(filled[7], 1)
            out_half(1, TT - 1)

        @block.vector
        def _(dve):
            dve.memset(ones[:, :], 1.0).then_inc(set_up, 1)
            dve.memset(eps6[:, :], 1e-6).then_inc(set_up, 1)
            dve.memset(eps5[:, :], 1e-5).then_inc(set_up, 1)

            def col(name, k):
                return vecs[:, COL[name] + k:COL[name] + k + 1]

            def lo_part(n, k, name, off=0):
                dve.wait_ge(hi_ready, KT * n + k + 1)
                dve.scalar_tensor_tensor(out=h_lo[:, k, :], in0=xT[:, k, :], scalar=col(name, off + k),
                                         in1=h_hi[:, k, :].bitcast(F32), op0=ALU.mult, op1=ALU.subtract)\
                    .then_inc(lo_ready, 1)

            def sum_square(i, k):
                if k:
                    dve.wait_ge(sq_ready, KT * (i - 1) + k + 1)
                if k == 1:
                    dve.tensor_tensor(ss[:, :], sq[:, 0, :], sq[:, 1, :], ALU.add).then_inc(sq_used, 2)
                elif k:
                    dve.wait_ge(sq_used, KT * (i - 1) + k)
                    dve.tensor_tensor(ss[:, :], ss[:, :], sq[:, k % 2, :], ALU.add).then_inc(sq_used, 1)

            def tiles_for_norm(n, i, make, name, off=0):
                for half in range(2):
                    tiles = [4 * half + k for k in range(4)]
                    for k in tiles:
                        make(k)
                        if k - 1 in tiles:
                            lo_part(n, k - 1, name, off)
                        if k - 2 in tiles:
                            sum_square(i, k - 2)
                    sum_square(i, tiles[2])
                    lo_part(n, tiles[3], name, off)
                    sum_square(i, tiles[3])

            def post_normed(i, rs_n, gain, name):
                dve.wait_ge(rs_ready, rs_n)
                for k in range(KT + 2):
                    if k < KT:
                        dve.scalar_tensor_tensor(out=acc[:, k, :], in0=acc[:, k, :], scalar=col(gain, k), in1=rs[:, :],
                                                 op0=ALU.mult, op1=ALU.mult).then_inc(post_step, 1)
                        dve.wait_ge(post_step, KT * i + k + 1)
                        dve.tensor_tensor(xT[:, k, :], xT[:, k, :], acc[:, k, :], ALU.add).then_inc(x_ready, 1)
                    if 1 <= k <= KT:
                        lo_part(i + 1, k - 1, name)
                    if k >= 2:
                        sum_square(2 * i + 2, k - 2)

            dve.wait_ge(gains_in, 16 * 2)
            for t in range(TT):
                dve.wait_ge(xrs_ready, 2 * t + 2)
                dve.tensor_scalar(xdiag[:, t, :], ident[:, :], xrs[:, t:t + 1], None, ALU.mult).then_inc(xdiag_ready, 1)
            dve.wait_ge(filled[4], nth("start", "vec"))
            dve.tensor_copy(vecs[:, :], bank("start", "vec")[:, 0:N_VEC]).then_inc(drained[4], 1)
            dve.wait_ge(drained[4], nth("start", "vec"))
            for k in range(KT):
                dve.wait_ge(hi_ready, k + 1)
                dve.scalar_tensor_tensor(out=h_lo[:, k, :], in0=bank("start", ("h", k)), scalar=col("g_pre_mix", k),
                                         in1=h_hi[:, k, :].bitcast(F32), op0=ALU.mult, op1=ALU.subtract)\
                    .then_inc(drained[k], 1)
            dve.wait_ge(filled[5], nth("small", "taps"))
            dve.tensor_copy(taps[:, :, :], bank("small", "taps")[:, 0:4 * TAPS].rearrange("p (t j) -> p t j", j=4))\
                .then_inc(drained[5], 1)
            dve.wait_ge(small_in, 16 * 5)
            for i in range(2):
                dve.wait_ge(filled[6 + i], nth("small", f"rel{i}"))
                dve.tensor_tensor(relrow[:, i * 512:(i + 1) * 512], bank("small", f"rel{i}")[0:N_HEADS, :],
                                  lnmult[:, i * 512:(i + 1) * 512], ALU.add).then_inc(drained[6 + i], 1)
            for i in range(2):
                dve.wait_ge(filled[4 + i], nth("small", f"ws{i}"))
                dve.tensor_copy(wsT[:, 4 * i:4 * i + 4, :], bank("small", f"ws{i}").rearrange("p (g t) -> p g t", t=P))\
                    .then_inc(drained[4 + i], 1)

            logits = [vecs[:, COL["hg_lb_logits_2"] + i * HG_HEADS:COL["hg_lb_logits_2"] + (i + 1) * HG_HEADS]
                      for i in range(2)]
            top, less, ex, tot, inv, p0, p1, lb = (lbt[:, i, :] for i in range(8))
            less1, ex1 = tot, inv
            dve.tensor_tensor(top, logits[0], logits[1], ALU.max).then_inc(lb_step, 1)
            dve.wait_ge(lb_step, 1)
            dve.tensor_tensor(less, logits[0], top, ALU.subtract).then_inc(lb_step, 1)
            dve.tensor_tensor(less1, logits[1], top, ALU.subtract).then_inc(lb_step, 1)
            dve.wait_ge(lb_exp, 2)
            dve.tensor_tensor(tot, ex, ex1, ALU.add).then_inc(lb_step, 1)
            dve.wait_ge(lb_step, 4)
            dve.reciprocal(top, tot).then_inc(lb_step, 1)
            dve.wait_ge(lb_step, 5)
            dve.tensor_tensor(p0, ex, top, ALU.mult).then_inc(lb_step, 1)
            dve.tensor_tensor(p1, ex1, top, ALU.mult).then_inc(lb_step, 1)
            dve.wait_ge(lb_step, 7)
            dve.tensor_tensor(lb, p0, p1, ALU.add).then_inc(lb_step, 1)
            dve.wait_ge(lb_step, 8)
            dve.tensor_tensor(hcol[:, :, 1], lb, p0, ALU.subtract).then_inc(lb_step, 1)
            dve.wait_ge(lb_step, 9)
            dve.tensor_scalar(hcol[:, :, 0], hcol[:, :, 1], -1.0, 1.0, ALU.mult, ALU.add).then_inc(lb_step, 1)
            dve.tensor_scalar(hcol[:, :, 2], hcol[:, :, 1], -1.0, None, ALU.add).then_inc(lb_step, 1)
            dve.tensor_copy(hcol[:, :, 3], vecs[:, COL["hg_gn_g_2"]:COL["hg_gn_g_2"] + HG_HEADS]).then_inc(lb_step, 1)
            dve.wait_ge(lb_step, 12)

            for k in range(0, KT, 2):
                b = banks.bank("x", ("x", k))
                dve.wait_ge(filled[b], nth("x", ("x", k)))
                dve.tensor_copy(xT[:, k, :], bank("x", ("x", k))).then_inc(drained[b], 1)

            def sum_tiles(total, tiles, ready, step, done):
                ready(0)
                for m in range(1, 4):
                    ready(m)
                    if m > 1:
                        dve.wait_ge(step, done + m - 1)
                    dve.tensor_tensor(total, tiles[:, 0, :] if m == 1 else total, tiles[:, m, :], ALU.add).then_inc(step, 1)

            sum_tiles(gsum[:, :], gv, lambda m: dve.wait_ge(drained[m], nth("zv", ("m", m))), gsum_step, 0)
            dve.wait_ge(filled[4], nth("zvnorm", "mean"))
            for m in range(4):
                dve.scalar_tensor_tensor(out=gv[:, m, :], in0=bank("zvnorm", "mean"), scalar=-1.0 / (4 * P), in1=gv[:, m, :],
                                         op0=ALU.mult, op1=ALU.add).then_inc(sgu_step, 1)
            dve.wait_ge(sgu_step, 4)
            dve.sem_inc(drained[4], 1)
            sum_tiles(gsum[:, :], sgu_vt, lambda m: dve.wait_ge(sgu_sq, m + 1), gsum_step, 3)
            dve.wait_ge(rs_ready, 1)
            for m in range(4):
                dve.tensor_tensor(gv[:, m, :], gv[:, m, :], rs[:, :], ALU.mult).then_inc(sgu_step, 1)
                dve.wait_ge(sgu_step, 5 + m)
                dve.tensor_scalar(gv[:, m, :], gv[:, m, :], col("sgu_ln_g", m), col("sgu_ln_b", m), ALU.mult, ALU.add)\
                    .then_inc(sgu_y, 1)
            def qk_low(e, p):
                own, other = own_rows(e), own_rows(1 - e)
                dve.wait_ge(qk_hi, p * 6 + 3 * e + 1)
                dve.tensor_tensor(k_lo[own, :], ps[own, 1, :], k_his[own, e, :].bitcast(F32), ALU.subtract)\
                    .then_inc(qk_lo, 1)
                dve.wait_ge(qk_hi, p * 6 + 3 * e + 2)
                dve.scalar_tensor_tensor(out=q_parts[other, e, :], in0=ps[own, 0, :], scalar=HEAD_DIM ** -0.5,
                                         in1=q_parts[own, e, :].bitcast(F32), op0=ALU.mult, op1=ALU.subtract)\
                    .then_inc(qk_lo, 1)
                if e:
                    dve.wait_ge(qk_lo, p * 4 + 4)
                    dve.sem_inc(drained[0], 1)
                    dve.sem_inc(drained[1], 1)

            qk_low(0, 0)
            qk_low(1, 0)
            dve.wait_ge(sgu_in, 32)
            for j in range(4):
                dve.wait_ge(filled[4 + j], nth("sgu", ("mix", j)))
                dve.tensor_tensor(gv[:, j, :].rearrange("p (t s) -> p t s", s=P),
                                  bank("sgu", ("mix", j)).rearrange("p (t s) -> p t s", s=P),
                                  sgub[:, j, :].unsqueeze(1).broadcast_to([P, TT, P]), ALU.add).then_inc(drained[4 + j], 1)

            def sgu_out(p):
                u_count = nth("qkv0", ("m", 3)) + p
                dve.wait_ge(drained[3], u_count)
                dve.tensor_tensor(ug[:, :], ug[:, :], tile_of(gv, p), ALU.mult).then_inc(sg_ready, 1)

            def sgu_low(p):
                dve.wait_ge(sg_hi, p + 1)
                dve.tensor_tensor(tile_of(m_lo, 4 + p), ug[:, :], tile_of(m_hi, 4 + p).bitcast(F32), ALU.subtract)\
                    .then_inc(sg_lo, 1)

            dve.wait_ge(drained[7], nth("sgu", ("mix", 3)))
            dve.wait_ge(btab_in, 16)

            def biased(i, p):
                e, t = i // 4, i % 4
                b = banks.bank("att", ("s", i))
                dve.wait_ge(filled[b], nth("att", ("s", i), p))
                tab = btab[:, 2 * p + e, (3 - t) * P:(3 - t) * P + SEQ]
                dve.tensor_tensor_reduce(sbias[:, i % 2, :], ps[:, b, :], tab, 1.0, -3e38, ALU.add, ALU.max,
                                         amax[:, i:i + 1]).then_inc(drained[b], 1)
                dve.wait_ge(drained[b], nth("att", ("s", i), p))
                dve.tensor_scalar(nmax[:, i:i + 1], amax[:, i:i + 1], -1.0, None, ALU.mult).then_inc(neg_ready, 1)

            def normal(e, p):
                cols = slice(HEAD_DIM * e, HEAD_DIM * (e + 1))
                dve.wait_ge(prob_ready, p * 8 + 4 * e + 4)
                dve.reciprocal(rden[:, 4 * e:4 * e + 4], den[:, 4 * e:4 * e + 4]).then_inc(den_inv, 1)
                dve.wait_ge(den_inv, p * 2 + e + 1)
                dve.wait_ge(filled[7], nth("att", ("o", e), p))
                dve.tensor_tensor(onorm[:, :, cols], ps[:, 7, :].rearrange("p (t f) -> p t f", f=P)[:, :, cols],
                                  rden[:, 4 * e:4 * e + 4].unsqueeze(2).broadcast_to([P, TT, HEAD_DIM]), ALU.mult)\
                    .then_inc(drained[7], 1)
                dve.wait_ge(drained[7], nth("att", ("o", e), p))
                dve.sem_inc(onorm_ready, 1)

            def pair_low(p):
                dve.wait_ge(o_hi, p + 1)
                dve.tensor_tensor(m_lo[:, p, :], ps[:, 7, :], m_hi[:, p, :].bitcast(F32), ALU.subtract)\
                    .then_inc(drained[7], 1)

            def attend(p):
                def turned(i):
                    dve.wait_ge(filled[6], nth("att", ("t", i), p))
                    dve.tensor_copy(probT[:, i % 2, :], ps[:, 6, :]).then_inc(drained[6], 1)

                sgu_out(p)
                turned(0)
                biased(2, p)
                turned(1)
                biased(3, p)
                sgu_low(p)
                if p:
                    pair_low(p - 1)
                turned(2)
                biased(4, p)
                turned(3)
                biased(5, p)
                normal(0, p)
                turned(4)
                biased(6, p)
                turned(5)
                biased(7, p)
                if p + 1 < PAIRS:
                    qk_low(0, p + 1)
                turned(6)
                if p + 1 < PAIRS:
                    biased(0, p + 1)
                turned(7)
                if p + 1 < PAIRS:
                    qk_low(1, p + 1)
                    biased(1, p + 1)
                normal(1, p)

            biased(0, 0)
            biased(1, 0)
            for p in range(PAIRS):
                attend(p)
            pair_low(PAIRS - 1)

            for k in range(KT):
                b = banks.bank("wout", ("h", k // 4, k % 4))
                dve.wait_ge(filled[b], nth("wout", ("h", k // 4, k % 4)))
                dve.tensor_copy(acc[:, k, :], ps[:, b, :]).then_inc(drained[b], 1)
                if k % 4:
                    sum_square(1, k - 1)
                if k % 4 == 3:
                    sum_square(1, k)
            post_normed(0, 2, "g_post_mix", "g_pre_ffn")
            dve.wait_ge(rs_ready, 3)

            def ffn_up(g, turn_of_bank, par):
                stage = "ffn0" if isinstance(g, int) and g == 0 else "ffnup"

                def hidden(m):
                    b = banks.bank(stage, ("m", m))
                    dve.wait_ge(filled[b], nth(stage, ("m", m), turn_of_bank))
                    dve.scalar_tensor_tensor(out=relu[:, m % 2, :], in0=ps[:, b, :], scalar=0.0, in1=rs[:, :],
                                             op0=ALU.max, op1=ALU.mult).then_inc(drained[b], 1)

                def parts(m):
                    dve.wait_ge(drained[banks.bank(stage, ("m", m))], nth(stage, ("m", m), turn_of_bank))
                    dve.tensor_tensor(hid[:, m % 2, :], relu[:, m % 2, :], relu[:, m % 2, :], ALU.mult)\
                        .then_inc(hid_ready, 1)
                    dve.wait_ge(hid_ready, g * 4 + (m + 1))
                    dve.wait_ge(hid_hi, g * 4 + (m + 1))
                    dve.tensor_tensor(m_lo[:, 4 * par + m, :], hid[:, m % 2, :], m_hi[:, 4 * par + m, :].bitcast(F32),
                                      ALU.subtract).then_inc(hid_lo, 1)

                hidden(0)
                for m in range(4):
                    if m < 3:
                        hidden(m + 1)
                    parts(m)

            def ffn_down(g, first=False, last=False):
                for h in range(2):
                    for m in range(4):
                        k = 4 * h + m
                        dve.wait_ge(filled[4 + m], nth("ffndown", ("d", h, m), g))
                        if first:
                            dve.tensor_copy(acc[:, k, :], ps[:, 4 + m, :]).then_inc(drained[4 + m], 1)
                        else:
                            dve.tensor_tensor(acc[:, k, :], acc[:, k, :], ps[:, 4 + m, :], ALU.add)\
                                .then_inc(drained[4 + m], 1)
                        if last and m:
                            sum_square(3, k - 1)
                    if last:
                        sum_square(3, 4 * h + 3)

            ffn_up(0, 0, 0)
            ffn_up(1, 0, 1)
            ffn_down(0, first=True)
            with dve.Fori(0, FFN_GROUPS // 2 - 1) as i:
                ffn_up(i * 2 + 2, i * 2 + 1, 0)
                ffn_down(i * 2 + 1)
                ffn_up(i * 2 + 3, i * 2 + 2, 1)
                ffn_down(i * 2 + 2)
            ffn_down(FFN_GROUPS - 1, last=True)
            post_normed(1, 4, "g_post_ffn", "norm_mix_g_2")
            dve.memset(apad[:, :, 0:PAD], 0.0).then_inc(set_up, 1)
            dve.memset(upad[:, :, 0:POOL_PAD], 0.0).then_inc(set_up, 1)
            dve.wait_ge(set_up, 5)
            dve.wait_ge(rs_ready, 5)

            def gates(g):
                for i in range(2):
                    b = banks.bank("cpin", ("g", g, 2 + i))
                    dve.wait_ge(filled[b], nth("cpin", ("g", g, 2 + i)))
                    dve.tensor_tensor(csig[:, i, :], ps[:, b, :], rs[:, :], ALU.mult).then_inc(drained[b], 1)
                for i in range(2):
                    b = banks.bank("cpin", ("g", g, i))
                    dve.wait_ge(filled[b], nth("cpin", ("g", g, i)))
                    dve.tensor_tensor(apad[:, 2 * g + i, PAD:], ps[:, b, :], rs[:, :], ALU.mult).then_inc(drained[b], 1)

            def gated(g):
                for i in range(2):
                    j = 2 * g + i
                    b = banks.bank("cpin", ("g", g, i))
                    dve.wait_ge(drained[b], nth("cpin", ("g", g, i)))
                    dve.wait_ge(csig_ready, j + 1)
                    dve.tensor_tensor(apad[:, j, PAD:], apad[:, j, PAD:], csig[:, i, :], ALU.mult)\
                        .then_inc(apad_ready, 1)

            def tap(j, i):
                a, w_i = apad[:, j, i:i + SEQ], taps[:, i, j:j + 1]
                if i == 0:
                    dve.tensor_scalar(conv[:, j, :], a, w_i, col("cp_dw_b_2", j), ALU.mult, ALU.add)\
                        .then_inc(tap_done[j], 1)
                else:
                    dve.wait_ge(tap_done[j], i)
                    dve.scalar_tensor_tensor(out=conv[:, j, :], in0=a, scalar=w_i, in1=conv[:, j, :], op0=ALU.mult,
                                             op1=ALU.add).then_inc(tap_done[j], 1)

            gates(0)
            gated(0)
            dve.wait_ge(apad_ready, 2)
            for i in range(TAPS):
                if i == 13:
                    for m in range(4):
                        b = banks.bank("cpin", ("g", 2, m))
                        dve.wait_ge(filled[b], nth("cpin", ("g", 2, m)))
                        dve.tensor_tensor(upad[:, m, POOL_PAD:], ps[:, b, :], rs[:, :], ALU.mult).then_inc(drained[b], 1)
                if i == 26:
                    gates(1)
                if i == 27:
                    gated(1)
                tap(0, i)
                tap(1, i)
            dve.wait_ge(apad_ready, 4)
            for i in range(TAPS):
                a, w_i = apad[:, 2, i:i + SEQ], taps[:, i, 2:3]
                if i == 0:
                    dve.tensor_scalar(conv[:, 2, :], a, w_i, col("cp_dw_b_2", 2), ALU.mult, ALU.add).then_inc(tap_done[2], 1)
                elif i == 1:
                    dve.tensor_scalar(odd[:, :], a, w_i, None, ALU.mult).then_inc(odd_done, 1)
                else:
                    t, done = (odd[:, :], odd_done) if i % 2 else (conv[:, 2, :], tap_done[2])
                    dve.wait_ge(done, i // 2)
                    dve.scalar_tensor_tensor(out=t, in0=a, scalar=w_i, in1=t, op0=ALU.mult, op1=ALU.add).then_inc(done, 1)
            dve.wait_ge(tap_done[2], (TAPS + 1) // 2)
            dve.wait_ge(odd_done, TAPS // 2)
            dve.tensor_tensor(conv[:, 2, :], conv[:, 2, :], odd[:, :], ALU.add).then_inc(tap_done[2], 1)
            def conv_tile(j):
                if j < 3:
                    dve.wait_ge(tap_done[j], TAPS if j < 2 else (TAPS + 1) // 2 + 1)
                else:
                    dve.wait_ge(drained[4], nth("cpin", "conv"))

            sum_tiles(csum[:, :], conv, conv_tile, csum_step, 0)
            dve.wait_ge(filled[5], nth("cpin", "mean"))
            for j in range(4):
                dve.scalar_tensor_tensor(out=conv[:, j, :], in0=bank("cpin", "mean"), scalar=-1.0 / (4 * P),
                                         in1=conv[:, j, :], op0=ALU.mult, op1=ALU.add).then_inc(cln_step, 1)
            dve.wait_ge(cln_step, 4)
            dve.sem_inc(drained[5], 1)
            sum_tiles(csum[:, :], csq, lambda j: dve.wait_ge(cln_sq, j + 1), csum_step, 3)
            dve.wait_ge(crs_ready, 1)
            for j in range(4):
                dve.tensor_tensor(conv[:, j, :], conv[:, j, :], crs[:, :], ALU.mult).then_inc(cln_y, 1)
            for j in range(4):
                dve.wait_ge(cs_hi, j + 1)
                dve.tensor_tensor(m_lo[:, j, :], csq[:, j, :], m_hi[:, j, :].bitcast(F32), ALU.subtract).then_inc(cs_lo, 1)

            def add_out(stage):
                def make(k):
                    b = banks.bank(stage, ("h", k // 4, k % 4))
                    dve.wait_ge(filled[b], nth(stage, ("h", k // 4, k % 4)))
                    dve.tensor_tensor(xT[:, k, :], xT[:, k, :], ps[:, b, :], ALU.add).then_inc(drained[b], 1)
                return make

            tiles_for_norm(3, 5, add_out("cpout"), "norm_ffn_g_2")

            def glu(layer, finish):
                stage = f"glu{layer}"
                done = 2 * GLU_GROUPS * layer
                dve.wait_ge(rs_ready, 6 + 2 * layer)

                def up(g, par):
                    for i in range(2):
                        dve.wait_ge(filled[i], nth(stage, ("m", i), g))
                        dve.tensor_tensor(gate[:, i, :], ps[:, i, :], rs[:, :], ALU.mult).then_inc(drained[i], 1)
                        dve.wait_ge(filled[2 + i], nth(stage, ("m", 2 + i), g))
                        if not isinstance(g, int):
                            dve.wait_ge(ghid_lo, g * 2 + (done + i - 1))
                        dve.tensor_tensor(ghid[:, i, :], ps[:, 2 + i, :], rs[:, :], ALU.mult).then_inc(drained[2 + i], 1)
                    for i in range(2):
                        dve.wait_ge(drained[2 + i], nth(stage, ("m", 2 + i), g))
                        dve.wait_ge(silu_ready, g * 2 + (done + i + 1))
                        dve.tensor_tensor(ghid[:, i, :], silu[:, i, :], ghid[:, i, :], ALU.mult).then_inc(ghid_ready, 1)
                    for i in range(2):
                        dve.wait_ge(ghid_ready, g * 2 + (done + i + 1))
                        dve.wait_ge(ghid_hi, g * 2 + (done + i + 1))
                        dve.tensor_tensor(m_lo[:, 2 * par + i, :], ghid[:, i, :], m_hi[:, 2 * par + i, :].bitcast(F32),
                                          ALU.subtract).then_inc(ghid_lo, 1)

                def down_tile(g, k):
                    h, m = k // 4, k % 4
                    dve.wait_ge(filled[4 + m], nth(stage, ("d", h, m), g))
                    dve.tensor_tensor(xT[:, k, :], xT[:, k, :], ps[:, 4 + m, :], ALU.add).then_inc(drained[4 + m], 1)

                def down(g):
                    for k in range(KT):
                        down_tile(g, k)

                up(0, 0)
                with dve.Fori(0, GLU_GROUPS // 2) as i:
                    up(i * 2 + 1, 1)
                    down(i * 2)
                    up(i * 2 + 2, 0)
                    down(i * 2 + 1)
                finish(lambda k: down_tile(GLU_GROUPS - 1, k))

            glu(0, lambda make: tiles_for_norm(4, 6, make, "norm_mix_g_2", KT))
            dve.memset(score[:, :], 0.0).then_inc(set_up, 1)
            dve.memset(klev[:, :, :], 0.0).then_inc(set_up, 1)
            dve.wait_ge(set_up, 7)
            dve.wait_ge(rs_ready, 7)
            dve.wait_ge(consts_in, 16 * 3)

            def f_cols(n):
                dve.tensor_copy(fcol[:, :], tile_of(hcol, n))\
                    .then_inc(fcol_ready, 1)

            f_cols(0)

            def drain_head(n, tiles):
                for m in tiles:
                    dst = (qh, sgf, iT, gT)[m]
                    dve.wait_ge(filled[m], nth("hgin", ("m", m), n))
                    dve.tensor_tensor(dst[:, :], ps[:, m, :], rs[:, :], ALU.mult).then_inc(drained[m], 1)

            def keys(n):
                dve.wait_ge(sgf_ready, n + 1)
                dve.wait_ge(fcol_ready, n + 1)
                dve.tensor_scalar(kk[:, :], sgf[:, :], fcol[:, 2:3], fcol[:, 0:1], ALU.mult, ALU.add).then_inc(kk_ready, 1)

            def gate_of(n):
                dve.wait_ge(fcol_ready, n + 1)
                dve.tensor_copy(gcol[:, :], fcol[:, 3:4]).then_inc(gcol_ready, 1)
                dve.wait_ge(drained[3], nth("hgin", ("m", 3), n))
                dve.wait_ge(sgg_ready, n + 1)
                dve.tensor_tensor(gs[:, :], gT[:, :], sgg[:, :], ALU.mult).then_inc(gs_ready, 1)

            def head_out(n):
                dve.wait_ge(hrs_ready, n + 1)
                dve.wait_ge(gcol_ready, n + 1)
                dve.wait_ge(gs_ready, n + 1)
                dve.scalar_tensor_tensor(out=hn[:, :], in0=bank("hg", "o"), scalar=gcol[:, :], in1=hrs[:, :],
                                         op0=ALU.mult, op1=ALU.mult).then_inc(drained[6], 1)
                dve.wait_ge(drained[6], nth("hg", "o", n))
                dve.tensor_tensor(ho[:, :], hn[:, :], gs[:, :], ALU.mult).then_inc(ho_ready, 1)

            def head_low(n):
                dve.wait_ge(ho_hi, n + 1)
                dve.tensor_tensor(tile_of(m_lo, n), ho[:, :], tile_of(m_hi, n).bitcast(F32), ALU.subtract).then_inc(ho_lo, 1)

            drain_head(0, (1, 3, 0, 2))
            keys(0)

            def core(n, before_it, last=False):
                L = len(LEVELS)
                dve.wait_ge(lf_ready, n + 1)
                for t in range(TT):
                    cols = slice(t * WIN, (t + 1) * WIN)
                    dve.tensor_tensor_scan(cum[:, cols], ones[:, :], lf[:, cols], 0.0, ALU.mult, ALU.add)\
                        .then_inc(cum_ready, 1)
                dve.wait_ge(cum_ready, 4 * n + 4)
                win = cum[:, :].rearrange("p (w t) -> p w t", t=WIN)
                dve.tensor_tensor(dend[:, :].rearrange("p (w t) -> p w t", t=WIN),
                                  win[:, :, WIN - 1:WIN].broadcast_to([P, TT, WIN]), win, ALU.subtract)\
                    .then_inc(dend_ready, 1)

                def diffs(i):
                    m = LEVELS[i]
                    c = levels(cum[:, :], m)
                    d = levels(dlev[:, i % 2, :], m)
                    mid = c[:, :, 0, m - 1:m].broadcast_to([P, SEQ // (2 * m), m])
                    if i >= 2:
                        dve.wait_ge(elev_ready, n * L + (i - 1))
                    dve.tensor_tensor(d[:, :, 1, :], c[:, :, 1, :], mid, ALU.subtract).then_inc(dlev_ready, 1)
                    dve.tensor_tensor(d[:, :, 0, :], mid, c[:, :, 0, :], ALU.subtract).then_inc(dlev_ready, 1)

                def decayed(i):
                    m = LEVELS[i]
                    e = levels(elev[:, i % 2, :], m)
                    dve.wait_ge(elev_ready, n * L + (i + 1))
                    dve.tensor_tensor(qlev[:, i, :].rearrange("p (n m) -> p n m", m=m), levels(qh[:, :], m)[:, :, 1, :],
                                      e[:, :, 1, :], ALU.mult).then_inc(qk_ready, 1)
                    dve.tensor_tensor(levels(klev[:, i, :], m)[:, :, 0, :], levels(kk[:, :], m)[:, :, 0, :],
                                      e[:, :, 0, :], ALU.mult).then_inc(qk_ready, 1)

                diffs(0)
                if before_it is not None:
                    dve.wait_ge(filled[6], nth("hg", "o", before_it))
                dve.wait_ge(drained[0], nth("hgin", ("m", 0), n))
                dve.wait_ge(kk_ready, n + 1)
                dve.wait_ge(e0_ready, n + 1)
                dve.tensor_tensor(qb[:, :], qh[:, :], e0[:, :], ALU.mult).then_inc(qb_ready, 1)
                dve.wait_ge(eend_ready, n + 1)
                dve.tensor_tensor(kend[:, :], kk[:, :], dend[:, :], ALU.mult).then_inc(kend_ready, 1)
                diffs(1)
                for i in range(L):
                    decayed(i)
                    if i + 2 < L:
                        diffs(i + 2)
                    if i == 1:
                        if before_it is not None:
                            head_out(before_it)
                            dve.wait_ge(ho_ready, before_it + 1)
                        gate_of(n)
                        if before_it is not None:
                            head_low(before_it)
                        if not last:
                            dve.wait_ge(gcol_ready, n + 1)
                            f_cols(n + 1)
                dve.wait_ge(filled[6], nth("hg", "u", n))
                for w_ in range(3):
                    u = ps[:, 6, w_ * P:(w_ + 1) * P]
                    if w_ == 0:
                        dve.tensor_copy(state[:, 0:P], u).then_inc(state_ready, 1)
                    else:
                        dve.wait_ge(state_ready, n * 3 + w_)
                        e = e0[:, w_ * WIN + WIN - 1:w_ * WIN + WIN]
                        dve.scalar_tensor_tensor(out=state[:, w_ * P:(w_ + 1) * P], in0=state[:, (w_ - 1) * P:w_ * P], scalar=e, in1=u,
                                                 op0=ALU.mult, op1=ALU.add).then_inc(state_ready, 1)
                dve.wait_ge(state_ready, n * 3 + 3)
                dve.sem_inc(drained[6], 1)
                for i in range(L):
                    m = LEVELS[i]
                    b = banks.bank("hg", ("s", i))
                    if i:
                        dve.wait_ge(drained[banks.bank("hg", ("s", i - 1))], nth("hg", ("s", i - 1), n))
                    dve.wait_ge(filled[b], nth("hg", ("s", i), n))
                    dve.sem_inc(placing, 1)
                    dst = score[:, :].rearrange("p (w n two m) -> p w n two m", w=TT, two=2, m=m)[:, :, :, 1, :]
                    src = ps[:, b, 0:256].rearrange("p (w n m) -> p w n m", w=TT, m=m)
                    msk = mask[:, i, :].rearrange("p (n m) -> p n m", m=m).unsqueeze(1).broadcast_to([P, TT, 64 // m, m])
                    dve.copy_predicated(dst, msk, src).then_inc(drained[b], 1)
                b = banks.bank("hg", ("s", L))
                dve.wait_ge(drained[banks.bank("hg", ("s", L - 1))], nth("hg", ("s", L - 1), n))
                dve.wait_ge(filled[b], nth("hg", ("s", L), n))
                dve.sem_inc(placing, 1)
                dve.copy_predicated(score[:, :].rearrange("p (w t) -> p w t", t=P),
                                    diag[:, :].unsqueeze(1).broadcast_to([P, TT, P]),
                                    ps[:, b, :].rearrange("p (w t) -> p w t", t=P)).then_inc(drained[b], 1)
                if not last:
                    dve.wait_ge(gs_ready, n + 1)
                    dve.wait_ge(drained[b], nth("hg", ("s", L), n))
                    drain_head(n + 1, (1, 3, 0, 2))
                    keys(n + 1)

            core(0, None)
            with dve.Fori(0, HG_HEADS - 2) as r:
                core(r + 1, r)
            core(HG_HEADS - 1, HG_HEADS - 2, True)
            head_out(HG_HEADS - 1)
            head_low(HG_HEADS - 1)
            tiles_for_norm(5, 7, add_out("hgout"), "norm_ffn_g_2", KT)

            def finish(make):
                for k in range(KT):
                    b = banks.bank("glu1", ("d", k // 4, k % 4))
                    make(k)
                    dve.wait_ge(drained[b], nth("glu1", ("d", k // 4, k % 4), GLU_GROUPS - 1))
                    dve.tensor_scalar(yT[:, k, :], xT[:, k, :], col("final_g_2", k), None, ALU.mult).then_inc(y_ready, 1)
                    if k % 4:
                        sum_square(8, k - 1)
                    if k % 4 == 3:
                        sum_square(8, k)

            glu(1, finish)
            dve.wait_ge(yrs_ready, 1)
            for t in range(TT):
                dve.wait_ge(filled[4 + t], nth("end", ("y", t, 1)))
                dve.tensor_scalar(otok[:, t, D // 2:], bank("end", ("y", t, 1)), yrs[:, t:t + 1], None, ALU.mult)\
                    .then_inc(drained[4 + t], 1)


def constants():
    dist = np.arange(1024) - (SEQ - 1)
    n = np.abs(dist)
    half = N_BUCKETS // 2
    exact = half // 2
    large = exact + (np.log(np.maximum(n, 1).astype(np.float32) / np.float32(exact))
                     / np.float32(math.log(REL_MAX / exact)) * np.float32(half - exact)).astype(np.int32)
    bucket = np.where(dist > 0, half, 0) + np.where(n < exact, n, np.minimum(large, half - 1))
    onehot = (bucket[None, :] == np.arange(N_BUCKETS)[:, None]).astype(np.float32)
    seen = sum(((n % dil == 0) & (n <= window // 2)).astype(np.int32) for window, dil in BRANCHES)
    lnmult = np.where(seen > 0, np.log(np.maximum(seen, 1)), -1e30).astype(np.float32)
    t = np.arange(P)
    mask = np.zeros((P, len(LEVELS), 64), np.int32)
    for i, m in enumerate(LEVELS):
        later = (np.arange(64) // m) * (2 * m) + m + np.arange(64) % m
        mask[:, i, :] = (t[:, None] // (2 * m) == later[None, :] // (2 * m)) & (t[:, None] % (2 * m) < m)
    inv = np.stack([1.0 / np.minimum(np.arange(POOL_PAD) + 1, w) for w in POOL_WINDOWS]).astype(np.float32)
    return {
        "ident": np.eye(P, dtype=np.float32),
        "onehot": onehot,
        "lnmult": np.ascontiguousarray(np.broadcast_to(lnmult, (N_HEADS, 1024))),
        "poolinv": np.ascontiguousarray(np.broadcast_to(inv, (P,) + inv.shape)),
        "mask": mask,
        "diag": np.eye(P, dtype=np.int32),
    }


WEIGHTS = ("w_in", "w_out", "w_ff1", "w_ff2", "cp_w_in_2", "cp_w_out_2", "hg_w_in_2", "hg_w_out_2",
           "ffn_w1_2", "ffn_w3_2", "ffn_w2_2")


def kernel(**inputs):
    import concourse.bacc as bacc
    from concourse.bass_utils import run_bass_kernel_spmd

    nc = bacc.Bacc("TRN2", target_bir_lowering=False, num_devices=1)
    arrays = {}

    def take(name, a):
        arrays[name] = np.ascontiguousarray(a)
        return nc.dram_tensor(name, arrays[name].shape, mybir.dt.from_np(arrays[name].dtype), kind="ExternalInput").ap()

    get = {k: np.asarray(v) for k, v in inputs.items()}
    x = take("in_x", get["x"][0])
    w = {}
    for name in WEIGHTS:
        a = get[name]
        w[name] = take("in_" + name, a if name.startswith("ffn_") else a[0])
    vec = take("in_vectors", np.concatenate([get[name].reshape(-1, P) for name, _ in VECTORS]))
    rest = [take("in_" + name, get[name][0]) for name in ("sgu_w", "sgu_b")]
    rest.append(take("in_rel_bias", get["rel_bias"]))
    rest += [take("in_" + name, get[name][0]) for name in ("cp_dw_w_2", "cp_pool_w_2")]
    c = constants()
    rest += [take("const_" + name, c[name]) for name in ("ident", "onehot", "lnmult", "poolinv", "mask", "diag")]
    scratch = nc.dram_tensor("bias_rows", (N_HEADS, P, 1025), F32, kind="Internal").ap()
    out = nc.dram_tensor("out_0", (SEQ, D), F32, kind="ExternalOutput").ap()
    build(nc, x, w, vec, *rest, scratch, out)
    r = run_bass_kernel_spmd(nc, [arrays], core_ids=[0])
    return r.results[0]["out_0"].reshape(1, SEQ, D)
```
